# Optimizing a Trainium2 kernel written in Bass

```python
import jax, jax.numpy as jnp
from jax import lax
import numpy as np

D_MODEL = 1024
BATCH = 1
SEQ = 256
DEPTH = 1
DEC_BATCH = 8
DEC_SEQ = 4
PAST_LEN = 2048
PAGE_SIZE = 128

MIX_WIDTH = D_MODEL
GDN_HEADS = 4
GDN_DK = 128
GDN_DV = MIX_WIDTH // 2 // GDN_HEADS
GLA_HEADS = 4
GLA_DK = 64
GLA_DV = (MIX_WIDTH - GDN_HEADS * GDN_DV) // GLA_HEADS
GLA_GATE_RANK = 16
GLA_GATE_NORMALIZER = 16.0
CONV_WIDTH = 4
CHUNK = 64
N_EXPERTS = 32
TOP_K = 4
D_FF = D_MODEL
SWIGLU_LIMIT = 7.0
SWIGLU_ALPHA = 1.702
MOE_BLOCK = 128
RMS_EPS = 1e-6
L2_EPS = 1e-6

GDN_QK_W = GDN_HEADS * GDN_DK
GDN_V_W = GDN_HEADS * GDN_DV
GDN_CONV_CH = 2 * GDN_QK_W + GDN_V_W
GLA_QK_W = GLA_HEADS * GLA_DK
GLA_V_W = GLA_HEADS * GLA_DV
IN_SPLITS = (GDN_CONV_CH, GDN_V_W, GDN_HEADS, GDN_HEADS, GLA_QK_W, GLA_QK_W, GLA_V_W, GLA_V_W, GLA_GATE_RANK)
IN_DIM = sum(IN_SPLITS)

kernel_name = "hymba_gdn_gla_moe_step"

def rmsnorm(x, w):
    xf = x.astype(jnp.float32)
    y = xf * lax.rsqrt(jnp.mean(xf * xf, axis=-1, keepdims=True) + RMS_EPS)
    return (y * w.astype(jnp.float32)).astype(x.dtype)

def gated_rmsnorm(o, w, z):
    of = o.astype(jnp.float32)
    y = of * lax.rsqrt(jnp.mean(of * of, axis=-1, keepdims=True) + RMS_EPS)
    return y * w.astype(jnp.float32) * jax.nn.silu(z.astype(jnp.float32))

def l2norm(x):
    return x * lax.rsqrt(jnp.sum(x * x, axis=-1, keepdims=True) + L2_EPS)

def split_cols(t, sizes):
    out, off = [], 0
    for s in sizes:
        out.append(t[..., off:off + s])
        off += s
    return out

def to_heads(t, n_heads):
    b, s, w = t.shape
    return t.reshape(b, s, n_heads, w // n_heads).transpose(0, 2, 1, 3)

def pad_time(t, pad):
    widths = [(0, 0)] * t.ndim
    widths[2] = (0, pad)
    return jnp.pad(t, widths)

def causal_conv(u, buf, w):
    t_len = u.shape[1]
    xc = jnp.concatenate([buf.astype(u.dtype), u], axis=1)
    out = xc[:, 0:t_len] * w[0]
    for i in range(1, CONV_WIDTH):
        out = out + xc[:, i:i + t_len] * w[i]
    return jax.nn.silu(out), xc[:, -(CONV_WIDTH - 1):]

def gated_delta_rule(q, k, v, g, beta, s0):
    b, h, t_len, dk = q.shape
    dv = v.shape[-1]
    c = min(CHUNK, t_len)
    pad = (-t_len) % c
    if pad:
        q, k, v, g, beta = (pad_time(a, pad) for a in (q, k, v, g, beta))
    n = (t_len + pad) // c
    q = q.reshape(b, h, n, c, dk)
    k = k.reshape(b, h, n, c, dk)
    v = v.reshape(b, h, n, c, dv)
    g_cum = jnp.cumsum(g.reshape(b, h, n, c), axis=-1)
    beta = beta.reshape(b, h, n, c)
    tril = jnp.tril(jnp.ones((c, c), bool))
    strict = jnp.tril(jnp.ones((c, c), bool), -1)
    decay = jnp.exp(jnp.where(tril, g_cum[..., :, None] - g_cum[..., None, :], -jnp.inf))
    kb = k * beta[..., None]
    vb = v * beta[..., None]
    m = jnp.where(strict, jnp.einsum('bhnid,bhnjd->bhnij', kb, k) * decay, 0.0)
    eye = jnp.eye(c, dtype=m.dtype)
    t_inv = lax.linalg.triangular_solve(eye + m, jnp.broadcast_to(eye, m.shape), left_side=True,
                                        lower=True, unit_diagonal=True)
    u = jnp.einsum('bhnij,bhnjd->bhnid', t_inv, vb)
    w = jnp.einsum('bhnij,bhnjd->bhnid', t_inv, kb * jnp.exp(g_cum)[..., None])
    a_intra = jnp.einsum('bhnid,bhnjd->bhnij', q, k) * decay

    def step(s, inp):
        q_c, k_c, u_c, w_c, gc_c, a_c = inp
        v_new = u_c - jnp.einsum('bhcd,bhde->bhce', w_c, s)
        o = jnp.einsum('bhcd,bhde->bhce', q_c * jnp.exp(gc_c)[..., None], s) + \
            jnp.einsum('bhij,bhje->bhie', a_c, v_new)
        g_last = gc_c[..., -1]
        s = s * jnp.exp(g_last)[..., None, None] + \
            jnp.einsum('bhcd,bhce->bhde', k_c * jnp.exp(g_last[..., None] - gc_c)[..., None], v_new)
        return s, o

    xs = tuple(jnp.moveaxis(a, 2, 0) for a in (q, k, u, w, g_cum, a_intra))
    s_fin, o = lax.scan(step, s0, xs)
    o = jnp.moveaxis(o, 0, 2).reshape(b, h, n * c, dv)[:, :, :t_len]
    return o, s_fin

def gla_chunked(q, k, v, gk, s0):
    b, h, t_len, dk = q.shape
    dv = v.shape[-1]
    c = min(CHUNK, t_len)
    pad = (-t_len) % c
    if pad:
        q, k, v, gk = (pad_time(a, pad) for a in (q, k, v, gk))
    n = (t_len + pad) // c
    q = q.reshape(b, h, n, c, dk)
    k = k.reshape(b, h, n, c, dk)
    v = v.reshape(b, h, n, c, dv)
    b_cum = jnp.cumsum(gk.reshape(b, h, n, c, dk), axis=-2)
    tril = jnp.tril(jnp.ones((c, c), bool))[:, :, None]

    def step(s, inp):
        q_c, k_c, v_c, b_c = inp
        o_inter = jnp.einsum('bhcd,bhde->bhce', q_c * jnp.exp(b_c), s)
        dec = jnp.exp(jnp.where(tril, b_c[:, :, :, None, :] - b_c[:, :, None, :, :], -jnp.inf))
        a = jnp.einsum('bhid,bhjd,bhijd->bhij', q_c, k_c, dec)
        o = o_inter + jnp.einsum('bhij,bhje->bhie', a, v_c)
        b_last = b_c[:, :, -1]
        s = jnp.exp(b_last)[..., None] * s + \
            jnp.einsum('bhcd,bhce->bhde', k_c * jnp.exp(b_last[:, :, None] - b_c), v_c)
        return s, o

    xs = tuple(jnp.moveaxis(a, 2, 0) for a in (q, k, v, b_cum))
    s_fin, o = lax.scan(step, s0, xs)
    o = jnp.moveaxis(o, 0, 2).reshape(b, h, n * c, dv)[:, :, :t_len]
    return o, s_fin

def token_mixers(h, conv_buf, s_gdn, s_gla, w_in, conv_w, gdn_a_log, gdn_dt_bias, gdn_norm_w,
                 gla_gk_w, gla_gk_b, gla_norm_w, w_out):
    f32 = jnp.float32
    b, t_len, _ = h.shape
    proj = h @ w_in
    qkv_raw, gdn_z, gdn_a, gdn_b, gla_q, gla_k, gla_v, gla_g, gla_lr = split_cols(proj, IN_SPLITS)

    qkv, conv_new = causal_conv(qkv_raw, conv_buf, conv_w)
    q, k, v = split_cols(qkv.astype(f32), (GDN_QK_W, GDN_QK_W, GDN_V_W))
    q = l2norm(to_heads(q, GDN_HEADS)) * (GDN_DK ** -0.5)
    k = l2norm(to_heads(k, GDN_HEADS))
    v = to_heads(v, GDN_HEADS)
    beta = jax.nn.sigmoid(gdn_b.astype(f32)).transpose(0, 2, 1)
    g = (-jnp.exp(gdn_a_log.astype(f32)) *
         jax.nn.softplus(gdn_a.astype(f32) + gdn_dt_bias.astype(f32))).transpose(0, 2, 1)
    o_gdn, s_gdn_new = gated_delta_rule(q, k, v, g, beta, s_gdn.astype(f32))
    o_gdn = gated_rmsnorm(o_gdn.transpose(0, 2, 1, 3), gdn_norm_w,
                          gdn_z.reshape(b, t_len, GDN_HEADS, GDN_DV)).reshape(b, t_len, GDN_V_W)

    gk = jax.nn.log_sigmoid((gla_lr @ gla_gk_w + gla_gk_b).astype(f32)) / GLA_GATE_NORMALIZER
    o_gla, s_gla_new = gla_chunked(to_heads(gla_q.astype(f32), GLA_HEADS) * (GLA_DK ** -0.5),
                                   to_heads(gla_k.astype(f32), GLA_HEADS),
                                   to_heads(gla_v.astype(f32), GLA_HEADS),
                                   to_heads(gk, GLA_HEADS), s_gla.astype(f32))
    o_gla = gated_rmsnorm(o_gla.transpose(0, 2, 1, 3), gla_norm_w,
                          gla_g.reshape(b, t_len, GLA_HEADS, GLA_DV)).reshape(b, t_len, GLA_V_W)

    out = jnp.concatenate([o_gdn, o_gla], axis=-1).astype(h.dtype) @ w_out
    return (out, conv_new.astype(conv_buf.dtype), s_gdn_new.astype(s_gdn.dtype),
            s_gla_new.astype(s_gla.dtype))

def moe(x2d, w_router, b_router, w_up, b_up, w_down, b_down):
    f32 = jnp.float32
    n_tok, d = x2d.shape
    logits = x2d.astype(f32) @ w_router.astype(f32) + b_router.astype(f32)
    top_v, top_i = lax.top_k(logits, TOP_K)
    gates = jax.nn.softmax(top_v, axis=-1)
    n_assign = n_tok * TOP_K
    flat_e = top_i.reshape(-1)
    flat_tok = jnp.arange(n_assign, dtype=jnp.int32) // TOP_K
    flat_g = gates.reshape(-1)
    order = jnp.argsort(flat_e)
    se = flat_e[order]
    counts = jnp.bincount(flat_e, length=N_EXPERTS)
    padded = (counts + MOE_BLOCK - 1) // MOE_BLOCK * MOE_BLOCK
    pend = jnp.cumsum(padded)
    pstart = pend - padded
    ustart = jnp.cumsum(counts) - counts
    dest = pstart[se] + (jnp.arange(n_assign, dtype=jnp.int32) - ustart[se])
    n_rows = (n_assign + MOE_BLOCK - 1) // MOE_BLOCK * MOE_BLOCK + N_EXPERTS * MOE_BLOCK
    n_blocks = n_rows // MOE_BLOCK
    row_tok = jnp.full((n_rows,), n_tok, jnp.int32).at[dest].set(flat_tok[order])
    row_gate = jnp.zeros((n_rows,), f32).at[dest].set(flat_g[order])
    block_e = jnp.minimum(jnp.searchsorted(pend, jnp.arange(n_blocks) * MOE_BLOCK, side='right'),
                          N_EXPERTS - 1)
    x_pad = jnp.concatenate([x2d, jnp.zeros((1, d), x2d.dtype)], axis=0)
    xb = x_pad[row_tok].reshape(n_blocks, MOE_BLOCK, d)

    def expert_block(args):
        xe, e = args
        gu = xe @ w_up[e] + b_up[e]
        gate = jnp.minimum(gu[:, :D_FF], SWIGLU_LIMIT)
        up = jnp.clip(gu[:, D_FF:], -SWIGLU_LIMIT, SWIGLU_LIMIT)
        act = (up + 1.0) * gate * jax.nn.sigmoid(SWIGLU_ALPHA * gate)
        return act @ w_down[e] + b_down[e]

    yb = lax.map(expert_block, (xb, block_e)).reshape(n_rows, d)
    out = jnp.zeros((n_tok + 1, d), f32).at[row_tok].add(yb.astype(f32) * row_gate[:, None])
    return out[:n_tok].astype(x2d.dtype)

def trunk(x, conv_st, gdn_st, gla_st, rms_mix_w, w_in, conv_w, gdn_a_log, gdn_dt_bias, gdn_norm_w,
          gla_gk_w, gla_gk_b, gla_norm_w, w_out, rms_ffn_w, w_router, b_router, w_up, b_up,
          w_down, b_down, rms_final_w):
    convs, gdns, glas = [], [], []
    for l in range(DEPTH):
        mix, c_new, g_new, a_new = token_mixers(
            rmsnorm(x, rms_mix_w[l]), conv_st[l], gdn_st[l], gla_st[l], w_in[l], conv_w[l],
            gdn_a_log[l], gdn_dt_bias[l], gdn_norm_w[l], gla_gk_w[l], gla_gk_b[l], gla_norm_w[l], w_out[l])
        x = x + mix
        b, t_len, d = x.shape
        x = x + moe(rmsnorm(x, rms_ffn_w[l]).reshape(b * t_len, d), w_router[l], b_router[l],
                    w_up[l], b_up[l], w_down[l], b_down[l]).reshape(b, t_len, d)
        convs.append(c_new)
        gdns.append(g_new)
        glas.append(a_new)
    return rmsnorm(x, rms_final_w), jnp.stack(convs), jnp.stack(gdns), jnp.stack(glas)

def setup_inputs(seed: int = 0) -> dict:
    key = jax.random.key(seed)
    ks = jax.random.split(key, 24)
    f32 = jnp.float32
    L, D = DEPTH, D_MODEL

    def nrm(k, shape, scale):
        return jax.random.normal(k, shape, f32) * scale

    dt = jnp.exp(jax.random.uniform(ks[9], (L, GDN_HEADS), f32, np.log(1e-3), np.log(1e-1)))
    return {
        "x_prompt": nrm(ks[0], (BATCH, SEQ, D), 1.0),
        "x_sample": nrm(ks[1], (DEC_BATCH, DEC_SEQ, D), 1.0),
        "state_gdn_conv": nrm(ks[2], (L, DEC_BATCH, CONV_WIDTH - 1, GDN_CONV_CH), 1.0),
        "state_gdn": nrm(ks[3], (L, DEC_BATCH, GDN_HEADS, GDN_DK, GDN_DV), 0.1),
        "state_gla": nrm(ks[4], (L, DEC_BATCH, GLA_HEADS, GLA_DK, GLA_DV), 0.1),
        "rms_mix_w": 1.0 + nrm(ks[5], (L, D), 0.02),
        "w_in": nrm(ks[6], (L, D, IN_DIM), D ** -0.5),
        "conv_w": nrm(ks[7], (L, CONV_WIDTH, GDN_CONV_CH), CONV_WIDTH ** -0.5),
        "gdn_a_log": jnp.log(jax.random.uniform(ks[8], (L, GDN_HEADS), f32, 1.0, 16.0)),
        "gdn_dt_bias": dt + jnp.log(-jnp.expm1(-dt)),
        "gdn_norm_w": 1.0 + nrm(ks[10], (L, GDN_DV), 0.02),
        "gla_gk_w": nrm(ks[11], (L, GLA_GATE_RANK, GLA_QK_W), GLA_GATE_RANK ** -0.5),
        "gla_gk_b": nrm(ks[12], (L, GLA_QK_W), 0.01),
        "gla_norm_w": 1.0 + nrm(ks[13], (L, GLA_DV), 0.02),
        "w_out": nrm(ks[14], (L, MIX_WIDTH, D), MIX_WIDTH ** -0.5),
        "rms_ffn_w": 1.0 + nrm(ks[15], (L, D), 0.02),
        "w_router": nrm(ks[16], (L, D, N_EXPERTS), D ** -0.5),
        "b_router": nrm(ks[17], (L, N_EXPERTS), 0.01),
        "w_up": nrm(ks[18], (L, N_EXPERTS, D, 2 * D_FF), D ** -0.5),
        "b_up": nrm(ks[19], (L, N_EXPERTS, 2 * D_FF), 0.01),
        "w_down": nrm(ks[20], (L, N_EXPERTS, D_FF, D), D_FF ** -0.5),
        "b_down": nrm(ks[21], (L, N_EXPERTS, D), 0.01),
        "rms_final_w": 1.0 + nrm(ks[22], (D,), 0.02),
    }

def reference(x_prompt, x_sample, state_gdn_conv, state_gdn, state_gla, rms_mix_w, w_in, conv_w,
              gdn_a_log, gdn_dt_bias, gdn_norm_w, gla_gk_w, gla_gk_b, gla_norm_w, w_out, rms_ffn_w,
              w_router, b_router, w_up, b_up, w_down, b_down, rms_final_w):
    bp = x_prompt.shape[0]
    conv0 = jnp.zeros((DEPTH, bp) + state_gdn_conv.shape[2:], state_gdn_conv.dtype)
    gdn0 = jnp.zeros((DEPTH, bp) + state_gdn.shape[2:], state_gdn.dtype)
    gla0 = jnp.zeros((DEPTH, bp) + state_gla.shape[2:], state_gla.dtype)
    y_prompt, conv_prompt, gdn_prompt, gla_prompt = trunk(
        x_prompt, conv0, gdn0, gla0, rms_mix_w, w_in, conv_w, gdn_a_log, gdn_dt_bias, gdn_norm_w,
        gla_gk_w, gla_gk_b, gla_norm_w, w_out, rms_ffn_w, w_router, b_router, w_up, b_up, w_down,
        b_down, rms_final_w)
    y_sample, conv_sample, gdn_sample, gla_sample = trunk(
        x_sample, state_gdn_conv, state_gdn, state_gla, rms_mix_w, w_in, conv_w, gdn_a_log,
        gdn_dt_bias, gdn_norm_w, gla_gk_w, gla_gk_b, gla_norm_w, w_out, rms_ffn_w, w_router,
        b_router, w_up, b_up, w_down, b_down, rms_final_w)
    return (y_prompt, y_sample, conv_prompt, gdn_prompt, gla_prompt, conv_sample, gdn_sample, gla_sample)


_drawn_inputs = setup_inputs


def setup_inputs(seed=0):
    import zlib

    import numpy as np

    out = dict(_drawn_inputs(seed))
    spreads = {}
    factors = {'gla_gk_b': 8.0,
     'b_up': 8.0,
     'b_down': 8.0,
     'rms_final_w': 22.633,
     'gdn_norm_w': 2.668,
     'b_router': 2.724,
     'gla_norm_w': 2.707}
    for name, (base, spread) in spreads.items():
        noise = np.random.default_rng([zlib.crc32(name.encode()), seed]).standard_normal(out[name].shape)
        drawn = base * np.exp(spread * noise) if base else spread * noise
        out[name] = __import__('jax').numpy.asarray(drawn.astype(out[name].dtype))
    for name, factor in factors.items():
        out[name] = (out[name] * factor).astype(out[name].dtype)
    return out
```

```python
from contextlib import ExitStack

import concourse.bass as bass
from concourse import mybir

P = 128
F32 = mybir.dt.float32
I32 = mybir.dt.int32
ALU = mybir.AluOpType
ACT = mybir.ActivationFunctionType
AX_X = mybir.AxisListType.X

D = 1024
KT = D // P
SEQ, NB, NS = 256, 8, 4
SMP = NB * NS
T = SEQ + SMP
NTT = 3
TN = [P, P, SMP]
TO = [0, P, 2 * P]
H = 4
QK = 512
CH = 3 * QK
HEAD = 3
RAW = HEAD + SEQ + NB * (HEAD + NS)
CW = RAW - HEAD
LEVELS = 7
E_N, TOPK, FF = 32, 4, 1024
CAP = 64
PAIRS = E_N // 2
EPS = 1e-6
NEG = -3.0e38
C_Z, C_A, C_B = 1536, 2048, 2052
C_GQ, C_GV, C_GG, C_LR = 2056, 2568, 3080, 3592


def program(nc, a, o):
    ctx = ExitStack()
    with ctx:
        def sb(name, shape, dt=F32):
            return ctx.enter_context(nc.sbuf_tensor(name, shape, dt))

        def sem(name):
            return ctx.enter_context(nc.semaphore(name))

        bank = [ctx.enter_context(nc.psum_tensor(f"bank{i}", [P, 512], F32)) for i in range(8)]

        def cut(base, at, *shape):
            n = 1
            for s in shape:
                n *= s
            v = base[:, at:at + n]
            if len(shape) == 2:
                v = v.rearrange("p (a b) -> p a b", a=shape[0])
            if len(shape) == 3:
                v = v.rearrange("p (a b c) -> p a b c", a=shape[0], b=shape[1])
            return v

        UNIT = 4096
        ring = sb("ring", [P, 6 * UNIT])
        slot = [ring[:, i * UNIT:(i + 1) * UNIT] for i in range(6)]
        sgs = cut(ring, 0, NB, H, P)
        S3 = 3 * UNIT
        KQ = cut(ring, S3, 2, H, T)
        kbT = cut(ring, S3 + 2304, H, T)
        nM = cut(ring, S3 + 3456, 2 * H, P)
        nMs = cut(ring, S3 + 4480, H, SMP)
        AT = cut(ring, S3 + 4608, 2 * H, P)
        ATs = cut(ring, S3 + 5632, H, SMP)
        U = cut(ring, S3 + 5760, 2 * H, P)
        Us = cut(ring, S3 + 6784, H, SMP)
        Ti = cut(ring, S3 + 6912, 2 * H, P)
        Tis = cut(ring, S3 + 7936, H, SMP)
        Y = cut(ring, S3 + 8064, 2 * H, P)
        Ys = cut(ring, S3 + 9088, H, SMP)
        Dt = cut(ring, S3 + 9216, 2 * H, P)
        Dts = cut(ring, S3 + 10240, H, SMP)
        gE = cut(ring, S3 + 10368, 2, T)
        gQ = cut(ring, S3 + 10944, 2, T)
        gK = cut(ring, S3 + 11520, 2, T)
        brow = cut(ring, S3 + 5760, 6, P)
        crow = ring[:, S3 + 8064:S3 + 8064 + CH]
        gdiag = cut(ring, S3 + 6912, H, T)
        AG = cut(ring, S3 + 8064, 2 * H, P)
        AGs = cut(ring, S3 + 9088, H, SMP)
        kdm = cut(ring, S3 + 9216, NB, P)

        osq = ring[:, S3:S3 + D]
        skT = sb("skT", [P, 2, P])
        xb = sb("xb", [P, 3 * D])
        xt = cut(xb, 0, 3, D)
        gqk = cut(xb, 0, 4, T)
        kdg = cut(xb, 0, 3, 256)
        vg = cut(xb, 1152, 3, 512)
        ob = sb("ob", [P, 3 * D])
        raw = cut(ob, 0, 4, RAW)
        ce = cut(ob, 1260, 4, RAW)
        ce_z = cut(ob, 1260, 4, T)
        ot = cut(ob, 0, 3, D)
        xeT = cut(xb, 0, KT, P)
        yr = xb[:, D:2 * D]
        yT = cut(xb, 2 * D, KT, P)
        hT = sb("hT", [P, KT, T])
        zg = sb("zg", [P, KT, T])
        zf = zg[:].rearrange("p a b -> p (a b)")
        gu = cut(zf, 0, 2, 4, CAP)
        aT = cut(zf, 512, 8, CAP)
        sg = cut(zf, 1024, 4, CAP)
        G = cut(zf, 1280, 3, P)
        GG = cut(zf, 1664, 3, P)
        convf = sb("convT", [P, 4 * T])
        convT = cut(convf, 0, 4, T)
        wbc = convf[:, 0:D]
        qf = sb("qkv", [P, 3 * CH])
        qkv = cut(qf, 0, 3, CH)
        x2 = cut(qf, 0, 3, D)
        vn = qkv[:, :, 0:QK]
        ident = sb("ident", [P, P])
        ones = sb("ones", [P, P])
        upi = sb("upi", [P, P])
        upis = sb("upis", [SMP, SMP])
        mu = sb("mu", [P, LEVELS, P], I32)
        mlf = sb("ml", [P, LEVELS * P])
        ml = cut(mlf[:].bitcast(I32), 0, LEVELS, P)
        mone = sb("mone", [P, P], I32)
        seqm = sb("seqm", [SMP, NB])
        resets = sb("resets", [P, T])
        sgp = sb("sgp", [P, H, P])
        sls = sb("sls", [P, 2, NB, P])
        slp = sb("slp", [P, 2, P])
        bTf = sb("bT", [P, 2 * T])
        bT = cut(bTf, 0, 2, T)
        S = bTf[:, 0:T]
        ta = cut(bTf, T, 4, CAP)
        lg = mlf[:, 0:96]
        m8 = sb("m8", [P, 3, 8])
        gts = mlf[:, 96:192]
        eqs = mlf[:, 192:288]
        pre = mlf[:, 288:384]
        selm = mlf[:, 384:480]
        gates = mlf[:, 480:576]
        posm = mlf[:, 576:672]
        r32 = mlf[:, 672:768]
        ndd = sb("ndd", [P, 3])
        den = sb("den", [P, 3])
        tri = sb("tri", [P, P])
        cnt = sb("cnt", [1, 2])
        cgt = sb("cgt", [1, 4])
        rnd = sb("rnd", [1, 1], I32)
        slots_io = sb("slots_io", [P, CAP])
        pp = sb("pp", [P, 3, 2])
        gp2 = sb("gp2", [P, 3, 2])
        bup = sb("bup", [P, 2, 2, 2, 4])
        bdn = sb("bdn", [P, 2, 8])
        wsmf = sb("wsm", [P, KT * 80])
        wsm = cut(wsmf, 0, KT, 80)
        wr = cut(wsmf, 0, KT, E_N)
        brt = wsmf[:, KT * E_N:KT * E_N + E_N]
        sm = sb("sm", [80, T])
        gb = sb("gb", [68, T])
        gtmp = sb("gtmp", [36, 2, T])
        kb = sb("kb", [P, QK])
        gt = sb("gt", [P, 3, 68])
        eg = sb("eg", [P, 3, H])
        ekd = sb("ekd", [P, 3, H])
        nbeg = sb("nbeg", [P, 3, H])
        egl = sb("egl", [P, H, 10])
        gate2 = sb("gate2", [4, 3])
        vrow = sb("vrow", [60, P])
        vecT = sb("vecT", [P, 60])
        gkw = sb("gkw", [80, 256])
        cT = sb("cT", [P, 12, 24])
        cs = sb("cs", [P, 12, 27])
        ss = sb("ss", [P, 3])
        rst = sb("rst", [P, 3])
        ss8 = sb("ss8", [P, 24])
        rs8 = sb("rs8", [P, 24])
        mhalf = sb("mhalf", [P, 24])
        ebl = sb("ebl", [P, 2, 10])
        biasT = sb("biasT", [P, 6, P])

        names = """ld_x ld_vec ld_gate ld_cst ld_sm ld_bias ld_st ld_router w_in1 w_in2
            ident_ok masks_ok v_step ss_ok rst_in rst_ok h_ok p_vec vec_ok p_hT
            hT_ok p_cT cT_ok p_bias bias_ok p_proj proj_ok conv_lin conv_sig conv_ok
            cs_ok p_convt convt_ok p_gk gk_x gk_e gk_l bT_ok gate_x gate_e
            gate_l gb_ok p_gt gt_ok gt_exp p_gi di_ok dexp_ok d_ok ss8_ok
            rs8_ok qkn_ok p_qkT qkT_ok p_MA MA_ok p_y y_ok p_inv inv_ok
            p_tm p_ch ch_ok vd_ok p_smp g_abs g_exp g_lvl p_glvl ag_ok
            ebl_ok zg_ok smk_ok smr_ok p_gkd kdg_ok p_gch gch_ok p_gs gsT_ok
            osq_ok o_ok p_oT oT_ok w_out w_out2 x_again p_x2 x2_ok p_xnT
            xnT_ok p_lg route_ok ss2_ok rs2_in xn_ok p_pos kdm_ok dec_ok p_up_s
            st_ok p_csr csr_ok out_done ld_ffn ld_fin lg_ok tri_ok rnd_ok G_ok
            p_gat p_up p_yd p_ty p_sc p_S w_used gu_rd gu_ok act_ok
            yb_ok sc_ok xe_ok yr_ok S_ok sig_ok ld_w0 ld_w1 ld_w2 ld_w3
            ld_w4 ld_w5 st_out st_out2 pp_ok pos_next acc_ok gexp_ok gu_cl ta_ok
            bp_ok ss3_ok rs3_in rs3_ok p_fin fin_x y_fin""".split()
        WSLOT = [3, 4, 2, 1, 5, 0]
        INV = [(l, t) for l in range(1, LEVELS) for t in ((0, 1, 2) if l == 1 else (0, 1))]
        inv_at = {(0, t): t + 1 for t in range(3)} | {x: 4 + i for i, x in enumerate(INV)}
        NMt = [nM[:, 0:H], nM[:, H:2 * H], nMs[0:SMP]]
        Att = [AT[:, 0:H], AT[:, H:2 * H], ATs[0:SMP]]
        Ut = [U[:, 0:H], U[:, H:2 * H], Us[0:SMP]]
        Tt = [Ti[:, 0:H], Ti[:, H:2 * H], Tis[0:SMP]]
        Yt = [Y[:, 0:H], Y[:, H:2 * H], Ys[0:SMP]]
        Dtt = [Dt[:, 0:H], Dt[:, H:2 * H], Dts[0:SMP]]
        AGt = [AG[:, 0:H], AG[:, H:2 * H], AGs[0:SMP]]
        sems = {n: sem(n) for n in names}
        block = ctx.enter_context(nc.Block())

        class Count:

            def __init__(self, eng):
                self.eng, self.n = eng, {}

            def tick(self, ins, name):
                ins.then_inc(sems[name], 1)
                self.n[name] = self.n.get(name, 0) + 1

            def done(self, ins, name):
                self.tick(ins, name)
                self.eng.wait_ge(sems[name], self.n[name])

        def wait(eng, name, value):
            if value > 0:
                eng.wait_ge(sems[name], value)

        def bc(ap, *shape):
            return ap.broadcast_to(list(shape))

        def samples(ap):
            return ap.rearrange("p (b j) -> p b j", b=NB)

        def hx(ap):
            return ap.unsqueeze(2)

        @block.sync
        def _(sp):
            sp.dma_start(xt[:, 0:2, :], a["x_prompt"].rearrange("a (t p) d -> p (a t) d", p=P)).then_inc(sems["ld_x"], 16)
            sp.dma_start(xt[0:SMP, 2, :], a["x_sample"].rearrange("b s d -> (b s) d")).then_inc(sems["ld_x"], 16)
            rows = [(a["rms_mix_w"].rearrange("l (k p) -> (l k) p", p=P), 0, 8),
                    (a["conv_w"].rearrange("l i (c p) -> (l i c) p", p=P), 8, 48),
                    (a["gla_gk_b"].rearrange("l (j p) -> (l j) p", p=P), 56, 2),
                    (a["gdn_norm_w"], 58, 1), (a["gla_norm_w"], 59, 1)]
            for src, at, n in rows:
                sp.dma_start(vrow[at:at + n, :], src).then_inc(sems["ld_vec"], 16)
            w_in = a["w_in"].rearrange("l (k p) n -> p (l k) n", p=P)
            sp.dma_start(wsm[:, :, 0:4], w_in[:, :, C_A:C_A + 4]).then_inc(sems["ld_sm"], 16)
            sp.dma_start(wsm[:, :, 32:36], w_in[:, :, C_B:C_B + 4]).then_inc(sems["ld_sm"], 16)
            sp.dma_start(wsm[:, :, 64:80], w_in[:, :, C_LR:C_LR + 16]).then_inc(sems["ld_sm"], 16)
            units = [0, 512, 1024, C_GQ, C_GV, C_Z, C_GG]
            for u in range(7):
                if u >= 2:
                    wait(sp, "p_proj", 1 + 4 * (u - 1))
                dst = slot[1 + u % 2].rearrange("p (k n) -> p k n", k=KT)
                sp.dma_start(dst, w_in[:, :, units[u]:units[u] + 512]).then_inc(sems[f"w_in{1 + u % 2}"], 16)
                if u == 1:
                    sp.dma_start(crow[0:24, :], a["state_gdn_conv"].rearrange("l b r c -> (l b r) c")).then_inc(sems["ld_cst"], 16)
                    sp.dma_start(brow[:, 0:4, :], a["b_up"].rearrange("l e (j p) -> (l e j) p", p=P).rearrange("(g r) p -> r g p", r=P)).then_inc(sems["ld_bias"], 16)
                    sp.dma_start(brow[:, 4:6, :], a["b_down"].rearrange("l e (j p) -> (l e j) p", p=P).rearrange("(g r) p -> r g p", r=P)).then_inc(sems["ld_bias"], 16)
                    sp.dma_start(gate2[:, 0:1], a["gdn_a_log"].rearrange("l h -> h l")).then_inc(sems["ld_gate"], 16)
                    sp.dma_start(gate2[:, 1:2], a["gdn_dt_bias"].rearrange("l h -> h l")).then_inc(sems["ld_gate"], 16)
                    sp.dma_start(gkw[64:80, :], a["gla_gk_w"][0]).then_inc(sems["ld_gate"], 16)
                    for h in range(H):
                        sp.dma_start(sgs[:, :, h, :], a["state_gdn"][0, :, h].rearrange("b k v -> k b v")).then_inc(sems["ld_st"], 16)
                    for h in range(H):
                        r = 64 * (h % 2)
                        sp.dma_start(sls[r:r + 64, h // 2, :, :], a["state_gla"][0, :, h].rearrange("b k v -> k b v")).then_inc(sems["ld_st"], 16)

            w_o = a["w_out"].rearrange("l (k p) n -> p (l k) n", p=P)
            for u in range(2):
                wait(sp, "p_proj", (25, 29)[u])
                dst = slot[2 - u].rearrange("p (k n) -> p k n", k=KT)
                sp.dma_start(dst, w_o[:, :, 512 * u:512 * (u + 1)]).then_inc(sems[("w_out", "w_out2")[u]], 16)

            for n in range(4):
                if n == 0:
                    wait(sp, "p_convt", 12)
                    sp.dma_start(wbc, a["rms_ffn_w"].partition_broadcast(P).rearrange("q l d -> q (l d)")).then_inc(sems["ld_ffn"], 16)
                    sp.dma_start(wr, a["w_router"].rearrange("l (k p) e -> p (l k) e", p=P)).then_inc(sems["ld_router"], 16)
                    sp.dma_start(brt, a["b_router"].partition_broadcast(P).rearrange("q l d -> q (l d)")).then_inc(sems["ld_router"], 16)
            wait(sp, "ch_ok", 6)
            sp.dma_start(x2[:, 0:2, :], a["x_prompt"].rearrange("a (t p) d -> p (a t) d", p=P)).then_inc(sems["x_again"], 16)
            sp.dma_start(x2[0:SMP, 2, :], a["x_sample"].rearrange("b s d -> (b s) d")).then_inc(sems["x_again"], 16)

            up = a["w_up"][0].rearrange("e (k p) (g h c) -> e p k g h c", p=P, g=2, h=2)
            dn = a["w_down"][0].rearrange("e (k p) n -> e p k n", p=P)

            def load_unit(e, u):
                if u < 4:
                    src = up[e, :, 4 * (u % 2):4 * (u % 2) + 4, :, u // 2, :]
                    for kk in range(4):
                        dst = slot[WSLOT[u]][:, 1024 * kk:1024 * (kk + 1)].rearrange("p (g c) -> p g c", g=2)
                        i = sp.dma_start(dst, src[:, kk])
                        i.then_inc(sems[f"ld_w{u}"], 16)
                else:
                    src = dn[e, :, 4 * (u - 4):4 * (u - 4) + 4, :]
                    dst = slot[WSLOT[u]].rearrange("p (k n) -> p k n", k=4)
                    sp.dma_start(dst, src).then_inc(sems[f"ld_w{u}"], 16)

            wait(sp, "osq_ok", 4)
            wait(sp, "p_oT", 1)
            load_unit(0, 0)
            load_unit(0, 1)
            wait(sp, "p_proj", 33)
            load_unit(0, 2)
            wait(sp, "p_proj", 37)
            load_unit(0, 3)
            wait(sp, "p_up_s", 6)
            wait(sp, "st_ok", 6)
            load_unit(0, 4)
            wait(sp, "out_done", 16 * 6)
            load_unit(0, 5)
            wait(sp, "xn_ok", 3)
            sp.dma_start(wbc, a["rms_final_w"].partition_broadcast(P)).then_inc(sems["ld_fin"], 16)
            wait(sp, "rnd_ok", 1)
            rounds = sp.value_load(rnd[0:1, 0:1], min_val=1, max_val=5)
            with sp.Fori(1, rounds * E_N) as m:
                e = m % E_N
                for u, (name, value) in enumerate([("w_used", m * 3 - 2), ("p_up", m * 2 - 1), ("w_used", m * 3 - 1),
                                                   ("p_up", m * 2), ("w_used", m * 3), ("p_yd", m)]):
                    sp.wait_ge(sems[name], value)
                    load_unit(e, u)
            for t in range(NTT):
                wait(sp, "y_fin", t + 1)
                dst = o[0][0, P * t:P * (t + 1), :] if t < 2 else o[1].rearrange("b s d -> (b s) d")
                sp.dma_start(dst, x2[0:TN[t], t, :]).then_inc(sems["st_out"], 16)
            wait(sp, "st_out", 48)

        @block.gpsimd
        def _(g):
            c = Count(g)
            g.memset(ident[:], 0.0)
            c.done(g.memset(ones[:], 1.0), "ident_ok")
            c.done(g.affine_select(out=ident[:], in_=ident[:], compare_op=ALU.not_equal, fill=1.0, base=0,
                                   pattern=[[-1, P]], channel_multiplier=1), "ident_ok")
            c.done(g.affine_select(out=upi[:], in_=ones[:], compare_op=ALU.is_ge, fill=0.0, base=0,
                                   pattern=[[1, P]], channel_multiplier=-1), "masks_ok")
            us = upis[:].rearrange("p (b s) -> p b s", b=NB)
            c.done(g.affine_select(out=us, in_=upi[0:SMP, 0:SMP].rearrange("p (b s) -> p b s", b=NB),
                                   compare_op=ALU.is_ge, fill=0.0, base=0, pattern=[[-NS, NB], [0, NS]],
                                   channel_multiplier=1), "masks_ok")
            c.done(g.affine_select(out=seqm[:], in_=ones[0:SMP, 0:NB], compare_op=ALU.is_ge, fill=0.0, base=0,
                                   pattern=[[-NS, NB]], channel_multiplier=1), "masks_ok")
            c.done(g.affine_select(out=seqm[:], in_=seqm[:], compare_op=ALU.is_ge, fill=0.0, base=NS - 1,
                                   pattern=[[NS, NB]], channel_multiplier=-1), "masks_ok")
            g.memset(mu[:], 0)
            c.done(g.memset(ml, 0), "masks_ok")
            for l in range(LEVELS):
                w, nb = 1 << l, P >> (l + 1)
                for m, lo, hi in ((mu, w, 2 * w), (ml, 0, w)):
                    v = m[:, l, :].rearrange("p (b r) -> p b r", b=nb)[:, :, lo:hi]
                    c.done(g.memset(v, 1), "masks_ok")
                    other = 0 if m is mu else w
                    c.done(g.affine_select(out=v, in_=v, compare_op=ALU.is_ge, fill=0.0, base=-other,
                                           pattern=[[-2 * w, nb], [0, w]], channel_multiplier=1), "masks_ok")
                    c.done(g.affine_select(out=v, in_=v, compare_op=ALU.is_ge, fill=0.0, base=other + w - 1,
                                           pattern=[[2 * w, nb], [0, w]], channel_multiplier=-1), "masks_ok")
            c.done(g.tensor_copy(mone[:], ident[:]), "masks_ok")
            wait(g, "rst_in", 2)
            c.done(g.tensor_tensor(rst[:], rst[:], mhalf[:, 0:3], ALU.pow), "rst_ok")
            for u in range(3):
                wait(g, "proj_ok", 1 + 4 * (u + 1))
                d = cs[:, 4 * u:4 * u + 4, :]
                g.tensor_copy(d[:, :, 0:3], raw[:, :, SEQ:SEQ + 3])
                for n in range(4):
                    r = samples(raw[:, n, HEAD + SEQ:RAW])
                    i = g.tensor_copy(samples(d[:, n, 3:27]), r[:, :, NS:NS + HEAD])
                c.done(i, "cs_ok")
            wait(g, "ss8_ok", 4)
            c.done(g.tensor_tensor(rs8[:], ss8[:], mhalf[:], ALU.pow), "rs8_ok")

            wait(g, "csr_ok", 3)
            g.dma_start(o[2][0, 0], crow[0:3, :]).then_inc(sems["out_done"], 16)
            g.dma_start(o[5].rearrange("l b r c -> (l b r) c"), crow[3:27, :]).then_inc(sems["out_done"], 16)
            wait(g, "osq_ok", 4)
            c.done(g.tensor_tensor(rs8[:], ss8[:], mhalf[:], ALU.pow), "rs8_ok")

            c.done(g.tensor_tensor(tri[:], upi[:], ident[:], ALU.subtract), "tri_ok")
            c.done(g.iota(slots_io[:], pattern=[[1, CAP]], base=0, channel_multiplier=0,
                          allow_small_or_imprecise_dtypes=True), "tri_ok")
            wait(g, "p_smp", 4)
            wait(g, "o_ok", 1)
            for h in range(6):
                if h < 4:
                    st, dec = sgs[:, :, h, :], bc(egl[:, h, 2:10].unsqueeze(2), P, NB, P)
                    c.tick(g.tensor_tensor(st, st, dec, ALU.mult), "dec_ok")
                else:
                    st, dec = sls[:, h - 4], bc(ebl[:, h - 4, 2:10].unsqueeze(2), P, NB, P)
                    c.tick(g.tensor_tensor(st, st, dec, ALU.mult), "dec_ok")
                wait(g, "p_up_s", h)
                src = qkv[0:SMP, 2, QK + h * P:QK + (h + 1) * P] if h < 4 else kdg[0:SMP, 2, (h - 4) * P:(h - 3) * P]
                c.tick(g.tensor_tensor(kdm[0:SMP], bc(src.unsqueeze(1), SMP, NB, P), bc(seqm[:].unsqueeze(2), SMP, NB, P), ALU.mult), "kdm_ok")
            wait(g, "ch_ok", 5)
            wait(g, "gch_ok", 3)
            wait(g, "st_ok", 4)
            g.dma_start(o[3][0, 0].rearrange("h k v -> k h v"), sgp[:]).then_inc(sems["out_done"], 16)
            g.dma_start(o[6][0].rearrange("b h k v -> k (b h) v"), ring[:, 0:UNIT].rearrange("p (a v) -> p a v", v=P)).then_inc(sems["out_done"], 16)
            wait(g, "st_ok", 6)
            for r in range(2):
                g.dma_start(o[4][0, 0].rearrange("(j r) k v -> r k j v", r=2)[r], slp[64 * r:64 * r + 64]).then_inc(sems["out_done"], 16)
            for h in range(H):
                r = 64 * (h % 2)
                g.dma_start(o[7][0, :, h].rearrange("b k v -> k b v"), sls[r:r + 64, h // 2, :, :]).then_inc(sems["st_out2"], 16)
            wait(g, "ss2_ok", 3)
            wait(g, "rs2_in", 1)
            c.done(g.tensor_tensor(rst[:], rst[:], mhalf[:, 0:3], ALU.pow), "rst_ok")
            wait(g, "rs3_in", 1)
            c.done(g.tensor_tensor(rst[:], rst[:], mhalf[:, 0:3], ALU.pow), "rs3_ok")
            wait(g, "out_done", 16 * 6)
            wait(g, "st_out2", 64)

        @block.tensor
        def _(pe):
            c = Count(pe)

            def turn(out, src, n):
                return pe.transpose(out, src, ident[0:n, 0:n])

            wait(pe, "ident_ok", 2)
            wait(pe, "ld_vec", 80)
            c.tick(turn(bank[7][:, 0:60], vrow[:], 60), "p_vec")
            wait(pe, "h_ok", 3)
            for k in range(KT):
                wait(pe, "hT_ok", k - 3)
                for t in range(NTT):
                    i = turn(bank[k % 4][:, TO[t]:TO[t] + TN[t]], xt[0:TN[t], t, k * P:(k + 1) * P], TN[t])
                c.tick(i, "p_hT")
            wait(pe, "ld_cst", 16)
            for n in range(12):
                i = turn(bank[4][:, 24 * n:24 * n + 24], crow[0:24, n * P:(n + 1) * P], 24)
            c.tick(i, "p_cT")
            wait(pe, "ld_bias", 32)
            for n in range(6):
                i = turn(bank[5 + n // 4][:, P * (n % 4):P * (n % 4) + P], brow[:, n, :], P)
            c.tick(i, "p_bias")

            def project(u):
                wait(pe, f"w_in{1 + u % 2}", 16 * (u // 2 + 1))
                w = slot[1 + u % 2].rearrange("p (k n) -> p k n", k=KT)
                for n in range(4):
                    at = 1 + 4 * u + n
                    wait(pe, "proj_ok", at - 3)
                    for k in range(KT):
                        i = pe.matmul(bank[at % 4][:, 0:T], w[:, k, n * P:(n + 1) * P], hT[:, k, :],
                                      start=k == 0, stop=k == KT - 1)
                    c.tick(i, "p_proj")

            def conv_rows(u):
                if u < 3:
                    wait(pe, "conv_ok", u + 1)
                else:
                    wait(pe, "proj_ok", 21)
                for t in range(NTT):
                    at = 3 * u + t
                    wait(pe, "convt_ok", at - 2)
                    for n in range(4):
                        i = turn(bank[4 + at % 3][0:TN[t], n * P:(n + 1) * P],
                                 convT[:, n, TO[t]:TO[t] + TN[t]], P)
                    c.tick(i, "p_convt")

            wait(pe, "hT_ok", 8)
            wait(pe, "ld_sm", 48)
            wait(pe, "v_step", 1)
            for k in range(KT):
                i = pe.matmul(bank[0][0:80, 0:T], wsm[:, k, :], hT[:, k, :], start=k == 0, stop=k == KT - 1)
            c.tick(i, "p_proj")
            project(0)
            wait(pe, "cT_ok", 1)
            wait(pe, "bias_ok", 2)
            conv_rows(0)
            project(1)
            conv_rows(1)
            project(2)
            conv_rows(2)
            project(3)
            wait(pe, "ld_gate", 48)
            wait(pe, "convt_ok", 9)
            for j in range(2):
                i = pe.matmul(bank[5 + j][:, 0:T], gkw[64:80, j * P:(j + 1) * P], sm[64:80, :], start=True, stop=True)
            c.tick(i, "p_gk")
            wait(pe, "gb_ok", 1)
            for t in range(NTT):
                i = turn(bank[7][0:TN[t], 68 * t:68 * t + 68], gb[:, TO[t]:TO[t] + TN[t]], 68)
            c.tick(i, "p_gt")
            project(4)
            wait(pe, "gk_x", 1)
            conv_rows(3)
            wait(pe, "cs_ok", 3)
            wait(pe, "gt_ok", 3)
            wait(pe, "convt_ok", 12)
            for n in range(12):
                i = turn(bank[4 + n // 4][0:27, (n % 4) * P:(n % 4) * P + P], cs[:, n, :], P)
            c.tick(i, "p_csr")
            project(5)
            project(6)

            for t in range(NTT):
                n = TN[t]
                wait(pe, "qkn_ok", 3 * (t + 1))
                for j in range(3):
                    at = 3 * t + j
                    wait(pe, "qkT_ok", at - 3)
                    src = qkv[0:n, t, (QK, 0, 3 * QK)[j]:(QK, 0, 3 * QK)[j] + QK] if j < 2 else kb[0:n, :]
                    for h in range(H):
                        i = turn(bank[4 + at % 4][:, h * n:(h + 1) * n], src[:, h * P:(h + 1) * P], n)
                    c.tick(i, "p_qkT")
            wait(pe, "proj_ok", 29)
            for t in range(NTT):
                n = TN[t]
                pe.matmul(bank[t][0:n, 0:H * n], ones[0:4, 0:n], gdiag[0:4, :, TO[t]:TO[t] + n], start=True, stop=True)
            pe.matmul(bank[3][:, 0:8], ones[0:4, :], gdiag[0:4, :, P - 1:SEQ:P], start=True, stop=True)
            c.tick(pe.matmul(bank[3][:, 8:40], ones[0:4, :], gdiag[0:4, :, SEQ + NS - 1:T:NS], start=True, stop=True), "p_gi")
            wait(pe, "qkT_ok", 9)
            wait(pe, "di_ok", 4)
            for t in range(NTT):
                n = TN[t]
                tok = slice(TO[t], TO[t] + n)
                for j in range(2):
                    b = bank[(4, 5, 6, 7, 0, 1)[2 * t + j]]
                    for h in range(H):
                        i = pe.matmul(b[0:n, h * n:(h + 1) * n], KQ[:, 0, h, tok],
                                      (kbT[:, h, tok], KQ[:, 1, h, tok])[j], start=True, stop=True)
                    c.tick(i, "p_MA")
            for t in range(NTT):
                n = TN[t]
                wait(pe, "MA_ok", 2 * t + 1)
                for h in range(H):
                    i = turn(bank[2 + t][0:n, h * n:(h + 1) * n], NMt[t][:, h, :], n)
                c.tick(i, "p_tm")
            wait(pe, "MA_ok", 6)
            for k, (l, t) in enumerate(INV):
                n = TN[t]
                by, bt, bu = ((0, 1, 2), (3, 5, 6), (7, 4, 4))[t]
                uo = H * n if bu == bt else 0
                wait(pe, "inv_ok", inv_at[l - 1, t])
                for h in range(H):
                    i = pe.matmul(bank[by][0:n, h * n:(h + 1) * n], NMt[t][:, h, :], Tt[t][:, h, :], start=True, stop=True)
                c.tick(i, "p_y")
                wait(pe, "y_ok", k + 1)
                for h in range(H):
                    pe.matmul(bank[bt][0:n, h * n:(h + 1) * n], Ut[t][:, h, :], Yt[t][:, h, :], start=True, stop=True)
                for h in range(H):
                    i = pe.matmul(bank[bu][0:n, uo + h * n:uo + (h + 1) * n], Yt[t][:, h, :], Ut[t][:, h, :], start=True, stop=True)
                c.tick(i, "p_inv")
            vr = lambda t, h: qkv[0:TN[t], t, 2 * QK + h * P:2 * QK + (h + 1) * P]
            kr = lambda t, h: qkv[0:TN[t], t, QK + h * P:QK + (h + 1) * P]
            nr = lambda t, h: vn[0:TN[t], t, h * P:(h + 1) * P]

            def heads(b, lhs, rhs, name, n=P):
                for h in range(H):
                    i = pe.matmul(b[0:n, h * P:(h + 1) * P], lhs(h), rhs(h), start=True, stop=True)
                if name:
                    c.tick(i, name)

            wait(pe, "inv_ok", 3 + len(INV))
            wait(pe, "vd_ok", 6)
            heads(bank[0], lambda h: Ut[0][:, h, :], lambda h: vr(0, h), "p_ch")
            wait(pe, "ch_ok", 1)
            heads(bank[1], lambda h: kr(0, h), lambda h: nr(0, h), "p_ch")
            heads(bank[5], lambda h: Att[0][:, h, :], lambda h: nr(0, h), None)
            wait(pe, "ch_ok", 2)
            heads(bank[2], lambda h: KQ[:, 0, h, P:SEQ], lambda h: sgp[:, h, :], None)
            heads(bank[3], lambda h: KQ[:, 1, h, P:SEQ], lambda h: sgp[:, h, :], "p_ch")
            wait(pe, "ch_ok", 3)
            heads(bank[0], lambda h: Ut[1][:, h, :], lambda h: vr(1, h), "p_ch")
            wait(pe, "ch_ok", 4)
            heads(bank[1], lambda h: kr(1, h), lambda h: nr(1, h), "p_ch")
            heads(bank[6], lambda h: Att[1][:, h, :], lambda h: nr(1, h), "p_ch")
            wait(pe, "ld_st", 128)
            for b in range(NB):
                for h in range(H):
                    ov = bank[7][:, 64 * h:64 * h + 64].rearrange("p (a i) -> p a i", a=2)[:, :, NS * b:NS * (b + 1)]
                    i = pe.matmul(ov, sgs[:, b, h, :], KQ[:, :, h, SEQ + NS * b:SEQ + NS * (b + 1)], start=True, stop=True)
            c.tick(i, "p_smp")
            wait(pe, "smk_ok", 1)
            for h in range(H):
                for j in range(2):
                    i = turn(bank[(4, 7)[j]][0:SMP, h * P:(h + 1) * P], skT[:].rearrange("p a b -> p (a b)")[:, 64 * h + 32 * j:64 * h + 32 * j + 32], P)
            c.tick(i, "p_smp")
            wait(pe, "smr_ok", 1)
            heads(bank[4], lambda h: Ut[2][:, h, :], lambda h: vr(2, h), "p_smp", SMP)
            wait(pe, "smr_ok", 2)
            heads(bank[4], lambda h: Att[2][:, h, :], lambda h: nr(2, h), "p_smp", SMP)

            wait(pe, "ch_ok", 6)
            wait(pe, "smr_ok", 3)
            for k in range(LEVELS + 1):
                gq, gk = (gqk[:, 0:2, :], gqk[:, 2:4, :]) if k == 0 else (gQ, gK)
                wait(pe, "g_lvl", k)
                wait(pe, "ag_ok", k - 1)
                b0 = 2 * (k % 2)
                for r in range(2):
                    rows_ = slice(64 * r, 64 * r + 64)
                    for t in range(2):
                        for j in range(2):
                            m = 2 * t + j
                            i = pe.matmul(bank[b0 + r][:, m * P:(m + 1) * P], gk[rows_, j, TO[t]:TO[t] + P],
                                          gq[rows_, j, TO[t]:TO[t] + P], start=True, stop=True)
                if k < 3:
                    wait(pe, "ag_ok", k)
                    for r in range(2):
                        rows_ = slice(64 * r, 64 * r + 64)
                        for j in range(2):
                            i = pe.matmul(bank[4 + r][0:SMP, j * SMP:(j + 1) * SMP], gk[rows_, j, SEQ:T],
                                          gq[rows_, j, SEQ:T], start=True, stop=True)
                c.tick(i, "p_glvl")
            wait(pe, "g_lvl", LEVELS + 1)
            wait(pe, "ag_ok", LEVELS + 1)
            for t in range(NTT):
                for j in range(2):
                    i = turn(bank[t][0:TN[t], j * P:(j + 1) * P], gK[:, j, TO[t]:TO[t] + TN[t]], P)
            c.tick(i, "p_gkd")
            vgr = lambda t, h: vg[0:TN[t], t, h * P:(h + 1) * P]

            def gla_state(t):
                for h in range(H):
                    r = 64 * (h % 2)
                    i = pe.matmul(bank[4][r:r + 64, (h // 2) * P:(h // 2) * P + P], kdg[:, t, 64 * h:64 * h + 64],
                                  vgr(t, h), start=True, stop=True)
                c.tick(i, "p_gch")

            wait(pe, "kdg_ok", 3)
            gla_state(0)
            heads(bank[3], lambda h: AGt[0][:, h, :], lambda h: vgr(0, h), None)
            heads(bank[7], lambda h: AGt[1][:, h, :], lambda h: vgr(1, h), None)
            wait(pe, "gch_ok", 1)
            for h in range(H):
                r = 64 * (h % 2)
                i = pe.matmul(bank[5 + h % 2][:, (h // 2) * P:(h // 2) * P + P], gQ[r:r + 64, h // 2, P:SEQ],
                              slp[r:r + 64, h // 2, :], start=True, stop=True)
            c.tick(i, "p_gch")
            gla_state(1)
            for b in range(NB):
                for h in range(H):
                    r = 64 * (h % 2)
                    at = 32 * (h // 2) + NS * b
                    i = pe.matmul(bank[h % 2][:, at:at + NS], sls[r:r + 64, h // 2, b, :],
                                  gQ[r:r + 64, h // 2, SEQ + NS * b:SEQ + NS * (b + 1)], start=True, stop=True)
            c.tick(i, "p_gs")
            wait(pe, "gsT_ok", 2)
            for h in range(H):
                i = turn(bank[2][0:SMP, h * P:(h + 1) * P], skT[:, h % 2, 32 * (h // 2):32 * (h // 2) + 32], P)
            wait(pe, "gch_ok", 3)
            heads(bank[4], lambda h: AGt[2][:, h, :], lambda h: vgr(2, h), "p_gs", SMP)
            for t in range(NTT):
                n = TN[t]
                wait(pe, "o_ok", t + 1)
                for j in range(2):
                    at = 2 * t + j
                    wait(pe, "oT_ok", at - 1)
                    for h in range(H):
                        i = turn(bank[at % 2][:, h * n:(h + 1) * n], ot[0:n, t, (4 * j + h) * P:(4 * j + h + 1) * P], n)
                    c.tick(i, "p_oT")
            wait(pe, "oT_ok", 6)
            for u in range(2):
                wait(pe, "w_out", 16 * (u + 1)) if u == 0 else wait(pe, "w_out2", 16)
                w = slot[2 - u].rearrange("p (k n) -> p k n", k=KT)
                for n in range(4):
                    at = 29 + 4 * u + n
                    wait(pe, "proj_ok", at - 3)
                    for k in range(KT):
                        i = pe.matmul(bank[at % 4][:, 0:T], w[:, k, n * P:(n + 1) * P], zg[:, k, :],
                                      start=k == 0, stop=k == KT - 1)
                    c.tick(i, "p_proj")

            for h in range(6):
                wait(pe, "kdm_ok", h + 1)
                b0 = (4, 6)[h % 2]
                wait(pe, "st_ok", h - 1)
                for b in range(NB):
                    ob_ = bank[b0 + b // 4]
                    cols = slice((b % 4) * P, (b % 4) * P + P)
                    if h < 4:
                        i = pe.matmul(ob_[:, cols], kdm[0:SMP, b, :], vn[0:SMP, 2, h * P:(h + 1) * P], start=True, stop=True)
                    else:
                        for r in range(2):
                            hh = 2 * (h - 4) + r
                            i = pe.matmul(ob_[64 * r:64 * r + 64, cols], kdm[0:SMP, b, 64 * r:64 * r + 64],
                                          vg[0:SMP, 2, hh * P:(hh + 1) * P], start=True, stop=True)
                c.tick(i, "p_up_s")
            wait(pe, "proj_ok", 37)
            wait(pe, "st_ok", 6)
            for t in range(NTT):
                for j in range(2):
                    at = 2 * t + j
                    wait(pe, "x2_ok", at - 3)
                    for n in range(4):
                        i = turn(bank[4 + at % 4][0:TN[t], n * P:(n + 1) * P], hT[:, 4 * j + n, TO[t]:TO[t] + TN[t]], P)
                    c.tick(i, "p_x2")
            wait(pe, "xn_ok", 3)
            for k in range(KT):
                wait(pe, "xnT_ok", k - 3)
                for t in range(NTT):
                    i = turn(bank[k % 4][:, TO[t]:TO[t] + TN[t]], ot[0:TN[t], t, k * P:(k + 1) * P], TN[t])
                c.tick(i, "p_xnT")
            wait(pe, "xnT_ok", 8)
            wait(pe, "ld_router", 32)
            for t in range(NTT):
                for k in range(KT):
                    i = pe.matmul(bank[4][0:TN[t], E_N * t:E_N * (t + 1)], hT[:, k, TO[t]:TO[t] + TN[t]], wr[:, k, :],
                                  start=k == 0, stop=k == KT - 1)
            c.tick(i, "p_lg")
            wait(pe, "route_ok", 1)
            wait(pe, "tri_ok", 2)
            sel = lambda t: selm[0:TN[t], E_N * t:E_N * (t + 1)]
            for t in range(NTT):
                for t2 in range(t + 1):
                    lhs = ones[0:TN[t2], 0:TN[t]] if t2 < t else tri[0:TN[t], 0:TN[t]]
                    pe.matmul(bank[5][0:TN[t], E_N * t:E_N * (t + 1)], lhs, sel(t2), start=t2 == 0, stop=t2 == t)
            for t in range(NTT):
                i = pe.matmul(bank[6][0:32, 0:E_N], ones[0:TN[t], 0:32], sel(t), start=t == 0, stop=t == NTT - 1)
            c.tick(i, "p_pos")

            def rows_of_y(w):
                pe.wait_ge(sems["yb_ok"], w * 2 + 1)
                pe.wait_ge(sems["yr_ok"], w * 2 + 1)
                for j in range(2):
                    for n in range(4):
                        i = turn(bank[5 + j][:, n * P:(n + 1) * P], yT[:, 4 * j + n, :], P)
                    i.then_inc(sems["p_ty"], 1)

            def scatter(w):
                pe.wait_ge(sems["yr_ok"], w * 2 + 3)
                for d in range(KT):
                    if d >= 2:
                        pe.wait_ge(sems["sc_ok"], w * 8 + d)
                    pe.matmul(bank[(7, 3)[d % 2]][:, 0:T], yr[:, d * P:(d + 1) * P], S, start=True, stop=True).then_inc(sems["p_sc"], 1)

            def up_half(i, q, hf):
                for kh in range(2):
                    u = 2 * hf + kh
                    pe.wait_ge(sems[f"ld_w{u}"], i * 128 + 64 * (q + 1))
                    w = slot[WSLOT[u]].rearrange("p (k n) -> p k n", k=4)
                    for n in range(8):
                        for kk in range(4):
                            k = 4 * kh + kk
                            last = pe.matmul(bank[hf][:, n * CAP:(n + 1) * CAP], w[:, kk, n * P:(n + 1) * P],
                                             xeT[:, k, q * CAP:(q + 1) * CAP], start=n == 0 and k == 0, stop=k == KT - 1,
                                             skip_group_check=True)
                    if kh == 0:
                        last.then_inc(sems["w_used"], 1)
                    else:
                        last.then_inc(sems["p_up"], 1)

            def down(i, q):
                for hf in range(2):
                    u = 4 + hf
                    pe.wait_ge(sems["act_ok"], i * 4 + (2 * q + hf + 1))
                    pe.wait_ge(sems[f"ld_w{u}"], i * 32 + 16 * (q + 1))
                    w = slot[WSLOT[u]].rearrange("p (k n) -> p k n", k=4)
                    for kk in range(4):
                        k = 4 * hf + kk
                        for n in range(8):
                            last = pe.matmul(bank[2][:, n * CAP:(n + 1) * CAP], w[:, kk, n * P:(n + 1) * P], aT[:, k, :],
                                             start=n == 0 and k == 0, stop=k == KT - 1, skip_group_check=True)
                    if hf == 0:
                        last.then_inc(sems["w_used"], 1)
                    else:
                        last.then_inc(sems["p_yd"], 1)

            wait(pe, "rnd_ok", 1)
            wait(pe, "p_S", 1)
            rounds = pe.value_load(rnd[0:1, 0:1], min_val=1, max_val=5)
            with pe.Fori(0, rounds * PAIRS) as i:
                pe.wait_ge(sems["G_ok"], i * 2 + 1)
                pe.wait_ge(sems["sc_ok"], i * 8 + 1)
                pe.wait_ge(sems["S_ok"], i + 1)
                for j in range(2):
                    for n in range(4):
                        d = 4 * j + n
                        for t in range(NTT):
                            last = pe.matmul(bank[3 + j][:, n * P:(n + 1) * P], ot[0:TN[t], t, d * P:(d + 1) * P], G[0:TN[t], t, :],
                                             start=t == 0, stop=t == NTT - 1)
                    last.then_inc(sems["p_gat"], 1)
                pe.wait_ge(sems["xe_ok"], i * 2 + 2)
                up_half(i, 0, 0)
                rows_of_y(i)
                up_half(i, 0, 1)
                scatter(i)
                pe.wait_ge(sems["G_ok"], i * 2 + 2)
                for t in range(NTT):
                    last = turn(bank[4][:, TO[t]:TO[t] + TN[t]], GG[0:TN[t], t, :], TN[t])
                last.then_inc(sems["p_S"], 1)
                down(i, 0)
                up_half(i, 1, 0)
                up_half(i, 1, 1)
                pe.wait_ge(sems["yb_ok"], i * 2 + 2)
                down(i, 1)
            total = rounds * PAIRS
            pe.wait_ge(sems["S_ok"], total + 1)
            pe.wait_ge(sems["sc_ok"], total * 8 + 1)
            rows_of_y(total)
            scatter(total)
            pe.wait_ge(sems["sc_ok"], total * 8 + 9)
            for t in range(NTT):
                for j in range(2):
                    at = 2 * t + j
                    wait(pe, "fin_x", at - 3)
                    for n in range(4):
                        i = turn(bank[at % 4][0:TN[t], n * P:(n + 1) * P], hT[:, 4 * j + n, TO[t]:TO[t] + TN[t]], P)
                    c.tick(i, "p_fin")

        @block.vector
        def _(v):
            c = Count(v)
            v.memset(wsm[:, :, 4:32], 0.0)
            c.done(v.memset(wsm[:, :, 36:64], 0.0), "v_step")
            v.memset(ss[:], 1.0)
            v.memset(ss8[:], 1.0)
            v.memset(mhalf[:], -0.5)
            v.memset(gb[:], 0.0)
            v.memset(resets[:], 1.0)
            c.done(v.memset(gt[:], 0.0), "v_step")
            c.done(v.memset(resets[:, 0:SEQ:P], 0.0), "v_step")
            c.done(v.memset(resets[:, SEQ:T:NS], 0.0), "v_step")
            c.done(v.memset(rst[:], 1.0), "rst_in")
            wait(v, "ss_ok", 3)
            c.done(v.tensor_scalar(rst[:], ss[:], 1.0 / D, EPS, ALU.mult, ALU.add), "rst_in")
            wait(v, "rst_ok", 1)
            for t in range(NTT):
                n = TN[t]
                c.done(v.tensor_scalar(xt[0:n, t, :], xt[0:n, t, :], rst[0:n, t:t + 1], None, ALU.mult), "h_ok")
            wait(v, "p_vec", 1)
            c.done(v.tensor_copy(vecT[:], bank[7][:, 0:60]), "vec_ok")
            for k in range(KT):
                wait(v, "p_hT", k + 1)
                c.done(v.tensor_scalar(hT[:, k, :], bank[k % 4][:, 0:T], vecT[:, k:k + 1], None, ALU.mult), "hT_ok")
            wait(v, "p_cT", 1)
            c.done(v.tensor_copy(cT[:].rearrange("p a b -> p (a b)"), bank[4][:, 0:288]), "cT_ok")
            wait(v, "p_bias", 1)
            c.done(v.tensor_copy(biasT[:, 0:4, :].rearrange("p a b -> p (a b)"), bank[5][:]), "bias_ok")
            c.done(v.tensor_copy(biasT[:, 4:6, :].rearrange("p a b -> p (a b)"), bank[6][:, 0:256]), "bias_ok")

            wait(v, "proj_ok", 1)
            wait(v, "ld_gate", 48)
            c.done(v.tensor_scalar(gtmp[0:4, 0, :], sm[0:4, :], gate2[:, 1:2], None, ALU.add), "v_step")
            c.tick(v.scalar_tensor_tensor(out=gtmp[0:4, 1, :], in0=gtmp[0:4, 0, :], scalar=-1.0, in1=gtmp[0:4, 0, :],
                                          op0=ALU.mult, op1=ALU.max), "gate_x")

            def conv(u):
                wait(v, "proj_ok", 1 + 4 * (u + 1))
                hist = cT[:, 4 * u:4 * u + 4, :]
                c.done(v.memset(raw[:, :, 0:HEAD], 0.0), "v_step")
                for n in range(4):
                    c.done(v.tensor_copy(samples(raw[:, n, HEAD + SEQ:RAW])[:, :, 0:HEAD], samples(hist[:, n, :])), "v_step")
                for i in range(4):
                    for n in range(4):
                        w = vecT[:, 8 + 12 * i + 4 * u + n:9 + 12 * i + 4 * u + n]
                        if i == 0:
                            c.done(v.tensor_scalar(ce[:, n, 0:CW], raw[:, n, 0:CW], w, None, ALU.mult), "v_step")
                        else:
                            c.done(v.scalar_tensor_tensor(out=ce[:, n, 0:CW], in0=raw[:, n, i:i + CW], scalar=w,
                                                          in1=ce[:, n, 0:CW], op0=ALU.mult, op1=ALU.add), "v_step")
                c.tick(v.memset(ss[:, 0:1], 1.0), "conv_lin")
                wait(v, "conv_sig", u + 1)
                e = raw[:, :, 0:CW]
                c.done(v.tensor_tensor(convT[:, :, 0:SEQ], ce[:, :, 0:SEQ], e[:, :, 0:SEQ], ALU.mult), "v_step")
                at = HEAD + SEQ
                for n in range(4):
                    r = lambda b: b[:, n, at:RAW].rearrange("p (b j) -> p b j", b=NB)[:, :, 0:NS]
                    i = v.tensor_tensor(convT[:, n, SEQ:T].rearrange("p (b j) -> p b j", b=NB), r(ce), r(raw), ALU.mult)
                c.done(i, "conv_ok")

            def rows(u):
                for t in range(NTT):
                    at = 3 * u + t
                    wait(v, "p_convt", at + 1)
                    dst = qkv[0:TN[t], t, QK * u:QK * (u + 1)] if u < 3 else vg[0:TN[t], t, :]
                    c.done(v.tensor_copy(dst, bank[4 + at % 3][0:TN[t], :]), "convt_ok")

            conv(0)
            wait(v, "gate_e", 3)
            wait(v, "gate_l", 1)
            g0 = gtmp[0:4, 0, :]
            c.done(v.tensor_scalar(g0, g0, 0.0, None, ALU.max), "v_step")
            c.done(v.tensor_tensor(g0, g0, gtmp[0:4, 1, :], ALU.add), "v_step")
            c.done(v.tensor_scalar(g0, g0, gate2[:, 2:3], -1.0, ALU.mult, ALU.mult), "v_step")
            c.done(v.tensor_tensor_scan(gb[0:4, :], resets[0:4, :], g0, 0.0, ALU.mult, ALU.add), "v_step")
            be = gtmp[32:36, 0, :]
            c.done(v.tensor_scalar(be, be, 1.0, None, ALU.add), "v_step")
            c.done(v.reciprocal(gb[32:36, :], be), "v_step")
            gp = gb[0:4, 0:SEQ].rearrange("p (c i) -> p c i", c=2)
            gs = gb[0:4, SEQ:T].rearrange("p (b j) -> p b j", b=NB)
            dp = gb[64:68, 0:SEQ].rearrange("p (c i) -> p c i", c=2)
            ds = gb[64:68, SEQ:T].rearrange("p (b j) -> p b j", b=NB)
            v.tensor_tensor(dp, bc(gp[:, :, P - 1:P], 4, 2, P), gp, ALU.subtract)
            v.tensor_tensor(ds, bc(gs[:, :, NS - 1:NS], 4, NB, NS), gs, ALU.subtract)
            c.done(v.tensor_tensor(gdiag[0:4], bc(gb[0:4, :].unsqueeze(1), 4, H, T),
                                   bc(ident[0:4, 0:4].unsqueeze(2), 4, H, T), ALU.mult), "gb_ok")
            rows(0)
            conv(1)
            rows(1)
            conv(2)
            rows(2)
            wait(v, "p_gk", 1)
            for j in range(2):
                c.done(v.tensor_scalar(gE[:, j, :], bank[5 + j][:, 0:T], vecT[:, 56 + j:57 + j], None, ALU.add), "v_step")
            c.tick(v.scalar_tensor_tensor(out=gQ, in0=gE, scalar=-1.0, in1=gE, op0=ALU.mult, op1=ALU.max), "gk_x")
            wait(v, "p_gt", 1)
            for t in range(NTT):
                c.done(v.tensor_copy(gt[0:TN[t], t, :], bank[7][0:TN[t], 68 * t:68 * t + 68]), "gt_ok")
            wait(v, "gk_l", 1)
            c.done(v.tensor_scalar(gE, gE, 0.0, None, ALU.min), "v_step")
            c.done(v.tensor_tensor(gE, gE, gQ, ALU.subtract), "v_step")
            c.done(v.tensor_scalar(gE, gE, 1.0 / 16, None, ALU.mult), "v_step")
            for j in range(2):
                c.done(v.tensor_tensor_scan(bT[:, j, :], resets[:], gE[:, j, :], 0.0, ALU.mult, ALU.add), "bT_ok")
            rows(3)
            wait(v, "p_csr", 1)
            for n in range(3):
                c.done(v.tensor_copy(crow[0:27, 512 * n:512 * (n + 1)], bank[4 + n][0:27, :]), "csr_ok")
            for u in range(2):
                wait(v, "proj_ok", 25 + 4 * u)
                z = zg[:, 4 * u:4 * u + 4, :]
                c.done(v.tensor_tensor(z, z, ce_z, ALU.mult), "zg_ok")

            for t in range(NTT):
                n = TN[t]
                wait(v, "h_ok", 3)
                sq = ob[0:n, 0:2 * QK]
                c.done(v.tensor_tensor(sq, qkv[0:n, t, 0:2 * QK], qkv[0:n, t, 0:2 * QK], ALU.mult), "v_step")
                c.done(v.tensor_reduce(ss8[0:n, 8 * t:8 * t + 8], sq.rearrange("p (a d) -> p a d", d=P), AX_X, ALU.add), "ss8_ok")
            c.done(v.tensor_scalar(ss8[:], ss8[:], EPS, None, ALU.add), "ss8_ok")
            wait(v, "rs8_ok", 1)
            r8 = rs8[:].rearrange("p (t a) -> p t a", t=3)
            c.done(v.tensor_scalar(r8[:, :, 0:4], r8[:, :, 0:4], float(P) ** -0.5, None, ALU.mult), "v_step")

            def hd(ap):
                return ap.rearrange("p (a d) -> p a d", d=P)

            wait(v, "gt_exp", 3)
            for t in range(NTT):
                n = TN[t]
                q, k, vv = (hd(qkv[0:n, t, QK * j:QK * (j + 1)]) for j in range(3))
                beta = bc(gt[0:n, t, 32:36].unsqueeze(2), n, H, P)
                c.done(v.tensor_tensor(hd(qkv[0:n, t, 0:2 * QK]), hd(qkv[0:n, t, 0:2 * QK]), bc(r8[0:n, t, :].unsqueeze(2), n, 8, P), ALU.mult), "qkn_ok")
                wait(v, "p_qkT", 3 * t)
                c.done(v.tensor_tensor(hd(kb[0:n, :]), k, beta, ALU.mult), "qkn_ok")
                c.done(v.tensor_tensor(vv, vv, beta, ALU.mult), "qkn_ok")
            c.done(v.tensor_tensor(nbeg[:], gt[:, :, 32:36], eg[:], ALU.mult), "v_step")
            c.done(v.tensor_scalar(nbeg[:], nbeg[:], -1.0, None, ALU.mult), "v_step")
            wait(v, "p_gi", 1)
            wait(v, "out_done", 32)
            for t in range(NTT):
                n = TN[t]
                for h in range(H):
                    i = v.tensor_scalar(Dtt[t][:, h, :], bank[t][0:n, h * n:(h + 1) * n], gt[0:n, t, h:h + 1], 0.0, ALU.subtract, ALU.min)
                c.done(i, "di_ok")
            v.tensor_copy(egl[:, :, 0:2], bank[3][:, 0:8].rearrange("p (h x) -> p h x", h=H))
            c.done(v.tensor_copy(egl[:, :, 2:10], bank[3][:, 8:40].rearrange("p (h x) -> p h x", h=H)), "di_ok")
            wait(v, "dexp_ok", 4)
            wait(v, "masks_ok", 48)
            for t in range(NTT):
                n = TN[t]
                m = upi[:] if t < 2 else upis[:]
                c.done(v.tensor_tensor(Dtt[t], Dtt[t], bc(m.unsqueeze(1), n, H, n), ALU.mult), "d_ok")
            for t in range(NTT):
                n = TN[t]
                for j in range(2):
                    wait(v, "p_MA", 2 * t + j + 1)
                    b = bank[(4, 5, 6, 7, 0, 1)[2 * t + j]][0:n, 0:H * n].rearrange("p (h i) -> p h i", h=H)
                    if j == 0:
                        c.done(v.scalar_tensor_tensor(out=NMt[t], in0=b, scalar=-1.0, in1=Dtt[t], op0=ALU.mult, op1=ALU.mult), "MA_ok")
                    else:
                        c.done(v.tensor_tensor(Att[t], b, Dtt[t], ALU.mult), "MA_ok")
            for t in range(NTT):
                n = TN[t]
                eye = bc(ident[0:n, 0:n].unsqueeze(1), n, H, n)
                v.tensor_copy(Ut[t], eye)
                c.done(v.tensor_copy(Tt[t], eye), "v_step")
                wait(v, "p_tm", t + 1)
                v.copy_predicated(Ut[t], bc(mu[0:n, 0, 0:n].unsqueeze(1), n, H, n), NMt[t])
                c.done(v.copy_predicated(Tt[t], bc(ml[0:n, 0, 0:n].unsqueeze(1), n, H, n),
                                         bank[2 + t][0:n, 0:H * n].rearrange("p (h i) -> p h i", h=H)), "inv_ok")
            for t in range(NTT):
                n = TN[t]
                k = hd(qkv[0:n, t, QK:2 * QK])
                c.done(v.tensor_tensor(k, k, bc(ekd[0:n, t, :].unsqueeze(2), n, H, P), ALU.mult), "vd_ok")
            for k, (l, t) in enumerate(INV):
                n = TN[t]
                bt, bu = ((1, 2), (5, 6), (4, 4))[t]
                uo = H * n if bu == bt else 0
                wait(v, "p_inv", k + 1)
                v.copy_predicated(Tt[t], bc(ml[0:n, l, 0:n].unsqueeze(1), n, H, n), bank[bt][0:n, 0:H * n].rearrange("p (h i) -> p h i", h=H))
                c.done(v.copy_predicated(Ut[t], bc(mu[0:n, l, 0:n].unsqueeze(1), n, H, n),
                                         bank[bu][0:n, uo:uo + H * n].rearrange("p (h i) -> p h i", h=H)), "inv_ok")
            for t in range(3):
                c.tick(v.memset(ss[:, t:t + 1], 1.0), "vd_ok")

            def col(ap, n):
                return bc(ap.unsqueeze(2), n, H, P)

            wait(v, "p_ch", 1)
            c.done(v.tensor_copy(vn[:, 0, :], bank[0][:]), "ch_ok")
            wait(v, "p_ch", 2)
            c.done(v.tensor_copy(sgp[:].rearrange("p h d -> p (h d)"), bank[1][:]), "ch_ok")
            wait(v, "p_ch", 3)
            tmp = hd(vn[:, 1, :])
            c.done(v.tensor_tensor(tmp, hd(bank[2][:]), col(nbeg[:, 1, :], P), ALU.mult), "v_step")
            vv = qkv[:, 1, 2 * QK:3 * QK]
            c.done(v.tensor_tensor(vv, vv, vn[:, 1, :], ALU.add), "ch_ok")
            o1 = ot[:, 1, 0:QK]
            c.done(v.tensor_tensor(hd(o1), hd(bank[3][:]), col(eg[:, 1, :], P), ALU.mult), "v_step")
            wait(v, "p_ch", 4)
            c.done(v.tensor_copy(vn[:, 1, :], bank[0][:]), "ch_ok")
            wait(v, "p_ch", 5)
            c.done(v.tensor_tensor(sgp[:], sgp[:], bc(egl[:, :, 1:2], P, H, P), ALU.mult), "v_step")
            c.done(v.tensor_tensor(sgp[:].rearrange("p h d -> p (h d)"), sgp[:].rearrange("p h d -> p (h d)"), bank[1][:], ALU.add), "ch_ok")
            wait(v, "p_ch", 6)
            v.tensor_copy(ot[:, 0, 0:QK], bank[5][:])
            c.done(v.tensor_tensor(o1, o1, bank[6][:], ALU.add), "ch_ok")
            wait(v, "p_smp", 2)
            os_ = ot[0:SMP, 2, 0:QK]
            vs = qkv[0:SMP, 2, 2 * QK:3 * QK]
            c.done(v.tensor_tensor(hd(vn[0:SMP, 2, :]), hd(bank[4][0:SMP, :]), col(nbeg[0:SMP, 2, :], SMP), ALU.mult), "v_step")
            v.tensor_tensor(hd(os_), hd(bank[7][0:SMP, :]), col(eg[0:SMP, 2, :], SMP), ALU.mult)
            c.done(v.tensor_tensor(vs, vs, vn[0:SMP, 2, :], ALU.add), "smr_ok")
            wait(v, "p_smp", 3)
            c.done(v.tensor_copy(vn[0:SMP, 2, :], bank[4][0:SMP, :]), "smr_ok")
            wait(v, "p_smp", 4)
            c.done(v.tensor_tensor(os_, os_, bank[4][0:SMP, :], ALU.add), "smr_ok")

            v.memset(AG[:], 0.0)
            c.done(v.memset(AGs[:], 0.0), "v_step")

            def level(l):
                w = 1 << l
                n = T if l < 2 else SEQ
                b4 = bT[:, :, 0:n].rearrange("p j (b r) -> p j b r", r=2 * w)
                e4 = gE[:, :, 0:n].rearrange("p j (b r) -> p j b r", r=2 * w)
                nb = n // (2 * w)
                e = gE[:, :, 0:n]
                c.done(v.tensor_tensor(e4, b4, bc(b4[:, :, :, w - 1:w], P, 2, nb, 2 * w), ALU.subtract), "v_step")
                c.done(v.scalar_tensor_tensor(out=e, in0=e, scalar=-1.0, in1=e, op0=ALU.mult, op1=ALU.min), "g_abs")
                wait(v, "g_exp", l + 1)
                if l > 0:
                    wait(v, "p_glvl", l + 1)
                v.tensor_tensor(gQ[:, :, 0:n], gqk[:, 0:2, 0:n], e, ALU.mult)
                c.done(v.tensor_tensor(gK[:, :, 0:n], gqk[:, 2:4, 0:n], e, ALU.mult), "g_lvl")

            def gather(k):
                wait(v, "p_glvl", k + 1)
                m = mone[:] if k == 0 else mu[:, k - 1, :]
                for r in range(2):
                    dst = AG[:].rearrange("p (q r) i -> p q r i", r=2)[:, :, r, :]
                    i = v.copy_predicated(dst, bc(m.unsqueeze(1), P, 4, P), bank[2 * (k % 2) + r][:].rearrange("p (q i) -> p q i", q=4))
                if k < 3:
                    for r in range(2):
                        dst = AGs[0:SMP].rearrange("p (q r) i -> p q r i", r=2)[:, :, r, :]
                        i = v.copy_predicated(dst, bc(m[0:SMP, 0:SMP].unsqueeze(1), SMP, 2, SMP),
                                              bank[4 + r][0:SMP, 0:2 * SMP].rearrange("p (q i) -> p q i", q=2))
                c.done(i, "ag_ok")

            for l in range(LEVELS):
                level(l)
                gather(l)
            gather(LEVELS)
            wait(v, "ebl_ok", 2)
            c.done(v.tensor_tensor(gQ, gqk[:, 0:2, :], gE, ALU.mult), "g_abs")
            for j in range(2):
                bp = bT[:, j, 0:SEQ].rearrange("p (c i) -> p c i", c=2)
                bs = bT[:, j, SEQ:T].rearrange("p (b i) -> p b i", b=NB)
                v.tensor_tensor(gE[:, j, 0:SEQ].rearrange("p (c i) -> p c i", c=2), bc(bp[:, :, P - 1:P], P, 2, P), bp, ALU.subtract)
                i = v.tensor_tensor(gE[:, j, SEQ:T].rearrange("p (b i) -> p b i", b=NB), bc(bs[:, :, NS - 1:NS], P, NB, NS), bs, ALU.subtract)
            c.done(i, "g_abs")
            wait(v, "ebl_ok", 3)
            c.done(v.tensor_tensor(gK, gqk[:, 2:4, :], gE, ALU.mult), "g_lvl")
            sl2 = slp[:].rearrange("p j d -> p (j d)")
            wait(v, "p_gch", 1)
            c.done(v.tensor_copy(sl2, bank[4][:, 0:256]), "gch_ok")
            wait(v, "p_gch", 2)
            v.tensor_copy(ot[:, 0, QK:D], bank[3][:])
            c.done(v.tensor_copy(ot[:, 1, QK:D], bank[7][:]), "v_step")
            for r in range(2):
                d = ot[:, 1, QK:D].rearrange("p (j r d) -> p j r d", j=2, r=2)[:, :, r, :]
                i = v.tensor_tensor(d, d, bank[5 + r][:, 0:256].rearrange("p (j d) -> p j d", j=2), ALU.add)
            c.done(i, "gch_ok")
            wait(v, "p_gch", 3)
            for j in range(2):
                i = v.scalar_tensor_tensor(out=slp[:, j, :], in0=slp[:, j, :], scalar=ebl[:, j, 1:2], in1=bank[4][:, j * P:(j + 1) * P],
                                           op0=ALU.mult, op1=ALU.add)
            c.done(i, "gch_ok")
            wait(v, "p_gs", 2)
            og = ot[0:SMP, 2, QK:D]
            c.done(v.tensor_copy(og, bank[2][0:SMP, :]), "v_step")
            c.done(v.tensor_tensor(og, og, bank[4][0:SMP, :], ALU.add), "v_step")
            for t in range(NTT):
                n = TN[t]
                c.done(v.tensor_tensor(osq[0:n], ot[0:n, t, :], ot[0:n, t, :], ALU.mult), "v_step")
                c.done(v.tensor_reduce(ss8[0:n, 8 * t:8 * t + 8], hd(osq[0:n]), AX_X, ALU.add), "osq_ok")
            c.done(v.tensor_scalar(ss8[:], ss8[:], 1.0 / P, EPS, ALU.mult, ALU.add), "osq_ok")
            wait(v, "rs8_ok", 2)
            for t in range(NTT):
                n = TN[t]
                c.done(v.tensor_tensor(hd(ot[0:n, t, :]), hd(ot[0:n, t, :]), bc(r8[0:n, t, :].unsqueeze(2), n, 8, P), ALU.mult), "o_ok")
            for t in range(NTT):
                n = TN[t]
                for j in range(2):
                    wait(v, "p_oT", 2 * t + j + 1)
                    z = zg[:, 4 * j:4 * j + 4, TO[t]:TO[t] + n]
                    c.done(v.scalar_tensor_tensor(out=z, in0=bank[j][:, 0:4 * n].rearrange("p (h i) -> p h i", h=H), scalar=vecT[:, 58 + j:59 + j],
                                                  in1=z, op0=ALU.mult, op1=ALU.mult), "oT_ok")

            for h in range(6):
                wait(v, "p_up_s", h + 1)
                wait(v, "dec_ok", h + 1)
                for k in range(2):
                    st = sgs[:, 4 * k:4 * k + 4, h, :] if h < 4 else sls[:, h - 4, 4 * k:4 * k + 4, :]
                    i = v.tensor_tensor(st, st, bank[(4, 6)[h % 2] + k][:].rearrange("p (b d) -> p b d", b=4), ALU.add)
                c.done(i, "st_ok")
            wait(v, "x_again", 32)
            for t in range(NTT):
                for j in range(2):
                    at = 2 * t + j
                    wait(v, "p_x2", at + 1)
                    d = x2[0:TN[t], t, 512 * j:512 * (j + 1)]
                    c.done(v.tensor_tensor(d, d, bank[4 + at % 4][0:TN[t], :], ALU.add), "x2_ok")
            wait(v, "ss2_ok", 3)
            c.done(v.tensor_scalar(rst[:], ss[:], 1.0 / D, EPS, ALU.mult, ALU.add), "rs2_in")
            wait(v, "rst_ok", 2)
            wait(v, "ld_ffn", 16)
            for t in range(NTT):
                n = TN[t]
                c.done(v.scalar_tensor_tensor(out=ot[0:n, t, :], in0=x2[0:n, t, :], scalar=rst[0:n, t:t + 1], in1=wbc[0:n], op0=ALU.mult, op1=ALU.mult), "xn_ok")
            v.memset(lg[:], 0.0)
            v.memset(r32[:], 1.0)
            c.done(v.memset(selm[:], 0.0), "v_step")
            c.done(v.memset(r32[:, 0:3 * E_N:E_N], 0.0), "v_step")
            wait(v, "p_lg", 1)
            for t in range(NTT):
                n = TN[t]
                c.done(v.tensor_tensor(lg[0:n, E_N * t:E_N * (t + 1)], bank[4][0:n, E_N * t:E_N * (t + 1)], brt[0:n], ALU.add), "lg_ok")
            for t in range(NTT):
                c.done(v.max(m8[:, t, :], lg[:, E_N * t:E_N * (t + 1)]), "v_step")
            e3 = lambda ap: ap[:].rearrange("p (t e) -> p t e", t=3)
            c3 = lambda ap: bc(ap, P, 3, E_N)
            m1, m4 = m8[:, :, 0:1], m8[:, :, 3:4]
            c.done(v.tensor_tensor(e3(gates), e3(lg), c3(m1), ALU.subtract), "lg_ok")
            c.done(v.tensor_tensor(e3(gts), e3(lg), c3(m4), ALU.is_gt), "v_step")
            c.done(v.tensor_tensor(e3(eqs), e3(lg), c3(m4), ALU.is_equal), "v_step")
            c.done(v.tensor_reduce(ndd[:], e3(gts), AX_X, ALU.add), "v_step")
            c.done(v.tensor_scalar(ndd[:], ndd[:], -1.0, float(TOPK), ALU.mult, ALU.add), "v_step")
            c.done(v.tensor_tensor_scan(pre[:], r32[:], eqs[:], 0.0, ALU.mult, ALU.add), "v_step")
            c.done(v.tensor_tensor(e3(pre), e3(pre), c3(ndd[:].unsqueeze(2)), ALU.is_le), "v_step")
            c.done(v.tensor_tensor(eqs[:], eqs[:], pre[:], ALU.mult), "v_step")
            c.done(v.tensor_tensor(selm[:], gts[:], eqs[:], ALU.add), "route_ok")
            wait(v, "gexp_ok", 1)
            c.done(v.tensor_tensor(gates[:], gates[:], selm[:], ALU.mult), "v_step")
            c.done(v.tensor_reduce(den[:], e3(gates), AX_X, ALU.add), "v_step")
            c.done(v.reciprocal(den[:], den[:]), "v_step")
            c.done(v.tensor_tensor(e3(gates), e3(gates), c3(den[:].unsqueeze(2)), ALU.mult), "v_step")
            c.done(v.memset(posm[:], 0.0), "v_step")
            wait(v, "p_pos", 1)
            for t in range(NTT):
                n = TN[t]
                cols = slice(E_N * t, E_N * (t + 1))
                c.done(v.scalar_tensor_tensor(out=posm[0:n, cols], in0=bank[5][0:n, cols], scalar=1.0, in1=selm[0:n, cols], op0=ALU.add, op1=ALU.mult), "v_step")
            c.done(v.tensor_scalar(posm[:], posm[:], -1.0, None, ALU.add), "v_step")
            c.done(v.tensor_reduce(cnt[0:1, 0:1], bank[6][0:1, 0:E_N], AX_X, ALU.max), "v_step")
            for k in range(4):
                c.done(v.tensor_scalar(cgt[0:1, k:k + 1], cnt[0:1, 0:1], float(CAP * (k + 1)), None, ALU.is_gt), "v_step")
            c.done(v.tensor_reduce(cnt[0:1, 1:2], cgt[0:1, :], AX_X, ALU.add), "v_step")
            c.done(v.tensor_scalar(cnt[0:1, 1:2], cnt[0:1, 1:2], 1.0, None, ALU.add), "v_step")
            c.done(v.tensor_copy(rnd[:], cnt[0:1, 1:2]), "rnd_ok")
            v.memset(hT[:], 0.0).then_inc(sems["sc_ok"], 1)
            v.memset(yT, 0.0).then_inc(sems["yb_ok"], 1)
            v.memset(S, 0.0).then_inc(sems["S_ok"], 1)
            v.memset(yr, 0.0).then_inc(sems["yr_ok"], 1)
            c.done(v.memset(gu, 0.0), "p_S")
            rounds = v.value_load(rnd[0:1, 0:1], min_val=1, max_val=5)
            bflat = biasT[:].rearrange("p a b -> p (a b)")

            def swiglu(i, q, hf):
                at = 2 * q + hf + 1
                v.wait_ge(sems["p_up"], i * 4 + at)
                v.tensor_tensor(gu, bank[hf][:].rearrange("p (g j c) -> p g j c", g=2, j=4),
                                bc(bup[:, q, :, hf, :].unsqueeze(3), P, 2, 4, CAP), ALU.add).then_inc(sems["gu_rd"], 1)
                v.wait_ge(sems["gu_rd"], i * 4 + at)
                v.tensor_scalar(gu[:, 0], gu[:, 0], 7.0, None, ALU.min).then_inc(sems["gu_ok"], 1)
                v.tensor_scalar(gu[:, 1], gu[:, 1], 7.0, -7.0, ALU.min, ALU.max).then_inc(sems["gu_cl"], 1)
                v.wait_ge(sems["gu_ok"], i * 4 + at)
                v.wait_ge(sems["gu_cl"], i * 4 + at)
                v.scalar_tensor_tensor(out=ta, in0=gu[:, 1], scalar=1.0, in1=gu[:, 0], op0=ALU.add, op1=ALU.mult).then_inc(sems["ta_ok"], 1)
                v.wait_ge(sems["ta_ok"], i * 4 + at)
                v.wait_ge(sems["sig_ok"], i * 4 + at)
                v.tensor_tensor(aT[:, 4 * hf:4 * hf + 4, :], ta, sg, ALU.mult).then_inc(sems["act_ok"], 1)
                v.wait_ge(sems["act_ok"], i * 4 + at)

            def gain(w):
                for d in range(KT):
                    v.wait_ge(sems["p_sc"], w * 8 + (d + 1))
                    v.tensor_tensor(hT[:, d, :], hT[:, d, :], bank[(7, 3)[d % 2]][:, 0:T], ALU.add).then_inc(sems["sc_ok"], 1)

            def out_rows(i, q):
                v.wait_ge(sems["p_yd"], i * 2 + (q + 1))
                v.tensor_tensor(yT[:, :, CAP * q:CAP * (q + 1)], bank[2][:].rearrange("p (n c) -> p n c", n=8),
                                bc(bdn[:, q, :].unsqueeze(2), P, 8, CAP), ALU.add).then_inc(sems["yb_ok"], 1)
                v.wait_ge(sems["yb_ok"], i * 2 + (q + 2))

            pos3 = posm[:].rearrange("p (t e) -> p t e", t=3)
            gat3 = gates[:].rearrange("p (t e) -> p t e", t=3)
            two = lambda ap: ap.rearrange("p (q c) -> p q c", q=2)
            wait(v, "tri_ok", 2)
            with v.Fori(0, rounds) as r:
                with v.Fori(0, PAIRS) as p:
                    i = r * PAIRS + p
                    v.tensor_copy(bup[:].rearrange("p q g h j -> p (q g h j)"), bflat[:, bass.ds(p * 32, 32)]).then_inc(sems["bp_ok"], 1)
                    v.tensor_copy(bdn[:].rearrange("p q n -> p (q n)"), bflat[:, bass.ds(p * 16 + 512, 16)]).then_inc(sems["bp_ok"], 1)
                    v.tensor_copy(pp[:], pos3[:, :, bass.ds(p * 2, 2)]).then_inc(sems["pp_ok"], 1)
                    v.tensor_copy(gp2[:], gat3[:, :, bass.ds(p * 2, 2)]).then_inc(sems["pp_ok"], 1)
                    v.wait_ge(sems["bp_ok"], i * 2 + 2)
                    v.wait_ge(sems["pp_ok"], i * 2 + 2)
                    v.wait_ge(sems["p_S"], i + 1)
                    for t in range(NTT):
                        n = TN[t]
                        last = v.tensor_tensor(two(G[0:n, t, :]), bc(slots_io[0:n].unsqueeze(1), n, 2, CAP), bc(pp[0:n, t, :].unsqueeze(2), n, 2, CAP), ALU.is_equal)
                    last.then_inc(sems["G_ok"], 1)
                    v.wait_ge(sems["G_ok"], i * 2 + 1)
                    for t in range(NTT):
                        n = TN[t]
                        last = v.tensor_tensor(two(GG[0:n, t, :]), two(G[0:n, t, :]), bc(gp2[0:n, t, :].unsqueeze(2), n, 2, CAP), ALU.mult)
                    last.then_inc(sems["G_ok"], 1)
                    swiglu(i, 0, 0)
                    gain(i)
                    swiglu(i, 0, 1)
                    out_rows(i, 0)
                    swiglu(i, 1, 0)
                    swiglu(i, 1, 1)
                    out_rows(i, 1)
                v.tensor_scalar(posm[:], posm[:], float(CAP), None, ALU.subtract).then_inc(sems["pos_next"], 1)
                v.wait_ge(sems["pos_next"], r + 1)
            total = rounds * PAIRS
            gain(total)
            for t in range(NTT):
                n = TN[t]
                for j in range(2):
                    at = 2 * t + j
                    wait(v, "p_fin", at + 1)
                    d = x2[0:n, t, 512 * j:512 * (j + 1)]
                    c.done(v.tensor_tensor(d, d, bank[at % 4][0:n, :], ALU.add), "fin_x")
            wait(v, "ss3_ok", 3)
            c.done(v.tensor_scalar(rst[:], ss[:], 1.0 / D, EPS, ALU.mult, ALU.add), "rs3_in")
            wait(v, "rs3_ok", 1)
            wait(v, "ld_fin", 16)
            for t in range(NTT):
                n = TN[t]
                c.tick(v.scalar_tensor_tensor(out=x2[0:n, t, :], in0=x2[0:n, t, :], scalar=rst[0:n, t:t + 1], in1=wbc[0:n], op0=ALU.mult, op1=ALU.mult), "y_fin")

        @block.scalar
        def _(act):
            c = Count(act)
            wait(act, "ld_x", 32)
            wait(act, "v_step", 2)
            for t in range(NTT):
                n = TN[t]
                c.done(act.activation(ot[0:n, t, :], xt[0:n, t, :], ACT.Square, accum_out=ss[0:n, t:t + 1]), "ss_ok")

            def land(at, n_mm=1):
                wait(act, "p_proj", at + 1)
                return bank[at % 4]

            b = land(0)
            c.done(act.copy(sm[:], b[0:80, 0:T]), "proj_ok")
            wait(act, "gate_x", 1)
            c.done(act.activation(gtmp[0:4, 1, :], gtmp[0:4, 1, :], ACT.Exp, scale=-1.0), "gate_e")
            c.done(act.activation(gtmp[32:36, 0, :], sm[32:36, :], ACT.Exp, scale=-1.0), "gate_e")
            c.done(act.activation(gate2[:, 2:3], gate2[:, 0:1], ACT.Exp), "gate_e")
            c.done(act.activation(gtmp[0:4, 1, :], gtmp[0:4, 1, :], ACT.Ln, bias=1.0), "gate_l")
            for u in range(3):
                wait(act, "conv_ok", u)
                wait(act, "cs_ok", u)
                for n in range(4):
                    at = 1 + 4 * u + n
                    b = land(at)
                    act.copy(raw[:, n, HEAD:HEAD + SEQ], b[:, 0:SEQ])
                    c.tick(act.copy(samples(raw[:, n, HEAD + SEQ:RAW])[:, :, HEAD:], samples(b[:, SEQ:T])), "proj_ok")
                wait(act, "conv_lin", u + 1)
                wait(act, "cs_ok", u + 1)
                c.tick(act.activation(raw[:, :, 0:CW], ce[:, :, 0:CW], ACT.Sigmoid), "conv_sig")
            for n in range(4):
                at = 13 + n
                b = land(at)
                c.tick(act.mul(gqk[:, n, :], b[:, 0:T], 0.125 if n < 2 else 1.0), "proj_ok")
            wait(act, "gk_x", 1)
            c.done(act.activation(gQ, gQ, ACT.Exp, scale=-1.0), "gk_e")
            c.done(act.activation(gQ, gQ, ACT.Ln, bias=1.0), "gk_l")
            wait(act, "p_convt", 9)
            for n in range(4):
                at = 17 + n
                b = land(at)
                c.tick(act.copy(convT[:, n, :], b[:, 0:T]), "proj_ok")
            for u in range(2):
                wait(act, "conv_ok", 3)
                wait(act, "zg_ok", u)
                for n in range(4):
                    at = 21 + 4 * u + n
                    b = land(at)
                    act.copy(zg[:, 4 * u + n, :], b[:, 0:T])
                    c.tick(act.activation(ce_z[:, n, :], b[:, 0:T], ACT.Sigmoid), "proj_ok")

            wait(act, "gt_ok", 3)
            c.done(act.activation(eg[:], gt[:, :, 0:4], ACT.Exp), "gt_exp")
            c.done(act.activation(ekd[:], gt[:, :, 64:68], ACT.Exp), "gt_exp")
            c.done(act.copy(ebl[:, :, 0:2], bT[:, :, P - 1:SEQ:P]), "gt_exp")
            for t in range(NTT):
                n = TN[t]
                for j in range(3):
                    at = 3 * t + j
                    wait(act, "p_qkT", at + 1)
                    dst = (KQ[:, 0], KQ[:, 1], kbT)[j][:, :, TO[t]:TO[t] + n]
                    c.tick(act.copy(dst, bank[4 + at % 4][:, 0:H * n].rearrange("p (h i) -> p h i", h=H)), "qkT_ok")
            for t in range(NTT):
                wait(act, "di_ok", t + 1)
                c.tick(act.activation(Dtt[t], Dtt[t], ACT.Exp), "dexp_ok")
            wait(act, "di_ok", 4)
            c.tick(act.activation(egl[:], egl[:], ACT.Exp), "dexp_ok")
            wait(act, "out_done", 32)
            for k, (l, t) in enumerate(INV):
                n = TN[t]
                wait(act, "p_y", k + 1)
                c.tick(act.copy(Yt[t], bank[(0, 3, 7)[t]][0:n, 0:H * n].rearrange("p (h i) -> p h i", h=H)), "y_ok")
            wait(act, "p_smp", 1)
            c.done(act.copy(skT[:].rearrange("p a b -> p (a b)"), bank[7][:, 0:256]), "smk_ok")
            for l in range(LEVELS):
                n = T if l < 2 else SEQ
                wait(act, "g_abs", l + 1)
                c.tick(act.activation(gE[:, :, 0:n], gE[:, :, 0:n], ACT.Exp), "g_exp")
            wait(act, "g_lvl", LEVELS)
            c.tick(act.activation(gE, bT, ACT.Exp), "ebl_ok")
            c.done(act.copy(ebl[:, :, 2:10], bT[:, :, SEQ + NS - 1:T:NS]), "gt_exp")
            c.done(act.activation(ebl[:], ebl[:], ACT.Exp), "ebl_ok")
            wait(act, "g_abs", LEVELS + 2)
            c.tick(act.activation(gE, gE, ACT.Exp), "ebl_ok")
            wait(act, "p_gkd", 1)
            for t in range(NTT):
                n = TN[t]
                c.tick(act.copy(kdg[0:n, t, :], bank[t][0:n, 0:256]), "kdg_ok")
            wait(act, "p_gs", 1)
            for r in range(2):
                c.tick(act.copy(skT[:, r, 0:64], bank[r][:, 0:64]), "gsT_ok")
            for n in range(8):
                at = 29 + n
                b = land(at)
                c.tick(act.copy(hT[:, n, :], b[:, 0:T]), "proj_ok")

            for t in range(NTT):
                n = TN[t]
                wait(act, "x2_ok", 2 * t + 2)
                c.tick(act.activation(zf[0:n, 0:D], x2[0:n, t, :], ACT.Square, accum_out=ss[0:n, t:t + 1]), "ss2_ok")
                wait(act, "ss2_ok", t + 1)
            for k in range(KT):
                wait(act, "p_xnT", k + 1)
                c.tick(act.copy(hT[:, k, :], bank[k % 4][:, 0:T]), "xnT_ok")
            wait(act, "lg_ok", 4)
            c.tick(act.activation(gates[:], gates[:], ACT.Exp), "gexp_ok")
            wait(act, "rnd_ok", 1)
            rounds = act.value_load(rnd[0:1, 0:1], min_val=1, max_val=5)

            def sigmoid(i, at):
                act.wait_ge(sems["gu_ok"], i * 4 + at)
                act.activation(sg, gu[:, 0], ACT.Sigmoid, scale=1.702).then_inc(sems["sig_ok"], 1)

            def y_rows(w):
                for j in range(2):
                    act.wait_ge(sems["p_ty"], w * 2 + (j + 1))
                    act.copy(yr[:, 512 * j:512 * (j + 1)], bank[5 + j][:]).then_inc(sems["yr_ok"], 1)

            with act.Fori(0, rounds * PAIRS) as i:
                for j in range(2):
                    act.wait_ge(sems["p_gat"], i * 2 + (j + 1))
                    act.copy(xeT[:, 4 * j:4 * j + 4, :].rearrange("p a b -> p (a b)"), bank[3 + j][:]).then_inc(sems["xe_ok"], 1)
                sigmoid(i, 1)
                y_rows(i)
                act.wait_ge(sems["p_S"], i + 2)
                act.copy(S, bank[4][:, 0:T]).then_inc(sems["S_ok"], 1)
                sigmoid(i, 2)
                sigmoid(i, 3)
                sigmoid(i, 4)
            y_rows(rounds * PAIRS)
            for t in range(NTT):
                n = TN[t]
                wait(act, "fin_x", 2 * t + 2)
                c.tick(act.activation(zf[0:n, 0:D], x2[0:n, t, :], ACT.Square, accum_out=ss[0:n, t:t + 1]), "ss3_ok")
                wait(act, "ss3_ok", t + 1)

_INS = ["x_prompt", "x_sample", "state_gdn_conv", "state_gdn", "state_gla", "rms_mix_w", "w_in", "conv_w",
        "gdn_a_log", "gdn_dt_bias", "gdn_norm_w", "gla_gk_w", "gla_gk_b", "gla_norm_w", "w_out", "rms_ffn_w",
        "w_router", "b_router", "w_up", "b_up", "w_down", "b_down", "rms_final_w"]
_OUTS = [(1, 256, 1024), (8, 4, 1024), (1, 1, 3, 1536), (1, 1, 4, 128, 128), (1, 1, 4, 64, 128),
         (1, 8, 3, 1536), (1, 8, 4, 128, 128), (1, 8, 4, 64, 128)]


def kernel(**inputs):
    import numpy as _np
    import concourse.bacc as _bacc
    from concourse import mybir as _mybir
    from concourse.bass_utils import run_bass_kernel_spmd as _run

    nc = _bacc.Bacc("TRN2", target_bir_lowering=False, num_devices=1)
    arrays, args = {}, {}
    for name in _INS:
        x = _np.ascontiguousarray(inputs[name])
        arrays[f"in_{name}"] = x
        args[name] = nc.dram_tensor(f"in_{name}", x.shape, _mybir.dt.from_np(x.dtype), kind="ExternalInput").ap()
    outs = [nc.dram_tensor(f"out_{i}", s, _mybir.dt.float32, kind="ExternalOutput").ap() for i, s in enumerate(_OUTS)]
    program(nc, args, outs)
    r = _run(nc, [arrays], core_ids=[0])
    return tuple(r.results[0][f"out_{i}"] for i in range(len(_OUTS)))
```

```python
from contextlib import ExitStack

import concourse.bass as bass
from concourse import mybir

P = 128
F32 = mybir.dt.float32
I32 = mybir.dt.int32
ALU = mybir.AluOpType
ACT = mybir.ActivationFunctionType
AX_X = mybir.AxisListType.X

D = 1024
KT = D // P
SEQ, NB, NS = 256, 8, 4
SMP = NB * NS
T = SEQ + SMP
NTT = 3
TN = [P, P, SMP]
TO = [0, P, 2 * P]
H = 4
QK = 512
CH = 3 * QK
HEAD = 3
RAW = HEAD + SEQ + NB * (HEAD + NS)
CW = RAW - HEAD
LEVELS = 7
E_N, TOPK, FF = 32, 4, 1024
CAP = 64
PAIRS = E_N // 2
EPS = 1e-6
NEG = -3.0e38
C_Z, C_A, C_B = 1536, 2048, 2052
C_GQ, C_GV, C_GG, C_LR = 2056, 2568, 3080, 3592


def program(nc, a, o):
    ctx = ExitStack()
    with ctx:
        def sb(name, shape, dt=F32):
            return ctx.enter_context(nc.sbuf_tensor(name, shape, dt))

        def sem(name):
            return ctx.enter_context(nc.semaphore(name))

        bank = [ctx.enter_context(nc.psum_tensor(f"bank{i}", [P, 512], F32)) for i in range(8)]

        def cut(base, at, *shape):
            n = 1
            for s in shape:
                n *= s
            v = base[:, at:at + n]
            if len(shape) == 2:
                v = v.rearrange("p (a b) -> p a b", a=shape[0])
            if len(shape) == 3:
                v = v.rearrange("p (a b c) -> p a b c", a=shape[0], b=shape[1])
            return v

        UNIT = 4096
        ring = sb("ring", [P, 6 * UNIT])
        slot = [ring[:, i * UNIT:(i + 1) * UNIT] for i in range(6)]
        sgs = cut(ring, 0, NB, H, P)
        S3 = 3 * UNIT
        KQ = cut(ring, S3, 2, H, T)
        kbT = cut(ring, S3 + 2304, H, T)
        nM = cut(ring, S3 + 3456, 2 * H, P)
        nMs = cut(ring, S3 + 4480, H, SMP)
        AT = cut(ring, S3 + 4608, 2 * H, P)
        ATs = cut(ring, S3 + 5632, H, SMP)
        U = cut(ring, S3 + 5760, 2 * H, P)
        Us = cut(ring, S3 + 6784, H, SMP)
        Ti = cut(ring, S3 + 6912, 2 * H, P)
        Tis = cut(ring, S3 + 7936, H, SMP)
        Y = cut(ring, S3 + 8064, 2 * H, P)
        Ys = cut(ring, S3 + 9088, H, SMP)
        Dt = cut(ring, S3 + 9216, 2 * H, P)
        Dts = cut(ring, S3 + 10240, H, SMP)
        gE = cut(ring, S3 + 10368, 2, T)
        gQ = cut(ring, S3 + 10944, 2, T)
        gK = cut(ring, S3 + 11520, 2, T)
        crow = ring[:, S3 + 8064:S3 + 8064 + CH]
        gdiag = cut(ring, S3 + 6912, H, T)
        kdm = cut(ring, S3 + 9216, NB, P)

        osq = ring[:, S3:S3 + D]
        skT = sb("skT", [P, 2, P])
        xb = sb("xb", [P, 3 * D])
        xt = cut(xb, 0, 3, D)
        gqk = cut(xb, 0, 4, T)
        kdg = cut(xb, 0, 3, 256)
        vg = cut(xb, 1152, 3, 512)
        ob = sb("ob", [P, 3 * D])
        raws = [cut(ob, 0, 4, RAW), cut(ring, S3, 4, RAW)]
        ces = [cut(ob, 4 * RAW, 4, RAW), cut(ring, S3 + 4 * RAW, 4, RAW)]
        ce_z = cut(ob, 1260, 4, T)
        ot = cut(ob, 0, 3, D)
        xeT = cut(xb, 0, KT, P)
        yr = xb[:, D:2 * D]
        gu = cut(xb, 2 * D, 2, 512)
        hT = sb("hT", [P, KT, T])
        hf_ = hT[:].rearrange("p a b -> p (a b)")
        b_gu = hf_[:, 0:512]
        b_dn = hf_[:, 512:1024]
        sel_gu = cut(hf_, 1024, 4, CAP)
        sel_dn = cut(hf_, 1280, 2, CAP)
        zg = sb("zg", [P, KT, T])
        zf = zg[:].rearrange("p a b -> p (a b)")
        aT = cut(zf, 0, 4, P)
        sg = cut(zf, 512, 512)
        G = cut(zf, 1280, 3, P)
        GG = cut(zf, 1664, 3, P)
        convf = sb("convT", [P, 4 * T])
        convT = cut(convf, 0, 4, T)
        AG = cut(convf, 0, 2 * H, P)
        AGs = cut(convf, 2 * H * P, H, SMP)
        wbc = convf[:, 0:D]
        qf = sb("qkv", [P, 3 * CH])
        qkv = cut(qf, 0, 3, CH)
        x2 = cut(qf, 0, 3, D)
        vn = qkv[:, :, 0:QK]
        ident = sb("ident", [P, P])
        ones = sb("ones", [P, P])
        upi = sb("upi", [P, P])
        upis = sb("upis", [SMP, SMP])
        mu = sb("mu", [P, LEVELS, P], I32)
        mlf = sb("ml", [P, LEVELS * P])
        ml = cut(mlf[:].bitcast(I32), 0, LEVELS, P)
        mone = sb("mone", [P, P], I32)
        seqm = sb("seqm", [SMP, NB])
        resets = sb("resets", [P, T])
        sgp = sb("sgp", [P, H, P])
        sls = sb("sls", [P, 2, NB, P])
        slp = sb("slp", [P, 2, P])
        bTf = sb("bT", [P, 2 * T])
        bT = cut(bTf, 0, 2, T)
        S = bTf[:, 0:T]
        lg = mlf[:, 0:96]
        m8 = sb("m8", [P, 3, 8])
        gts = mlf[:, 96:192]
        eqs = mlf[:, 192:288]
        pre = mlf[:, 288:384]
        selm = mlf[:, 384:480]
        gates = mlf[:, 480:576]
        posm = mlf[:, 576:672]
        r32 = mlf[:, 672:768]
        ndd = sb("ndd", [P, 3])
        den = sb("den", [P, 3])
        tri = sb("tri", [P, P])
        cnt = sb("cnt", [1, 2])
        cgt = sb("cgt", [1, 4])
        rnd = sb("rnd", [1, 1], I32)
        slots_io = sb("slots_io", [P, CAP])
        pp = sb("pp", [P, 3, 2])
        gp2 = sb("gp2", [P, 3, 2])
        wsmf = sb("wsm", [P, KT * 80])
        wsm = cut(wsmf, 0, KT, 80)
        wr = cut(wsmf, 0, KT, E_N)
        brt = wsmf[:, KT * E_N:KT * E_N + E_N]
        sm = sb("sm", [80, T])
        gb = sb("gb", [68, T])
        gtmp = sb("gtmp", [36, 2, T])
        kb = sb("kb", [P, QK])
        gt = sb("gt", [P, 3, 68])
        eg = sb("eg", [P, 3, H])
        ekd = sb("ekd", [P, 3, H])
        nbeg = sb("nbeg", [P, 3, H])
        egl = sb("egl", [P, H, 10])
        gate2 = sb("gate2", [4, 3])
        vrow = sb("vrow", [60, P])
        vecT = sb("vecT", [P, 60])
        gkw = sb("gkw", [80, 256])
        cT = sb("cT", [P, 12, 24])
        cs = sb("cs", [P, 12, 27])
        ss = sb("ss", [P, 3])
        rst = sb("rst", [P, 3])
        ss8 = sb("ss8", [P, 24])
        rs8 = sb("rs8", [P, 24])
        mhalf = sb("mhalf", [P, 24])
        ebl = sb("ebl", [P, 2, 10])

        names = """ld_x ld_vec ld_gate ld_cst ld_sm ld_bias ld_st ld_router w_in1 w_in2
            ident_ok masks_ok v_step ss_ok rst_in rst_ok h_ok p_vec vec_ok p_hT
            hT_ok p_cT cT_ok p_at p_proj proj_ok conv_lin conv_sig conv_ok
            cs_ok p_convt convt_ok p_gk gk_x gk_e gk_l bT_ok gate_x gate_e
            gate_l gb_ok p_gt gt_ok gt_exp p_gi di_ok dexp_ok d_ok ss8_ok
            rs8_ok qkn_ok p_qkT qkT_ok p_MA MA_ok p_y y_ok p_inv inv_ok
            p_tm p_ch ch_ok vd_ok p_smp g_abs g_exp g_lvl p_glvl p_low ag_ok
            ebl_ok zg_ok smk_ok smr_ok p_gkd kdg_ok p_gch gch_ok p_gs gsT_ok
            osq_ok o_ok p_oT oT_ok w_out w_out2 x_again p_x2 x2_ok p_xnT
            xnT_ok p_lg route_ok ss2_ok rs2_in xn_ok p_pos kdm_ok dec_ok p_up_s
            st_ok p_csr csr_ok out_done ld_ffn ld_fin lg_ok tri_ok rnd_ok G_ok
            p_gat p_up p_yd p_ty p_sc p_S w_used gu_rd gu_ok act_ok
            yb_ok sc_ok xe_ok sel_ok S_ok sig_ok ld_w0 ld_w1 ld_w2 ld_w3
            ld_w4 ld_w5 st_out st_out2 pp_ok pos_next acc_ok gexp_ok gu_cl ta_ok
            aT_ok ss3_ok rs3_in rs3_ok y_fin""".split()
        WSLOT = [3, 4, 2, 1, 5, 0]
        INV = [(l, t) for l in range(1, LEVELS) for t in ((0, 1, 2) if l == 1 else (0, 1))]
        FILL = [2 if k < 3 else 1 for k in range(len(INV))]
        HALVES = [sum(FILL[:k]) for k in range(len(INV) + 1)]
        gate_tiles = [range(HALVES[k] // 2, HALVES[k + 1] // 2) for k in range(len(INV))]
        INV_BANKS = ((2, 3), (4, 5), (6, 6))
        inv_at = {(0, t): t + 1 for t in range(3)} | {x: 4 + i for i, x in enumerate(INV)}
        NMt = [nM[:, 0:H], nM[:, H:2 * H], nMs[0:SMP]]
        Att = [AT[:, 0:H], AT[:, H:2 * H], ATs[0:SMP]]
        Ut = [U[:, 0:H], U[:, H:2 * H], Us[0:SMP]]
        Tt = [Ti[:, 0:H], Ti[:, H:2 * H], Tis[0:SMP]]
        Yt = [Y[:, 0:H], Y[:, H:2 * H], Ys[0:SMP]]
        Dtt = [Dt[:, 0:H], Dt[:, H:2 * H], Dts[0:SMP]]
        AGt = [AG[:, 0:H], AG[:, H:2 * H], AGs[0:SMP]]
        sems = {n: sem(n) for n in names}
        block = ctx.enter_context(nc.Block())

        class Count:

            def __init__(self, eng):
                self.eng, self.n = eng, {}

            def tick(self, ins, name):
                ins.then_inc(sems[name], 1)
                self.n[name] = self.n.get(name, 0) + 1

            def done(self, ins, name):
                self.tick(ins, name)
                self.eng.wait_ge(sems[name], self.n[name])

        def wait(eng, name, value):
            if value > 0:
                eng.wait_ge(sems[name], value)

        def bc(ap, *shape):
            return ap.broadcast_to(list(shape))

        def samples(ap):
            return ap.rearrange("p (b j) -> p b j", b=NB)

        def hx(ap):
            return ap.unsqueeze(2)

        @block.sync
        def _(sp):
            sp.dma_start(xt[:, 0:2, :], a["x_prompt"].rearrange("a (t p) d -> p (a t) d", p=P)).then_inc(sems["ld_x"], 16)
            sp.dma_start(xt[0:SMP, 2, :], a["x_sample"].rearrange("b s d -> (b s) d")).then_inc(sems["ld_x"], 16)
            rows = [(a["rms_mix_w"].rearrange("l (k p) -> (l k) p", p=P), 0, 8),
                    (a["conv_w"].rearrange("l i (c p) -> (l i c) p", p=P), 8, 48),
                    (a["gla_gk_b"].rearrange("l (j p) -> (l j) p", p=P), 56, 2),
                    (a["gdn_norm_w"], 58, 1), (a["gla_norm_w"], 59, 1)]
            for src, at, n in rows:
                sp.dma_start(vrow[at:at + n, :], src).then_inc(sems["ld_vec"], 16)
            w_in = a["w_in"].rearrange("l (k p) n -> p (l k) n", p=P)
            sp.dma_start(wsm[:, :, 0:4], w_in[:, :, C_A:C_A + 4]).then_inc(sems["ld_sm"], 16)
            sp.dma_start(wsm[:, :, 32:36], w_in[:, :, C_B:C_B + 4]).then_inc(sems["ld_sm"], 16)
            sp.dma_start(wsm[:, :, 64:80], w_in[:, :, C_LR:C_LR + 16]).then_inc(sems["ld_sm"], 16)
            units = [0, 512, 1024, C_GQ, C_GV, C_Z, C_GG]
            for u in range(7):
                if u >= 2:
                    wait(sp, "p_proj", 1 + 4 * (u - 1))
                dst = slot[1 + u % 2].rearrange("p (k n) -> p k n", k=KT)
                sp.dma_start(dst, w_in[:, :, units[u]:units[u] + 512]).then_inc(sems[f"w_in{1 + u % 2}"], 16)
                if u == 1:
                    sp.dma_start(crow[0:24, :], a["state_gdn_conv"].rearrange("l b r c -> (l b r) c")).then_inc(sems["ld_cst"], 16)
                    sp.dma_start(gate2[:, 0:1], a["gdn_a_log"].rearrange("l h -> h l")).then_inc(sems["ld_gate"], 16)
                    sp.dma_start(gate2[:, 1:2], a["gdn_dt_bias"].rearrange("l h -> h l")).then_inc(sems["ld_gate"], 16)
                    sp.dma_start(gkw[64:80, :], a["gla_gk_w"][0]).then_inc(sems["ld_gate"], 16)
                    for h in range(H):
                        sp.dma_start(sgs[:, :, h, :], a["state_gdn"][0, :, h].rearrange("b k v -> k b v")).then_inc(sems["ld_st"], 16)
                    for h in range(H):
                        r = 64 * (h % 2)
                        sp.dma_start(sls[r:r + 64, h // 2, :, :], a["state_gla"][0, :, h].rearrange("b k v -> k b v")).then_inc(sems["ld_st"], 16)

            w_o = a["w_out"].rearrange("l (k p) n -> p (l k) n", p=P)
            for u in range(2):
                wait(sp, "p_proj", (25, 29)[u])
                dst = slot[2 - u].rearrange("p (k n) -> p k n", k=KT)
                sp.dma_start(dst, w_o[:, :, 512 * u:512 * (u + 1)]).then_inc(sems[("w_out", "w_out2")[u]], 16)

            for n in range(4):
                if n == 0:
                    wait(sp, "p_gs", 2)
                    sp.dma_start(wbc, a["rms_ffn_w"].partition_broadcast(P).rearrange("q l d -> q (l d)")).then_inc(sems["ld_ffn"], 16)
                    sp.dma_start(wr, a["w_router"].rearrange("l (k p) e -> p (l k) e", p=P)).then_inc(sems["ld_router"], 16)
                    sp.dma_start(brt, a["b_router"].partition_broadcast(P).rearrange("q l d -> q (l d)")).then_inc(sems["ld_router"], 16)
            wait(sp, "ch_ok", 6)
            sp.dma_start(x2[:, 0:2, :], a["x_prompt"].rearrange("a (t p) d -> p (a t) d", p=P)).then_inc(sems["x_again"], 16)
            sp.dma_start(x2[0:SMP, 2, :], a["x_sample"].rearrange("b s d -> (b s) d")).then_inc(sems["x_again"], 16)

            up = a["w_up"][0].rearrange("e (p k) n -> e p (k n)", p=P)
            dn = a["w_down"][0].rearrange("e (k p) n -> e p k n", p=P)

            def load_unit(e, u):
                dst = slot[WSLOT[u]]
                if u < 4:
                    src = up[e, :, UNIT * u:UNIT * (u + 1)]
                else:
                    dst = dst.rearrange("p (k n) -> p k n", k=4)
                    src = dn[e, :, 4 * (u - 4):4 * (u - 4) + 4, :]
                sp.dma_start(dst, src).then_inc(sems[f"ld_w{u}"], 16)

            wait(sp, "osq_ok", 4)
            wait(sp, "p_oT", 1)
            load_unit(0, 0)
            load_unit(0, 1)
            wait(sp, "p_proj", 33)
            load_unit(0, 2)
            wait(sp, "p_proj", 37)
            load_unit(0, 3)
            wait(sp, "p_up_s", 6)
            wait(sp, "st_ok", 6)
            load_unit(0, 4)
            wait(sp, "out_done", 16 * 6)
            load_unit(0, 5)
            wait(sp, "p_lg", 1)
            sp.dma_start(b_gu, a["b_up"].rearrange("l e (j n) -> (l e j) n", n=512)).then_inc(sems["ld_bias"], 16)
            sp.dma_start(b_dn[0:2 * E_N], a["b_down"].rearrange("l e (j n) -> (l e j) n", n=512)).then_inc(sems["ld_bias"], 16)
            wait(sp, "xn_ok", 3)
            sp.dma_start(wbc, a["rms_final_w"].partition_broadcast(P)).then_inc(sems["ld_fin"], 16)
            wait(sp, "rnd_ok", 1)
            rounds = sp.value_load(rnd[0:1, 0:1], min_val=1, max_val=5)
            with sp.Fori(1, rounds * E_N) as m:
                e = m % E_N
                for u, (name, value) in enumerate([("w_used", m * 4 - 3), ("w_used", m * 4 - 2), ("w_used", m * 4 - 1),
                                                   ("p_up", m), ("w_used", m * 4), ("p_yd", m)]):
                    sp.wait_ge(sems[name], value)
                    load_unit(e, u)
            for t in range(NTT):
                wait(sp, "y_fin", t + 1)
                dst = o[0][0, P * t:P * (t + 1), :] if t < 2 else o[1].rearrange("b s d -> (b s) d")
                sp.dma_start(dst, x2[0:TN[t], t, :]).then_inc(sems["st_out"], 16)
            wait(sp, "st_out", 48)

        @block.gpsimd
        def _(g):
            c = Count(g)
            g.memset(ident[:], 0.0)
            c.done(g.memset(ones[:], 1.0), "ident_ok")
            c.done(g.affine_select(out=ident[:], in_=ident[:], compare_op=ALU.not_equal, fill=1.0, base=0,
                                   pattern=[[-1, P]], channel_multiplier=1), "ident_ok")
            wait(g, "rst_in", 2)
            c.done(g.tensor_tensor(rst[:], rst[:], mhalf[:, 0:3], ALU.pow), "rst_ok")
            c.done(g.affine_select(out=upi[:], in_=ones[:], compare_op=ALU.is_ge, fill=0.0, base=0,
                                   pattern=[[1, P]], channel_multiplier=-1), "masks_ok")
            us = upis[:].rearrange("p (b s) -> p b s", b=NB)
            c.done(g.affine_select(out=us, in_=upi[0:SMP, 0:SMP].rearrange("p (b s) -> p b s", b=NB),
                                   compare_op=ALU.is_ge, fill=0.0, base=0, pattern=[[-NS, NB], [0, NS]],
                                   channel_multiplier=1), "masks_ok")
            c.done(g.affine_select(out=seqm[:], in_=ones[0:SMP, 0:NB], compare_op=ALU.is_ge, fill=0.0, base=0,
                                   pattern=[[-NS, NB]], channel_multiplier=1), "masks_ok")
            c.done(g.affine_select(out=seqm[:], in_=seqm[:], compare_op=ALU.is_ge, fill=0.0, base=NS - 1,
                                   pattern=[[NS, NB]], channel_multiplier=-1), "masks_ok")
            g.memset(mu[:], 0)
            c.done(g.memset(ml, 0), "masks_ok")
            for l in range(LEVELS):
                w, nb = 1 << l, P >> (l + 1)
                for m, lo, hi in ((mu, w, 2 * w), (ml, 0, w)):
                    v = m[:, l, :].rearrange("p (b r) -> p b r", b=nb)[:, :, lo:hi]
                    c.done(g.memset(v, 1), "masks_ok")
                    other = 0 if m is mu else w
                    c.done(g.affine_select(out=v, in_=v, compare_op=ALU.is_ge, fill=0.0, base=-other,
                                           pattern=[[-2 * w, nb], [0, w]], channel_multiplier=1), "masks_ok")
                    c.done(g.affine_select(out=v, in_=v, compare_op=ALU.is_ge, fill=0.0, base=other + w - 1,
                                           pattern=[[2 * w, nb], [0, w]], channel_multiplier=-1), "masks_ok")
            c.done(g.tensor_copy(mone[:], ident[:]), "masks_ok")
            for u in range(3):
                wait(g, "proj_ok", 1 + 4 * (u + 1))
                d, raw = cs[:, 4 * u:4 * u + 4, :], raws[u % 2]
                g.tensor_copy(d[:, :, 0:3], raw[:, :, SEQ:SEQ + 3])
                for n in range(4):
                    r = samples(raw[:, n, HEAD + SEQ:RAW])
                    i = g.tensor_copy(samples(d[:, n, 3:27]), r[:, :, NS:NS + HEAD])
                c.done(i, "cs_ok")
            wait(g, "ss8_ok", 4)
            c.done(g.tensor_tensor(rs8[:], ss8[:], mhalf[:], ALU.pow), "rs8_ok")

            wait(g, "csr_ok", 3)
            g.dma_start(o[2][0, 0], crow[0:3, :]).then_inc(sems["out_done"], 16)
            g.dma_start(o[5].rearrange("l b r c -> (l b r) c"), crow[3:27, :]).then_inc(sems["out_done"], 16)
            wait(g, "osq_ok", 4)
            c.done(g.tensor_tensor(rs8[:], ss8[:], mhalf[:], ALU.pow), "rs8_ok")

            c.done(g.tensor_tensor(tri[:], upi[:], ident[:], ALU.subtract), "tri_ok")
            c.done(g.iota(slots_io[:], pattern=[[1, CAP]], base=0, channel_multiplier=0,
                          allow_small_or_imprecise_dtypes=True), "tri_ok")
            wait(g, "p_smp", 4)
            wait(g, "o_ok", 1)
            for h in range(6):
                if h < 4:
                    st, dec = sgs[:, :, h, :], bc(egl[:, h, 2:10].unsqueeze(2), P, NB, P)
                    c.tick(g.tensor_tensor(st, st, dec, ALU.mult), "dec_ok")
                else:
                    st, dec = sls[:, h - 4], bc(ebl[:, h - 4, 2:10].unsqueeze(2), P, NB, P)
                    c.tick(g.tensor_tensor(st, st, dec, ALU.mult), "dec_ok")
                wait(g, "p_up_s", h)
                src = qkv[0:SMP, 2, QK + h * P:QK + (h + 1) * P] if h < 4 else kdg[0:SMP, 2, (h - 4) * P:(h - 3) * P]
                c.tick(g.tensor_tensor(kdm[0:SMP], bc(src.unsqueeze(1), SMP, NB, P), bc(seqm[:].unsqueeze(2), SMP, NB, P), ALU.mult), "kdm_ok")
            wait(g, "ch_ok", 5)
            wait(g, "gch_ok", 3)
            wait(g, "st_ok", 4)
            g.dma_start(o[3][0, 0].rearrange("h k v -> k h v"), sgp[:]).then_inc(sems["out_done"], 16)
            g.dma_start(o[6][0].rearrange("b h k v -> k (b h) v"), ring[:, 0:UNIT].rearrange("p (a v) -> p a v", v=P)).then_inc(sems["out_done"], 16)
            wait(g, "st_ok", 6)
            for r in range(2):
                g.dma_start(o[4][0, 0].rearrange("(j r) k v -> r k j v", r=2)[r], slp[64 * r:64 * r + 64]).then_inc(sems["out_done"], 16)
            for h in range(H):
                r = 64 * (h % 2)
                g.dma_start(o[7][0, :, h].rearrange("b k v -> k b v"), sls[r:r + 64, h // 2, :, :]).then_inc(sems["st_out2"], 16)
            wait(g, "ss2_ok", 3)
            wait(g, "rs2_in", 1)
            c.done(g.tensor_tensor(rst[:], rst[:], mhalf[:, 0:3], ALU.pow), "rst_ok")
            wait(g, "rs3_in", 1)
            c.done(g.tensor_tensor(rst[:], rst[:], mhalf[:, 0:3], ALU.pow), "rs3_ok")
            wait(g, "out_done", 16 * 6)
            wait(g, "st_out2", 64)

        @block.tensor
        def _(pe):
            c = Count(pe)

            def turn(out, src, n):
                return pe.transpose(out, src, ident[0:n, 0:n])

            wait(pe, "ident_ok", 2)
            wait(pe, "ld_vec", 80)
            c.tick(turn(bank[7][:, 0:60], vrow[:], 60), "p_vec")
            wait(pe, "h_ok", 3)
            for k in range(KT):
                wait(pe, "hT_ok", k - 3)
                for t in range(NTT):
                    i = turn(bank[k % 4][:, TO[t]:TO[t] + TN[t]], xt[0:TN[t], t, k * P:(k + 1) * P], TN[t])
                c.tick(i, "p_hT")
            wait(pe, "ld_cst", 16)
            for n in range(12):
                i = turn(bank[4][:, 24 * n:24 * n + 24], crow[0:24, n * P:(n + 1) * P], 24)
            c.tick(i, "p_cT")
            def project(u):
                wait(pe, f"w_in{1 + u % 2}", 16 * (u // 2 + 1))
                w = slot[1 + u % 2].rearrange("p (k n) -> p k n", k=KT)
                for n in range(4):
                    at = 1 + 4 * u + n
                    wait(pe, "proj_ok", at - 3)
                    for k in range(KT):
                        i = pe.matmul(bank[at % 4][:, 0:T], w[:, k, n * P:(n + 1) * P], hT[:, k, :],
                                      start=k == 0, stop=k == KT - 1)
                    c.tick(i, "p_proj")

            def conv_rows(u):
                if u < 3:
                    wait(pe, "conv_ok", u + 1)
                else:
                    wait(pe, "proj_ok", 21)
                for t in range(NTT):
                    at = 3 * u + t
                    wait(pe, "convt_ok", at - 2)
                    for n in range(4):
                        i = turn(bank[4 + at % 3][0:TN[t], n * P:(n + 1) * P],
                                 convT[:, n, TO[t]:TO[t] + TN[t]], P)
                    c.tick(i, "p_convt")

            wait(pe, "hT_ok", 8)
            wait(pe, "ld_sm", 48)
            wait(pe, "v_step", 1)
            for k in range(KT):
                i = pe.matmul(bank[0][0:80, 0:T], wsm[:, k, :], hT[:, k, :], start=k == 0, stop=k == KT - 1)
            c.tick(i, "p_proj")
            project(0)
            wait(pe, "cT_ok", 1)
            project(1)
            conv_rows(0)
            project(2)
            wait(pe, "gb_ok", 1)
            for t in range(NTT):
                i = turn(bank[7][0:TN[t], 68 * t:68 * t + 68], gb[:, TO[t]:TO[t] + TN[t]], 68)
            c.tick(i, "p_gt")
            conv_rows(1)
            project(3)
            conv_rows(2)
            wait(pe, "ld_gate", 48)
            wait(pe, "convt_ok", 9)
            for j in range(2):
                i = pe.matmul(bank[5 + j][:, 0:T], gkw[64:80, j * P:(j + 1) * P], sm[64:80, :], start=True, stop=True)
            c.tick(i, "p_gk")
            project(4)
            wait(pe, "gk_x", 1)
            for t in range(NTT):
                n = TN[t]
                wait(pe, "qkn_ok", 3 * (t + 1))
                for j in range(3):
                    at = 3 * t + j
                    wait(pe, "qkT_ok", at - 3)
                    src = qkv[0:n, t, (QK, 0, 3 * QK)[j]:(QK, 0, 3 * QK)[j] + QK] if j < 2 else kb[0:n, :]
                    for h in range(H):
                        i = turn(bank[4 + at % 4][:, h * n:(h + 1) * n], src[:, h * P:(h + 1) * P], n)
                    c.tick(i, "p_qkT")
            wait(pe, "qkT_ok", 9)
            conv_rows(3)
            wait(pe, "cs_ok", 3)
            wait(pe, "convt_ok", 12)
            for n in range(12):
                i = turn(bank[4 + n // 4][0:27, (n % 4) * P:(n % 4) * P + P], cs[:, n, :], P)
            c.tick(i, "p_csr")
            wait(pe, "proj_ok", 21)
            for t in range(NTT):
                n = TN[t]
                pe.matmul(bank[t][0:n, 0:H * n], ones[0:4, 0:n], gdiag[0:4, :, TO[t]:TO[t] + n], start=True, stop=True)
            pe.matmul(bank[3][:, 0:8], ones[0:4, :], gdiag[0:4, :, P - 1:SEQ:P], start=True, stop=True)
            c.tick(pe.matmul(bank[3][:, 8:40], ones[0:4, :], gdiag[0:4, :, SEQ + NS - 1:T:NS], start=True, stop=True), "p_gi")
            wait(pe, "qkT_ok", 9)
            wait(pe, "di_ok", 4)
            for t in range(NTT):
                n = TN[t]
                tok = slice(TO[t], TO[t] + n)
                for j in range(2):
                    b = bank[(4, 5, 6, 7, 0, 1)[2 * t + j]]
                    for h in range(H):
                        i = pe.matmul(b[0:n, h * n:(h + 1) * n], KQ[:, 0, h, tok],
                                      (kbT[:, h, tok], KQ[:, 1, h, tok])[j], start=True, stop=True)
                    c.tick(i, "p_MA")
            def gate_half(x):
                u, n, at = 5 + x // 8, x // 2 % 4, 21 + x // 2
                if x % 2 == 0:
                    wait(pe, f"w_in{1 + u % 2}", 16 * (u // 2 + 1))
                    wait(pe, "proj_ok", at)
                w = slot[1 + u % 2].rearrange("p (k n) -> p k n", k=KT)
                for k in range(4 * (x % 2), 4 * (x % 2) + 4):
                    i = pe.matmul(bank[0][:, 0:T], w[:, k, n * P:(n + 1) * P], hT[:, k, :],
                                  start=k == 0, stop=k == KT - 1)
                if x % 2:
                    c.tick(i, "p_proj")

            def gla_level(k):
                gq, gk = (gqk[:, 0:2, :], gqk[:, 2:4, :]) if k == 0 else (gQ, gK)
                wait(pe, "g_lvl", k)
                wait(pe, "ag_ok", k)
                for r in range(2):
                    rows_ = slice(64 * r, 64 * r + 64)
                    for t in range(2):
                        for j in range(2):
                            m = 2 * t + j
                            i = pe.matmul(bank[6 + r][:, m * P:(m + 1) * P], gk[rows_, j, TO[t]:TO[t] + P],
                                          gq[rows_, j, TO[t]:TO[t] + P], start=True, stop=True)
                if k < 3:
                    for r in range(2):
                        rows_ = slice(64 * r, 64 * r + 64)
                        for j in range(2):
                            i = pe.matmul(bank[1][0:SMP, (2 * j + r) * SMP:(2 * j + r + 1) * SMP], gk[rows_, j, SEQ:T],
                                          gq[rows_, j, SEQ:T], start=True, stop=True)
                        if r == 0:
                            c.done(i, "p_low")
                c.tick(i, "p_glvl")

            for t in range(NTT):
                n = TN[t]
                wait(pe, "MA_ok", 2 * t + 1)
                for h in range(H):
                    i = turn(bank[INV_BANKS[t][0]][0:n, h * n:(h + 1) * n], NMt[t][:, h, :], n)
                c.tick(i, "p_tm")
            wait(pe, "MA_ok", 6)
            for k, (l, t) in enumerate(INV):
                n = TN[t]
                by, bu = INV_BANKS[t]
                bt, uo = by, H * n if bu == by else 0
                wait(pe, "inv_ok", inv_at[l - 1, t])
                for h in range(H):
                    i = pe.matmul(bank[by][0:n, h * n:(h + 1) * n], NMt[t][:, h, :], Tt[t][:, h, :], start=True, stop=True)
                c.tick(i, "p_y")
                for x in range(HALVES[k], HALVES[k + 1]):
                    gate_half(x)
                wait(pe, "y_ok", k + 1)
                for h in range(H):
                    pe.matmul(bank[bt][0:n, h * n:(h + 1) * n], Ut[t][:, h, :], Yt[t][:, h, :], start=True, stop=True)
                for h in range(H):
                    i = pe.matmul(bank[bu][0:n, uo + h * n:uo + (h + 1) * n], Yt[t][:, h, :], Ut[t][:, h, :], start=True, stop=True)
                c.tick(i, "p_inv")
                if k == 3:
                    wait(pe, "inv_ok", inv_at[1, 2])
                if 3 <= k <= LEVELS + 3:
                    gla_level(k - 3)
            vr = lambda t, h: qkv[0:TN[t], t, 2 * QK + h * P:2 * QK + (h + 1) * P]
            kr = lambda t, h: qkv[0:TN[t], t, QK + h * P:QK + (h + 1) * P]
            nr = lambda t, h: vn[0:TN[t], t, h * P:(h + 1) * P]

            def heads(b, lhs, rhs, name, n=P):
                for h in range(H):
                    i = pe.matmul(b[0:n, h * P:(h + 1) * P], lhs(h), rhs(h), start=True, stop=True)
                if name:
                    c.tick(i, name)

            wait(pe, "inv_ok", 3 + len(INV))
            wait(pe, "vd_ok", 6)
            wait(pe, "proj_ok", 29)
            heads(bank[0], lambda h: Ut[0][:, h, :], lambda h: vr(0, h), "p_ch")
            wait(pe, "ch_ok", 1)
            heads(bank[1], lambda h: kr(0, h), lambda h: nr(0, h), "p_ch")
            heads(bank[5], lambda h: Att[0][:, h, :], lambda h: nr(0, h), None)
            wait(pe, "ch_ok", 2)
            heads(bank[2], lambda h: KQ[:, 0, h, P:SEQ], lambda h: sgp[:, h, :], None)
            heads(bank[3], lambda h: KQ[:, 1, h, P:SEQ], lambda h: sgp[:, h, :], "p_ch")
            wait(pe, "ch_ok", 3)
            heads(bank[0], lambda h: Ut[1][:, h, :], lambda h: vr(1, h), "p_ch")
            wait(pe, "ch_ok", 4)
            heads(bank[1], lambda h: kr(1, h), lambda h: nr(1, h), "p_ch")
            heads(bank[6], lambda h: Att[1][:, h, :], lambda h: nr(1, h), "p_ch")
            wait(pe, "ld_st", 128)
            for b in range(NB):
                for h in range(H):
                    ov = bank[7][:, 64 * h:64 * h + 64].rearrange("p (a i) -> p a i", a=2)[:, :, NS * b:NS * (b + 1)]
                    i = pe.matmul(ov, sgs[:, b, h, :], KQ[:, :, h, SEQ + NS * b:SEQ + NS * (b + 1)], start=True, stop=True)
            c.tick(i, "p_smp")
            wait(pe, "smk_ok", 1)
            for h in range(H):
                for j in range(2):
                    i = turn(bank[(4, 7)[j]][0:SMP, h * P:(h + 1) * P], skT[:].rearrange("p a b -> p (a b)")[:, 64 * h + 32 * j:64 * h + 32 * j + 32], P)
            c.tick(i, "p_smp")
            wait(pe, "smr_ok", 1)
            heads(bank[4], lambda h: Ut[2][:, h, :], lambda h: vr(2, h), "p_smp", SMP)
            wait(pe, "smr_ok", 2)
            heads(bank[4], lambda h: Att[2][:, h, :], lambda h: nr(2, h), "p_smp", SMP)

            wait(pe, "ch_ok", 6)
            wait(pe, "smr_ok", 3)
            wait(pe, "g_lvl", LEVELS + 1)
            wait(pe, "ag_ok", LEVELS + 1)
            for t in range(NTT):
                for j in range(2):
                    i = turn(bank[t][0:TN[t], j * P:(j + 1) * P], gK[:, j, TO[t]:TO[t] + TN[t]], P)
            c.tick(i, "p_gkd")
            vgr = lambda t, h: vg[0:TN[t], t, h * P:(h + 1) * P]

            def gla_state(t):
                for h in range(H):
                    r = 64 * (h % 2)
                    i = pe.matmul(bank[4][r:r + 64, (h // 2) * P:(h // 2) * P + P], kdg[:, t, 64 * h:64 * h + 64],
                                  vgr(t, h), start=True, stop=True)
                c.tick(i, "p_gch")

            wait(pe, "kdg_ok", 3)
            gla_state(0)
            heads(bank[3], lambda h: AGt[0][:, h, :], lambda h: vgr(0, h), None)
            heads(bank[7], lambda h: AGt[1][:, h, :], lambda h: vgr(1, h), None)
            wait(pe, "gch_ok", 1)
            for h in range(H):
                r = 64 * (h % 2)
                i = pe.matmul(bank[5 + h % 2][:, (h // 2) * P:(h // 2) * P + P], gQ[r:r + 64, h // 2, P:SEQ],
                              slp[r:r + 64, h // 2, :], start=True, stop=True)
            c.tick(i, "p_gch")
            gla_state(1)
            for b in range(NB):
                for h in range(H):
                    r = 64 * (h % 2)
                    at = 32 * (h // 2) + NS * b
                    i = pe.matmul(bank[h % 2][:, at:at + NS], sls[r:r + 64, h // 2, b, :],
                                  gQ[r:r + 64, h // 2, SEQ + NS * b:SEQ + NS * (b + 1)], start=True, stop=True)
            c.tick(i, "p_gs")
            wait(pe, "gsT_ok", 2)
            for h in range(H):
                i = turn(bank[2][0:SMP, h * P:(h + 1) * P], skT[:, h % 2, 32 * (h // 2):32 * (h // 2) + 32], P)
            wait(pe, "gch_ok", 3)
            heads(bank[4], lambda h: AGt[2][:, h, :], lambda h: vgr(2, h), "p_gs", SMP)
            for t in range(NTT):
                n = TN[t]
                wait(pe, "o_ok", t + 1)
                for j in range(2):
                    at = 2 * t + j
                    wait(pe, "oT_ok", at - 1)
                    for h in range(H):
                        i = turn(bank[at % 2][:, h * n:(h + 1) * n], ot[0:n, t, (4 * j + h) * P:(4 * j + h + 1) * P], n)
                    c.tick(i, "p_oT")
            wait(pe, "oT_ok", 6)
            for u in range(2):
                wait(pe, "w_out", 16 * (u + 1)) if u == 0 else wait(pe, "w_out2", 16)
                w = slot[2 - u].rearrange("p (k n) -> p k n", k=KT)
                for n in range(4):
                    at = 29 + 4 * u + n
                    wait(pe, "proj_ok", at - 3)
                    for k in range(KT):
                        i = pe.matmul(bank[at % 4][:, 0:T], w[:, k, n * P:(n + 1) * P], zg[:, k, :],
                                      start=k == 0, stop=k == KT - 1)
                    c.tick(i, "p_proj")

            for h in range(6):
                wait(pe, "kdm_ok", h + 1)
                b0 = (4, 6)[h % 2]
                wait(pe, "st_ok", h - 1)
                for b in range(NB):
                    ob_ = bank[b0 + b // 4]
                    cols = slice((b % 4) * P, (b % 4) * P + P)
                    if h < 4:
                        i = pe.matmul(ob_[:, cols], kdm[0:SMP, b, :], vn[0:SMP, 2, h * P:(h + 1) * P], start=True, stop=True)
                    else:
                        for r in range(2):
                            hh = 2 * (h - 4) + r
                            i = pe.matmul(ob_[64 * r:64 * r + 64, cols], kdm[0:SMP, b, 64 * r:64 * r + 64],
                                          vg[0:SMP, 2, hh * P:(hh + 1) * P], start=True, stop=True)
                c.tick(i, "p_up_s")
            wait(pe, "proj_ok", 37)
            wait(pe, "st_ok", 6)
            for t in range(NTT):
                for j in range(2):
                    at = 2 * t + j
                    wait(pe, "x2_ok", at - 3)
                    for n in range(4):
                        i = turn(bank[4 + at % 4][0:TN[t], n * P:(n + 1) * P], hT[:, 4 * j + n, TO[t]:TO[t] + TN[t]], P)
                    c.tick(i, "p_x2")
            wait(pe, "xn_ok", 3)
            for k in range(KT):
                wait(pe, "xnT_ok", k - 3)
                for t in range(NTT):
                    i = turn(bank[k % 4][:, TO[t]:TO[t] + TN[t]], ot[0:TN[t], t, k * P:(k + 1) * P], TN[t])
                c.tick(i, "p_xnT")
            wait(pe, "xnT_ok", 8)
            wait(pe, "ld_router", 32)
            for t in range(NTT):
                for k in range(KT):
                    i = pe.matmul(bank[4][0:TN[t], E_N * t:E_N * (t + 1)], hT[:, k, TO[t]:TO[t] + TN[t]], wr[:, k, :],
                                  start=k == 0, stop=k == KT - 1)
            c.tick(i, "p_lg")
            wait(pe, "route_ok", 1)
            wait(pe, "tri_ok", 2)
            sel = lambda t: selm[0:TN[t], E_N * t:E_N * (t + 1)]
            for t in range(NTT):
                for t2 in range(t + 1):
                    lhs = ones[0:TN[t2], 0:TN[t]] if t2 < t else tri[0:TN[t], 0:TN[t]]
                    pe.matmul(bank[5][0:TN[t], E_N * t:E_N * (t + 1)], lhs, sel(t2), start=t2 == 0, stop=t2 == t)
            for t in range(NTT):
                i = pe.matmul(bank[6][0:32, 0:E_N], ones[0:TN[t], 0:32], sel(t), start=t == 0, stop=t == NTT - 1)
            c.tick(i, "p_pos")

            def scatter(w, ats):
                for at in ats:
                    t, j = at // 2, at % 2
                    pe.wait_ge(sems["sc_ok"], w * 6 + max(at, 1))
                    pe.matmul(bank[6 + at % 2][0:TN[t], :], S[:, TO[t]:TO[t] + TN[t]], yr[:, 512 * j:512 * (j + 1)],
                              start=True, stop=True).then_inc(sems["p_sc"], 1)

            def start(b, row_of, bias):
                for h in range(2):
                    pe.matmul(bank[b][CAP * h:CAP * (h + 1), :], row_of[:, h, :], bias, start=True, stop=False, skip_group_check=True)

            def up(i, q):
                pe.wait_ge(sems["sel_ok"], i * 4 + (2 * q + 1))
                for g in range(2):
                    start(g, sel_gu[:, 2 * g:2 * g + 2, :], b_gu)
                for u in range(4):
                    pe.wait_ge(sems[f"ld_w{u}"], i * 32 + 16 * (q + 1))
                    w = slot[WSLOT[u]].rearrange("p (k g h n) -> p k g h n", k=2, g=2, h=2)
                    for kk in range(2):
                        k = 2 * u + kk
                        for g in range(2):
                            for h in range(2):
                                last = pe.matmul(bank[g][CAP * h:CAP * (h + 1), :], xeT[:, k, q * CAP:(q + 1) * CAP], w[:, kk, g, h, :],
                                                 start=False, stop=k == KT - 1, skip_group_check=True)
                    last.then_inc(sems["w_used" if u < 3 else "p_up"], 1)

            def act_t(w):
                pe.wait_ge(sems["act_ok"], w)
                for j in range(4):
                    last = turn(bank[2][:, j * P:(j + 1) * P], gu[:, 1, j * P:(j + 1) * P], P)
                last.then_inc(sems["p_at"], 1)

            def down(i, q):
                pe.wait_ge(sems["sel_ok"], i * 4 + (2 * q + 3))
                start(3, sel_dn, b_dn)
                for u in range(4, 6):
                    pe.wait_ge(sems[f"ld_w{u}"], i * 32 + 16 * (q + 1))
                    w = slot[WSLOT[u]].rearrange("p (k h n) -> p k h n", k=4, h=2)
                    for k in range(4):
                        for h in range(2):
                            last = pe.matmul(bank[3][CAP * h:CAP * (h + 1), :], aT[:, k, CAP * (u - 4):CAP * (u - 3)], w[:, k, h, :],
                                             start=False, stop=u == 5 and k == 3, skip_group_check=True)
                    last.then_inc(sems["w_used" if u < 5 else "p_yd"], 1)

            def gather(j):
                for n in range(4):
                    for t in range(NTT):
                        lhs = ot[0:TN[t], t, :].rearrange("p (m k) -> p k m", k=KT)[:, 4 * j + n, :]
                        last = pe.matmul(bank[4 + j][:, n * P:(n + 1) * P], lhs, G[0:TN[t], t, :], start=t == 0, stop=t == NTT - 1)
                last.then_inc(sems["p_gat"], 1)

            wait(pe, "rnd_ok", 1)
            wait(pe, "p_S", 1)
            wait(pe, "G_ok", 1)
            gather(0)
            gather(1)
            wait(pe, "ld_bias", 32)
            rounds = pe.value_load(rnd[0:1, 0:1], min_val=1, max_val=5)
            with pe.Fori(0, rounds * PAIRS) as i:
                pe.wait_ge(sems["xe_ok"], i * 2 + 2)
                up(i, 0)
                pe.wait_ge(sems["G_ok"], i * 2 + 2)
                for t in range(NTT):
                    last = turn(bank[4][:, TO[t]:TO[t] + TN[t]], GG[0:TN[t], t, :], TN[t])
                last.then_inc(sems["p_S"], 1)
                pe.wait_ge(sems["yb_ok"], i * 4 + 1)
                scatter(i, range(2))
                act_t(i * 2 + 1)
                scatter(i, range(2, 6))
                pe.wait_ge(sems["aT_ok"], i * 2 + 1)
                down(i, 0)
                up(i, 1)
                pe.wait_ge(sems["S_ok"], i + 2)
                pe.wait_ge(sems["G_ok"], i * 2 + 3)
                gather(0)
                act_t(i * 2 + 2)
                gather(1)
                pe.wait_ge(sems["aT_ok"], i * 2 + 2)
                pe.wait_ge(sems["yb_ok"], i * 4 + 3)
                down(i, 1)
            total = rounds * PAIRS
            pe.wait_ge(sems["S_ok"], total + 1)
            pe.wait_ge(sems["yb_ok"], total * 4 + 1)
            scatter(total, range(6))

        @block.vector
        def _(v):
            c = Count(v)
            v.memset(wsm[:, :, 4:32], 0.0)
            c.done(v.memset(wsm[:, :, 36:64], 0.0), "v_step")
            v.memset(ss[:], 1.0)
            v.memset(ss8[:], 1.0)
            v.memset(mhalf[:], -0.5)
            v.memset(gb[:], 0.0)
            v.memset(resets[:], 1.0)
            c.done(v.memset(gt[:], 0.0), "v_step")
            c.done(v.memset(resets[:, 0:SEQ:P], 0.0), "v_step")
            c.done(v.memset(resets[:, SEQ:T:NS], 0.0), "v_step")
            c.done(v.memset(rst[:], 1.0), "rst_in")
            wait(v, "ss_ok", 3)
            c.done(v.tensor_scalar(rst[:], ss[:], 1.0 / D, EPS, ALU.mult, ALU.add), "rst_in")
            wait(v, "rst_ok", 1)
            for t in range(NTT):
                n = TN[t]
                c.done(v.tensor_scalar(xt[0:n, t, :], xt[0:n, t, :], rst[0:n, t:t + 1], None, ALU.mult), "h_ok")
            wait(v, "p_vec", 1)
            c.done(v.tensor_copy(vecT[:], bank[7][:, 0:60]), "vec_ok")
            for k in range(KT):
                wait(v, "p_hT", k + 1)
                c.done(v.tensor_scalar(hT[:, k, :], bank[k % 4][:, 0:T], vecT[:, k:k + 1], None, ALU.mult), "hT_ok")
            wait(v, "p_cT", 1)
            c.done(v.tensor_copy(cT[:].rearrange("p a b -> p (a b)"), bank[4][:, 0:288]), "cT_ok")
            wait(v, "proj_ok", 1)
            wait(v, "ld_gate", 48)
            c.done(v.tensor_scalar(gtmp[0:4, 0, :], sm[0:4, :], gate2[:, 1:2], None, ALU.add), "v_step")
            c.tick(v.scalar_tensor_tensor(out=gtmp[0:4, 1, :], in0=gtmp[0:4, 0, :], scalar=-1.0, in1=gtmp[0:4, 0, :],
                                          op0=ALU.mult, op1=ALU.max), "gate_x")

            def conv(u):
                wait(v, "proj_ok", 1 + 4 * (u + 1))
                hist = cT[:, 4 * u:4 * u + 4, :]
                raw, ce = raws[u % 2], ces[u % 2]
                c.done(v.memset(raw[:, :, 0:HEAD], 0.0), "v_step")
                for n in range(4):
                    c.done(v.tensor_copy(samples(raw[:, n, HEAD + SEQ:RAW])[:, :, 0:HEAD], samples(hist[:, n, :])), "v_step")
                for i in range(4):
                    for n in range(4):
                        w = vecT[:, 8 + 12 * i + 4 * u + n:9 + 12 * i + 4 * u + n]
                        if i == 0:
                            c.done(v.tensor_scalar(ce[:, n, 0:CW], raw[:, n, 0:CW], w, None, ALU.mult), "v_step")
                        else:
                            c.done(v.scalar_tensor_tensor(out=ce[:, n, 0:CW], in0=raw[:, n, i:i + CW], scalar=w,
                                                          in1=ce[:, n, 0:CW], op0=ALU.mult, op1=ALU.add), "v_step")
                c.tick(v.memset(ss[:, 0:1], 1.0), "conv_lin")
                wait(v, "conv_sig", u + 1)
                e = raw[:, :, 0:CW]
                c.done(v.tensor_tensor(convT[:, :, 0:SEQ], ce[:, :, 0:SEQ], e[:, :, 0:SEQ], ALU.mult), "v_step")
                at = HEAD + SEQ
                for n in range(4):
                    r = lambda b: b[:, n, at:RAW].rearrange("p (b j) -> p b j", b=NB)[:, :, 0:NS]
                    i = v.tensor_tensor(convT[:, n, SEQ:T].rearrange("p (b j) -> p b j", b=NB), r(ce), r(raw), ALU.mult)
                c.done(i, "conv_ok")

            def rows(u):
                for t in range(NTT):
                    at = 3 * u + t
                    wait(v, "p_convt", at + 1)
                    dst = qkv[0:TN[t], t, QK * u:QK * (u + 1)] if u < 3 else vg[0:TN[t], t, :]
                    c.done(v.tensor_copy(dst, bank[4 + at % 3][0:TN[t], :]), "convt_ok")

            conv(0)
            wait(v, "gate_e", 3)
            wait(v, "gate_l", 1)
            g0 = gtmp[0:4, 0, :]
            c.done(v.tensor_scalar(g0, g0, 0.0, None, ALU.max), "v_step")
            c.done(v.tensor_tensor(g0, g0, gtmp[0:4, 1, :], ALU.add), "v_step")
            c.done(v.tensor_scalar(g0, g0, gate2[:, 2:3], -1.0, ALU.mult, ALU.mult), "v_step")
            c.done(v.tensor_tensor_scan(gb[0:4, :], resets[0:4, :], g0, 0.0, ALU.mult, ALU.add), "v_step")
            be = gtmp[32:36, 0, :]
            c.done(v.tensor_scalar(be, be, 1.0, None, ALU.add), "v_step")
            c.done(v.reciprocal(gb[32:36, :], be), "v_step")
            gp = gb[0:4, 0:SEQ].rearrange("p (c i) -> p c i", c=2)
            gs = gb[0:4, SEQ:T].rearrange("p (b j) -> p b j", b=NB)
            dp = gb[64:68, 0:SEQ].rearrange("p (c i) -> p c i", c=2)
            ds = gb[64:68, SEQ:T].rearrange("p (b j) -> p b j", b=NB)
            v.tensor_tensor(dp, bc(gp[:, :, P - 1:P], 4, 2, P), gp, ALU.subtract)
            v.tensor_tensor(ds, bc(gs[:, :, NS - 1:NS], 4, NB, NS), gs, ALU.subtract)
            c.done(v.tensor_tensor(gdiag[0:4], bc(gb[0:4, :].unsqueeze(1), 4, H, T),
                                   bc(ident[0:4, 0:4].unsqueeze(2), 4, H, T), ALU.mult), "gb_ok")
            rows(0)
            conv(1)
            wait(v, "p_gt", 1)
            for t in range(NTT):
                c.done(v.tensor_copy(gt[0:TN[t], t, :], bank[7][0:TN[t], 68 * t:68 * t + 68]), "gt_ok")
            rows(1)
            conv(2)
            rows(2)
            for t in range(NTT):
                n = TN[t]
                wait(v, "h_ok", 3)
                sq = ob[0:n, 0:2 * QK]
                c.done(v.tensor_tensor(sq, qkv[0:n, t, 0:2 * QK], qkv[0:n, t, 0:2 * QK], ALU.mult), "v_step")
                c.done(v.tensor_reduce(ss8[0:n, 8 * t:8 * t + 8], sq.rearrange("p (a d) -> p a d", d=P), AX_X, ALU.add), "ss8_ok")
            c.done(v.tensor_scalar(ss8[:], ss8[:], EPS, None, ALU.add), "ss8_ok")
            wait(v, "p_gk", 1)
            for j in range(2):
                c.done(v.tensor_scalar(gE[:, j, :], bank[5 + j][:, 0:T], vecT[:, 56 + j:57 + j], None, ALU.add), "v_step")
            c.tick(v.scalar_tensor_tensor(out=gQ, in0=gE, scalar=-1.0, in1=gE, op0=ALU.mult, op1=ALU.max), "gk_x")
            wait(v, "rs8_ok", 1)
            r8 = rs8[:].rearrange("p (t a) -> p t a", t=3)
            c.done(v.tensor_scalar(r8[:, :, 0:4], r8[:, :, 0:4], float(P) ** -0.5, None, ALU.mult), "v_step")

            def hd(ap):
                return ap.rearrange("p (a d) -> p a d", d=P)

            wait(v, "gt_exp", 2)
            for t in range(NTT):
                n = TN[t]
                q, k, vv = (hd(qkv[0:n, t, QK * j:QK * (j + 1)]) for j in range(3))
                beta = bc(gt[0:n, t, 32:36].unsqueeze(2), n, H, P)
                c.done(v.tensor_tensor(hd(qkv[0:n, t, 0:2 * QK]), hd(qkv[0:n, t, 0:2 * QK]), bc(r8[0:n, t, :].unsqueeze(2), n, 8, P), ALU.mult), "qkn_ok")
                wait(v, "p_qkT", 3 * t)
                c.done(v.tensor_tensor(hd(kb[0:n, :]), k, beta, ALU.mult), "qkn_ok")
                c.done(v.tensor_tensor(vv, vv, beta, ALU.mult), "qkn_ok")
            wait(v, "gk_l", 1)
            c.done(v.tensor_scalar(gE, gE, 0.0, None, ALU.min), "v_step")
            c.done(v.tensor_tensor(gE, gE, gQ, ALU.subtract), "v_step")
            c.done(v.tensor_scalar(gE, gE, 1.0 / 16, None, ALU.mult), "v_step")
            for j in range(2):
                c.done(v.tensor_tensor_scan(bT[:, j, :], resets[:], gE[:, j, :], 0.0, ALU.mult, ALU.add), "bT_ok")
            rows(3)
            wait(v, "p_csr", 1)
            for n in range(3):
                c.done(v.tensor_copy(crow[0:27, 512 * n:512 * (n + 1)], bank[4 + n][0:27, :]), "csr_ok")

            c.done(v.tensor_tensor(nbeg[:], gt[:, :, 32:36], eg[:], ALU.mult), "v_step")
            c.done(v.tensor_scalar(nbeg[:], nbeg[:], -1.0, None, ALU.mult), "v_step")
            wait(v, "p_gi", 1)
            wait(v, "out_done", 32)
            for t in range(NTT):
                n = TN[t]
                for h in range(H):
                    i = v.tensor_scalar(Dtt[t][:, h, :], bank[t][0:n, h * n:(h + 1) * n], gt[0:n, t, h:h + 1], 0.0, ALU.subtract, ALU.min)
                c.done(i, "di_ok")
            v.tensor_copy(egl[:, :, 0:2], bank[3][:, 0:8].rearrange("p (h x) -> p h x", h=H))
            c.done(v.tensor_copy(egl[:, :, 2:10], bank[3][:, 8:40].rearrange("p (h x) -> p h x", h=H)), "di_ok")
            wait(v, "dexp_ok", 4)
            wait(v, "masks_ok", 48)
            for t in range(NTT):
                n = TN[t]
                m = upi[:] if t < 2 else upis[:]
                c.done(v.tensor_tensor(Dtt[t], Dtt[t], bc(m.unsqueeze(1), n, H, n), ALU.mult), "d_ok")
            for t in range(NTT):
                n = TN[t]
                for j in range(2):
                    wait(v, "p_MA", 2 * t + j + 1)
                    b = bank[(4, 5, 6, 7, 0, 1)[2 * t + j]][0:n, 0:H * n].rearrange("p (h i) -> p h i", h=H)
                    if j == 0:
                        c.done(v.scalar_tensor_tensor(out=NMt[t], in0=b, scalar=-1.0, in1=Dtt[t], op0=ALU.mult, op1=ALU.mult), "MA_ok")
                    else:
                        c.done(v.tensor_tensor(Att[t], b, Dtt[t], ALU.mult), "MA_ok")
            for t in range(NTT):
                n = TN[t]
                eye = bc(ident[0:n, 0:n].unsqueeze(1), n, H, n)
                v.tensor_copy(Ut[t], eye)
                c.done(v.tensor_copy(Tt[t], eye), "v_step")
                wait(v, "p_tm", t + 1)
                v.copy_predicated(Ut[t], bc(mu[0:n, 0, 0:n].unsqueeze(1), n, H, n), NMt[t])
                c.done(v.copy_predicated(Tt[t], bc(ml[0:n, 0, 0:n].unsqueeze(1), n, H, n),
                                         bank[INV_BANKS[t][0]][0:n, 0:H * n].rearrange("p (h i) -> p h i", h=H)), "inv_ok")
            for t in range(NTT):
                n = TN[t]
                k = hd(qkv[0:n, t, QK:2 * QK])
                c.done(v.tensor_tensor(k, k, bc(ekd[0:n, t, :].unsqueeze(2), n, H, P), ALU.mult), "vd_ok")
            v.memset(AG[:], 0.0)
            c.done(v.memset(AGs[:], 0.0), "v_step")

            def level(l):
                w = 1 << l
                n = T if l < 2 else SEQ
                b4 = bT[:, :, 0:n].rearrange("p j (b r) -> p j b r", r=2 * w)
                e4 = gE[:, :, 0:n].rearrange("p j (b r) -> p j b r", r=2 * w)
                nb = n // (2 * w)
                e = gE[:, :, 0:n]
                c.done(v.tensor_tensor(e4, b4, bc(b4[:, :, :, w - 1:w], P, 2, nb, 2 * w), ALU.subtract), "v_step")
                c.done(v.scalar_tensor_tensor(out=e, in0=e, scalar=-1.0, in1=e, op0=ALU.mult, op1=ALU.min), "g_abs")

            def decayed(l):
                n = T if l < 2 else SEQ
                e = gE[:, :, 0:n]
                wait(v, "g_exp", l + 1)
                v.tensor_tensor(gQ[:, :, 0:n], gqk[:, 0:2, 0:n], e, ALU.mult)
                c.done(v.tensor_tensor(gK[:, :, 0:n], gqk[:, 2:4, 0:n], e, ALU.mult), "g_lvl")

            def gather(k):
                wait(v, "p_glvl", k + 1)
                m = mone[:] if k == 0 else mu[:, k - 1, :]
                for r in range(2):
                    dst = AG[:].rearrange("p (q r) i -> p q r i", r=2)[:, :, r, :]
                    i = v.copy_predicated(dst, bc(m.unsqueeze(1), P, 4, P), bank[6 + r][:].rearrange("p (q i) -> p q i", q=4))
                if k < 3:
                    i = v.copy_predicated(AGs[0:SMP], bc(m[0:SMP, 0:SMP].unsqueeze(1), SMP, H, SMP),
                                          bank[1][0:SMP, 0:H * SMP].rearrange("p (q i) -> p q i", q=H))
                c.done(i, "ag_ok")

            for k, (l, t) in enumerate(INV):
                n = TN[t]
                bt, bu = INV_BANKS[t]
                uo = H * n if bu == bt else 0
                wait(v, "p_inv", k + 1)
                v.copy_predicated(Tt[t], bc(ml[0:n, l, 0:n].unsqueeze(1), n, H, n), bank[bt][0:n, 0:H * n].rearrange("p (h i) -> p h i", h=H))
                c.done(v.copy_predicated(Ut[t], bc(mu[0:n, l, 0:n].unsqueeze(1), n, H, n),
                                         bank[bu][0:n, uo:uo + H * n].rearrange("p (h i) -> p h i", h=H)), "inv_ok")
                for x in gate_tiles[k]:
                    wait(v, "proj_ok", 22 + x)
                    c.done(v.tensor_tensor(zg[:, x, :], zg[:, x, :], ce_z[:, x % 4, :], ALU.mult), "zg_ok")
                if 3 <= k <= LEVELS + 3:
                    gather(k - 3)
                if 3 <= k < LEVELS + 3:
                    decayed(k - 3)
                if 2 <= k < LEVELS + 2:
                    level(k - 2)
                if k == 4 + LEVELS:
                    wait(v, "ebl_ok", 2)
                    c.done(v.tensor_tensor(gQ, gqk[:, 0:2, :], gE, ALU.mult), "g_abs")
                    for j in range(2):
                        bp = bT[:, j, 0:SEQ].rearrange("p (c i) -> p c i", c=2)
                        bs = bT[:, j, SEQ:T].rearrange("p (b i) -> p b i", b=NB)
                        v.tensor_tensor(gE[:, j, 0:SEQ].rearrange("p (c i) -> p c i", c=2), bc(bp[:, :, P - 1:P], P, 2, P), bp, ALU.subtract)
                        i = v.tensor_tensor(gE[:, j, SEQ:T].rearrange("p (b i) -> p b i", b=NB), bc(bs[:, :, NS - 1:NS], P, NB, NS), bs, ALU.subtract)
                    c.done(i, "g_abs")
            wait(v, "ebl_ok", 3)
            c.done(v.tensor_tensor(gK, gqk[:, 2:4, :], gE, ALU.mult), "g_lvl")
            for t in range(3):
                c.tick(v.memset(ss[:, t:t + 1], 1.0), "vd_ok")

            def col(ap, n):
                return bc(ap.unsqueeze(2), n, H, P)

            wait(v, "p_ch", 1)
            c.done(v.tensor_copy(vn[:, 0, :], bank[0][:]), "ch_ok")
            wait(v, "p_ch", 2)
            c.done(v.tensor_copy(sgp[:].rearrange("p h d -> p (h d)"), bank[1][:]), "ch_ok")
            wait(v, "p_ch", 3)
            tmp = hd(vn[:, 1, :])
            c.done(v.tensor_tensor(tmp, hd(bank[2][:]), col(nbeg[:, 1, :], P), ALU.mult), "v_step")
            vv = qkv[:, 1, 2 * QK:3 * QK]
            c.done(v.tensor_tensor(vv, vv, vn[:, 1, :], ALU.add), "ch_ok")
            o1 = ot[:, 1, 0:QK]
            c.done(v.tensor_tensor(hd(o1), hd(bank[3][:]), col(eg[:, 1, :], P), ALU.mult), "v_step")
            wait(v, "p_ch", 4)
            c.done(v.tensor_copy(vn[:, 1, :], bank[0][:]), "ch_ok")
            wait(v, "p_ch", 5)
            c.done(v.tensor_tensor(sgp[:], sgp[:], bc(egl[:, :, 1:2], P, H, P), ALU.mult), "v_step")
            c.done(v.tensor_tensor(sgp[:].rearrange("p h d -> p (h d)"), sgp[:].rearrange("p h d -> p (h d)"), bank[1][:], ALU.add), "ch_ok")
            wait(v, "p_ch", 6)
            v.tensor_copy(ot[:, 0, 0:QK], bank[5][:])
            c.done(v.tensor_tensor(o1, o1, bank[6][:], ALU.add), "ch_ok")
            wait(v, "p_smp", 2)
            os_ = ot[0:SMP, 2, 0:QK]
            vs = qkv[0:SMP, 2, 2 * QK:3 * QK]
            c.done(v.tensor_tensor(hd(vn[0:SMP, 2, :]), hd(bank[4][0:SMP, :]), col(nbeg[0:SMP, 2, :], SMP), ALU.mult), "v_step")
            v.tensor_tensor(hd(os_), hd(bank[7][0:SMP, :]), col(eg[0:SMP, 2, :], SMP), ALU.mult)
            c.done(v.tensor_tensor(vs, vs, vn[0:SMP, 2, :], ALU.add), "smr_ok")
            wait(v, "p_smp", 3)
            c.done(v.tensor_copy(vn[0:SMP, 2, :], bank[4][0:SMP, :]), "smr_ok")
            wait(v, "p_smp", 4)
            c.done(v.tensor_tensor(os_, os_, bank[4][0:SMP, :], ALU.add), "smr_ok")

            sl2 = slp[:].rearrange("p j d -> p (j d)")
            wait(v, "p_gch", 1)
            c.done(v.tensor_copy(sl2, bank[4][:, 0:256]), "gch_ok")
            wait(v, "p_gch", 2)
            v.tensor_copy(ot[:, 0, QK:D], bank[3][:])
            c.done(v.tensor_copy(ot[:, 1, QK:D], bank[7][:]), "v_step")
            for r in range(2):
                d = ot[:, 1, QK:D].rearrange("p (j r d) -> p j r d", j=2, r=2)[:, :, r, :]
                i = v.tensor_tensor(d, d, bank[5 + r][:, 0:256].rearrange("p (j d) -> p j d", j=2), ALU.add)
            c.done(i, "gch_ok")
            wait(v, "p_gch", 3)
            for j in range(2):
                i = v.scalar_tensor_tensor(out=slp[:, j, :], in0=slp[:, j, :], scalar=ebl[:, j, 1:2], in1=bank[4][:, j * P:(j + 1) * P],
                                           op0=ALU.mult, op1=ALU.add)
            c.done(i, "gch_ok")
            wait(v, "p_gs", 2)
            og = ot[0:SMP, 2, QK:D]
            c.done(v.tensor_copy(og, bank[2][0:SMP, :]), "v_step")
            c.done(v.tensor_tensor(og, og, bank[4][0:SMP, :], ALU.add), "v_step")
            for t in range(NTT):
                n = TN[t]
                c.done(v.tensor_tensor(osq[0:n], ot[0:n, t, :], ot[0:n, t, :], ALU.mult), "v_step")
                c.done(v.tensor_reduce(ss8[0:n, 8 * t:8 * t + 8], hd(osq[0:n]), AX_X, ALU.add), "osq_ok")
            c.done(v.tensor_scalar(ss8[:], ss8[:], 1.0 / P, EPS, ALU.mult, ALU.add), "osq_ok")
            wait(v, "rs8_ok", 2)
            for t in range(NTT):
                n = TN[t]
                c.done(v.tensor_tensor(hd(ot[0:n, t, :]), hd(ot[0:n, t, :]), bc(r8[0:n, t, :].unsqueeze(2), n, 8, P), ALU.mult), "o_ok")
            for t in range(NTT):
                n = TN[t]
                for j in range(2):
                    wait(v, "p_oT", 2 * t + j + 1)
                    z = zg[:, 4 * j:4 * j + 4, TO[t]:TO[t] + n]
                    c.done(v.scalar_tensor_tensor(out=z, in0=bank[j][:, 0:4 * n].rearrange("p (h i) -> p h i", h=H), scalar=vecT[:, 58 + j:59 + j],
                                                  in1=z, op0=ALU.mult, op1=ALU.mult), "oT_ok")

            for h in range(6):
                wait(v, "p_up_s", h + 1)
                wait(v, "dec_ok", h + 1)
                for k in range(2):
                    st = sgs[:, 4 * k:4 * k + 4, h, :] if h < 4 else sls[:, h - 4, 4 * k:4 * k + 4, :]
                    i = v.tensor_tensor(st, st, bank[(4, 6)[h % 2] + k][:].rearrange("p (b d) -> p b d", b=4), ALU.add)
                c.done(i, "st_ok")
            wait(v, "x_again", 32)
            for t in range(NTT):
                for j in range(2):
                    at = 2 * t + j
                    wait(v, "p_x2", at + 1)
                    d = x2[0:TN[t], t, 512 * j:512 * (j + 1)]
                    c.done(v.tensor_tensor(d, d, bank[4 + at % 4][0:TN[t], :], ALU.add), "x2_ok")
            wait(v, "ss2_ok", 3)
            c.done(v.tensor_scalar(rst[:], ss[:], 1.0 / D, EPS, ALU.mult, ALU.add), "rs2_in")
            wait(v, "rst_ok", 2)
            wait(v, "ld_ffn", 16)
            for t in range(NTT):
                n = TN[t]
                c.done(v.scalar_tensor_tensor(out=ot[0:n, t, :], in0=x2[0:n, t, :], scalar=rst[0:n, t:t + 1], in1=wbc[0:n], op0=ALU.mult, op1=ALU.mult), "xn_ok")
            v.memset(lg[:], 0.0)
            v.memset(r32[:], 1.0)
            c.done(v.memset(selm[:], 0.0), "v_step")
            c.done(v.memset(r32[:, 0:3 * E_N:E_N], 0.0), "v_step")
            wait(v, "p_lg", 1)
            for t in range(NTT):
                n = TN[t]
                c.done(v.tensor_tensor(lg[0:n, E_N * t:E_N * (t + 1)], bank[4][0:n, E_N * t:E_N * (t + 1)], brt[0:n], ALU.add), "lg_ok")
            for t in range(NTT):
                c.done(v.max(m8[:, t, :], lg[:, E_N * t:E_N * (t + 1)]), "v_step")
            e3 = lambda ap: ap[:].rearrange("p (t e) -> p t e", t=3)
            c3 = lambda ap: bc(ap, P, 3, E_N)
            m1, m4 = m8[:, :, 0:1], m8[:, :, 3:4]
            c.done(v.tensor_tensor(e3(gates), e3(lg), c3(m1), ALU.subtract), "lg_ok")
            c.done(v.tensor_tensor(e3(gts), e3(lg), c3(m4), ALU.is_gt), "v_step")
            c.done(v.tensor_tensor(e3(eqs), e3(lg), c3(m4), ALU.is_equal), "v_step")
            c.done(v.tensor_reduce(ndd[:], e3(gts), AX_X, ALU.add), "v_step")
            c.done(v.tensor_scalar(ndd[:], ndd[:], -1.0, float(TOPK), ALU.mult, ALU.add), "v_step")
            c.done(v.tensor_tensor_scan(pre[:], r32[:], eqs[:], 0.0, ALU.mult, ALU.add), "v_step")
            c.done(v.tensor_tensor(e3(pre), e3(pre), c3(ndd[:].unsqueeze(2)), ALU.is_le), "v_step")
            c.done(v.tensor_tensor(eqs[:], eqs[:], pre[:], ALU.mult), "v_step")
            c.done(v.tensor_tensor(selm[:], gts[:], eqs[:], ALU.add), "route_ok")
            wait(v, "gexp_ok", 1)
            c.done(v.tensor_tensor(gates[:], gates[:], selm[:], ALU.mult), "v_step")
            c.done(v.tensor_reduce(den[:], e3(gates), AX_X, ALU.add), "v_step")
            c.done(v.reciprocal(den[:], den[:]), "v_step")
            c.done(v.tensor_tensor(e3(gates), e3(gates), c3(den[:].unsqueeze(2)), ALU.mult), "v_step")
            c.done(v.memset(posm[:], 0.0), "v_step")
            wait(v, "p_pos", 1)
            for t in range(NTT):
                n = TN[t]
                cols = slice(E_N * t, E_N * (t + 1))
                c.done(v.scalar_tensor_tensor(out=posm[0:n, cols], in0=bank[5][0:n, cols], scalar=1.0, in1=selm[0:n, cols], op0=ALU.add, op1=ALU.mult), "v_step")
            c.done(v.tensor_scalar(posm[:], posm[:], -1.0, None, ALU.add), "v_step")
            c.done(v.tensor_reduce(cnt[0:1, 0:1], bank[6][0:1, 0:E_N], AX_X, ALU.max), "v_step")
            for k in range(4):
                c.done(v.tensor_scalar(cgt[0:1, k:k + 1], cnt[0:1, 0:1], float(CAP * (k + 1)), None, ALU.is_gt), "v_step")
            c.done(v.tensor_reduce(cnt[0:1, 1:2], cgt[0:1, :], AX_X, ALU.add), "v_step")
            c.done(v.tensor_scalar(cnt[0:1, 1:2], cnt[0:1, 1:2], 1.0, None, ALU.add), "v_step")
            c.done(v.tensor_copy(rnd[:], cnt[0:1, 1:2]), "rnd_ok")
            v.memset(S, 0.0).then_inc(sems["S_ok"], 1)
            v.memset(yr, 0.0).then_inc(sems["yb_ok"], 1)
            v.memset(den[:], 1.0).then_inc(sems["sc_ok"], 1)
            c.done(v.memset(gu, 0.0), "p_S")
            rounds = v.value_load(rnd[0:1, 0:1], min_val=1, max_val=5)

            def pick_gu(e):
                v.tensor_copy(sel_gu, bc(ident[:, bass.ds(e * 4, 4)].unsqueeze(2), P, 4, CAP)).then_inc(sems["sel_ok"], 1)

            def pick_dn(e):
                v.tensor_copy(sel_dn, bc(ident[:, bass.ds(e * 2, 2)].unsqueeze(2), P, 2, CAP)).then_inc(sems["sel_ok"], 1)

            def swiglu(i, q):
                at = q + 1
                v.wait_ge(sems["p_up"], i * 2 + at)
                v.tensor_scalar(gu[:, 0], bank[0][:], 7.0, None, ALU.min).then_inc(sems["gu_ok"], 1)
                v.tensor_scalar(gu[:, 1], bank[1][:], 7.0, -7.0, ALU.min, ALU.max).then_inc(sems["gu_cl"], 1)
                v.wait_ge(sems["gu_ok"], i * 2 + at)
                v.wait_ge(sems["gu_cl"], i * 2 + at)
                v.scalar_tensor_tensor(out=gu[:, 1], in0=gu[:, 1], scalar=1.0, in1=gu[:, 0], op0=ALU.add, op1=ALU.mult).then_inc(sems["ta_ok"], 1)
                v.wait_ge(sems["ta_ok"], i * 2 + at)
                v.wait_ge(sems["sig_ok"], i * 2 + at)
                v.tensor_tensor(gu[:, 1], gu[:, 1], sg, ALU.mult).then_inc(sems["act_ok"], 1)
                e = i % PAIRS * 2 + q
                pick_dn(e)
                pick_gu(e + 1 if q == 0 else (i + 1) % PAIRS * 2)

            def gain(w):
                for at in range(6):
                    t, j = at // 2, at % 2
                    v.wait_ge(sems["p_sc"], w * 6 + (at + 1))
                    d = x2[0:TN[t], t, 512 * j:512 * (j + 1)]
                    v.tensor_tensor(d, d, bank[6 + at % 2][0:TN[t], :], ALU.add).then_inc(sems["sc_ok"], 1)

            pos3 = posm[:].rearrange("p (t e) -> p t e", t=3)
            gat3 = gates[:].rearrange("p (t e) -> p t e", t=3)
            two = lambda ap: ap.rearrange("p (q c) -> p q c", q=2)
            def gates_of(p):
                v.tensor_copy(pp[:], pos3[:, :, bass.ds(p * 2, 2)]).then_inc(sems["pp_ok"], 1)
                v.tensor_copy(gp2[:], gat3[:, :, bass.ds(p * 2, 2)]).then_inc(sems["pp_ok"], 1)
                return v.tensor_scalar(pos3[:, :, bass.ds(p * 2, 2)], pos3[:, :, bass.ds(p * 2, 2)], float(CAP), None, ALU.subtract)

            def token_rows(gcount, pcount):
                v.wait_ge(sems["pp_ok"], pcount)
                for t in range(NTT):
                    n = TN[t]
                    last = v.tensor_tensor(two(G[0:n, t, :]), bc(slots_io[0:n].unsqueeze(1), n, 2, CAP), bc(pp[0:n, t, :].unsqueeze(2), n, 2, CAP), ALU.is_equal)
                last.then_inc(sems["G_ok"], 1)
                v.wait_ge(sems["G_ok"], gcount)
                for t in range(NTT):
                    n = TN[t]
                    last = v.tensor_tensor(two(GG[0:n, t, :]), two(G[0:n, t, :]), bc(gp2[0:n, t, :].unsqueeze(2), n, 2, CAP), ALU.mult)
                last.then_inc(sems["G_ok"], 1)

            wait(v, "tri_ok", 2)
            v.memset(b_dn[2 * E_N:P], 0.0)
            pick_gu(0)
            gates_of(0).then_inc(sems["pp_ok"], 1)
            token_rows(1, 3)
            with v.Fori(0, rounds * PAIRS) as i:
                swiglu(i, 0)
                gain(i)
                v.wait_ge(sems["p_S"], i + 2)
                gates_of((i + 1) % PAIRS).then_inc(sems["pp_ok"], 1)
                token_rows(i * 2 + 3, i * 3 + 6)
                swiglu(i, 1)
            total = rounds * PAIRS
            gain(total)
            v.wait_ge(sems["sc_ok"], total * 6 + 7)
            wait(v, "ss3_ok", 3)
            c.done(v.tensor_scalar(rst[:], ss[:], 1.0 / D, EPS, ALU.mult, ALU.add), "rs3_in")
            wait(v, "rs3_ok", 1)
            wait(v, "ld_fin", 16)
            for t in range(NTT):
                n = TN[t]
                c.tick(v.scalar_tensor_tensor(out=x2[0:n, t, :], in0=x2[0:n, t, :], scalar=rst[0:n, t:t + 1], in1=wbc[0:n], op0=ALU.mult, op1=ALU.mult), "y_fin")

        @block.scalar
        def _(act):
            c = Count(act)
            wait(act, "ld_x", 32)
            wait(act, "v_step", 2)
            for t in range(NTT):
                n = TN[t]
                c.done(act.activation(ot[0:n, t, :], xt[0:n, t, :], ACT.Square, accum_out=ss[0:n, t:t + 1]), "ss_ok")

            def land(at, n_mm=1):
                wait(act, "p_proj", at + 1)
                return bank[at % 4]

            b = land(0)
            c.done(act.copy(sm[:], b[0:80, 0:T]), "proj_ok")
            wait(act, "gate_x", 1)
            c.done(act.activation(gtmp[0:4, 1, :], gtmp[0:4, 1, :], ACT.Exp, scale=-1.0), "gate_e")
            c.done(act.activation(gtmp[32:36, 0, :], sm[32:36, :], ACT.Exp, scale=-1.0), "gate_e")
            c.done(act.activation(gate2[:, 2:3], gate2[:, 0:1], ACT.Exp), "gate_e")
            c.done(act.activation(gtmp[0:4, 1, :], gtmp[0:4, 1, :], ACT.Ln, bias=1.0), "gate_l")
            for u in range(3):
                raw, ce = raws[u % 2], ces[u % 2]
                wait(act, "conv_ok", u - 1)
                wait(act, "cs_ok", u - 1)
                for n in range(4):
                    at = 1 + 4 * u + n
                    b = land(at)
                    act.copy(raw[:, n, HEAD:HEAD + SEQ], b[:, 0:SEQ])
                    c.tick(act.copy(samples(raw[:, n, HEAD + SEQ:RAW])[:, :, HEAD:], samples(b[:, SEQ:T])), "proj_ok")
                wait(act, "conv_lin", u + 1)
                wait(act, "cs_ok", u + 1)
                c.tick(act.activation(raw[:, :, 0:CW], ce[:, :, 0:CW], ACT.Sigmoid), "conv_sig")
            for n in range(4):
                at = 13 + n
                b = land(at)
                c.tick(act.mul(gqk[:, n, :], b[:, 0:T], 0.125 if n < 2 else 1.0), "proj_ok")
            wait(act, "gt_ok", 3)
            c.done(act.activation(eg[:], gt[:, :, 0:4], ACT.Exp), "gt_exp")
            c.done(act.activation(ekd[:], gt[:, :, 64:68], ACT.Exp), "gt_exp")
            wait(act, "gk_x", 1)
            c.done(act.activation(gQ, gQ, ACT.Exp, scale=-1.0), "gk_e")
            c.done(act.activation(gQ, gQ, ACT.Ln, bias=1.0), "gk_l")
            wait(act, "p_convt", 9)
            for n in range(4):
                at = 17 + n
                b = land(at)
                c.tick(act.copy(convT[:, n, :], b[:, 0:T]), "proj_ok")
            wait(act, "conv_ok", 3)
            wait(act, "cs_ok", 3)
            for t in range(NTT):
                n = TN[t]
                for j in range(3):
                    at = 3 * t + j
                    wait(act, "p_qkT", at + 1)
                    dst = (KQ[:, 0], KQ[:, 1], kbT)[j][:, :, TO[t]:TO[t] + n]
                    c.tick(act.copy(dst, bank[4 + at % 4][:, 0:H * n].rearrange("p (h i) -> p h i", h=H)), "qkT_ok")
            for t in range(NTT):
                wait(act, "di_ok", t + 1)
                c.tick(act.activation(Dtt[t], Dtt[t], ACT.Exp), "dexp_ok")
            wait(act, "di_ok", 4)
            c.tick(act.activation(egl[:], egl[:], ACT.Exp), "dexp_ok")
            wait(act, "out_done", 32)
            for k, (l, t) in enumerate(INV):
                n = TN[t]
                wait(act, "p_y", k + 1)
                c.tick(act.copy(Yt[t], bank[INV_BANKS[t][0]][0:n, 0:H * n].rearrange("p (h i) -> p h i", h=H)), "y_ok")
                for x in gate_tiles[k]:
                    wait(act, "p_proj", 22 + x)
                    wait(act, "zg_ok", x - 3)
                    b = bank[0]
                    act.copy(zg[:, x, :], b[:, 0:T])
                    c.tick(act.activation(ce_z[:, x % 4, :], b[:, 0:T], ACT.Sigmoid), "proj_ok")
                if 3 <= k < 3 + LEVELS:
                    n = T if k - 3 < 2 else SEQ
                    wait(act, "g_abs", k - 2)
                    c.tick(act.activation(gE[:, :, 0:n], gE[:, :, 0:n], ACT.Exp), "g_exp")
                if k == 3 + LEVELS:
                    wait(act, "g_lvl", LEVELS)
                    c.tick(act.activation(gE, bT, ACT.Exp), "ebl_ok")
                    act.copy(ebl[:, :, 0:2], bT[:, :, P - 1:SEQ:P])
                    c.done(act.copy(ebl[:, :, 2:10], bT[:, :, SEQ + NS - 1:T:NS]), "gt_exp")
                    c.done(act.activation(ebl[:], ebl[:], ACT.Exp), "ebl_ok")
                if k == 5 + LEVELS:
                    wait(act, "g_abs", LEVELS + 2)
                    c.tick(act.activation(gE, gE, ACT.Exp), "ebl_ok")
            wait(act, "p_smp", 1)
            c.done(act.copy(skT[:].rearrange("p a b -> p (a b)"), bank[7][:, 0:256]), "smk_ok")
            wait(act, "p_gkd", 1)
            for t in range(NTT):
                n = TN[t]
                c.tick(act.copy(kdg[0:n, t, :], bank[t][0:n, 0:256]), "kdg_ok")
            wait(act, "p_gs", 1)
            for r in range(2):
                c.tick(act.copy(skT[:, r, 0:64], bank[r][:, 0:64]), "gsT_ok")
            for n in range(8):
                at = 29 + n
                b = land(at)
                c.tick(act.copy(hT[:, n, :], b[:, 0:T]), "proj_ok")

            for t in range(NTT):
                n = TN[t]
                wait(act, "x2_ok", 2 * t + 2)
                c.tick(act.activation(zf[0:n, 0:D], x2[0:n, t, :], ACT.Square, accum_out=ss[0:n, t:t + 1]), "ss2_ok")
                wait(act, "ss2_ok", t + 1)
            for k in range(KT):
                wait(act, "p_xnT", k + 1)
                c.tick(act.copy(hT[:, k, :], bank[k % 4][:, 0:T]), "xnT_ok")
            wait(act, "lg_ok", 4)
            c.tick(act.activation(gates[:], gates[:], ACT.Exp), "gexp_ok")
            wait(act, "rnd_ok", 1)
            rounds = act.value_load(rnd[0:1, 0:1], min_val=1, max_val=5)

            def rows_in(j, value):
                act.wait_ge(sems["p_gat"], value)
                act.copy(xeT[:, 4 * j:4 * j + 4, :].rearrange("p a b -> p (a b)"), bank[4 + j][:]).then_inc(sems["xe_ok"], 1)

            def activation(w):
                act.wait_ge(sems["gu_ok"], w)
                act.activation(sg, gu[:, 0], ACT.Sigmoid, scale=1.702).then_inc(sems["sig_ok"], 1)
                act.wait_ge(sems["p_at"], w)
                act.copy(aT.rearrange("p a b -> p (a b)"), bank[2][:]).then_inc(sems["aT_ok"], 1)

            def rows_out(q, w):
                act.wait_ge(sems["p_yd"], w)
                for h in range(2):
                    act.copy(yr[CAP * q:CAP * (q + 1), 512 * h:512 * (h + 1)], bank[3][CAP * h:CAP * (h + 1), :]).then_inc(sems["yb_ok"], 1)

            rows_in(0, 1)
            rows_in(1, 2)
            with act.Fori(0, rounds * PAIRS) as i:
                activation(i * 2 + 1)
                act.wait_ge(sems["p_sc"], i * 6 + 6)
                act.wait_ge(sems["p_S"], i + 2)
                act.copy(S, bank[4][:, 0:T]).then_inc(sems["S_ok"], 1)
                rows_out(0, i * 2 + 1)
                activation(i * 2 + 2)
                rows_in(0, i * 2 + 3)
                rows_in(1, i * 2 + 4)
                rows_out(1, i * 2 + 2)
            act.wait_ge(sems["sc_ok"], rounds * (PAIRS * 6) + 7)
            for t in range(NTT):
                n = TN[t]
                c.tick(act.activation(zf[0:n, 0:D], x2[0:n, t, :], ACT.Square, accum_out=ss[0:n, t:t + 1]), "ss3_ok")
                wait(act, "ss3_ok", t + 1)

_INS = ["x_prompt", "x_sample", "state_gdn_conv", "state_gdn", "state_gla", "rms_mix_w", "w_in", "conv_w",
        "gdn_a_log", "gdn_dt_bias", "gdn_norm_w", "gla_gk_w", "gla_gk_b", "gla_norm_w", "w_out", "rms_ffn_w",
        "w_router", "b_router", "w_up", "b_up", "w_down", "b_down", "rms_final_w"]
_OUTS = [(1, 256, 1024), (8, 4, 1024), (1, 1, 3, 1536), (1, 1, 4, 128, 128), (1, 1, 4, 64, 128),
         (1, 8, 3, 1536), (1, 8, 4, 128, 128), (1, 8, 4, 64, 128)]


def kernel(**inputs):
    import numpy as _np
    import concourse.bacc as _bacc
    from concourse import mybir as _mybir
    from concourse.bass_utils import run_bass_kernel_spmd as _run

    nc = _bacc.Bacc("TRN2", target_bir_lowering=False, num_devices=1)
    arrays, args = {}, {}
    for name in _INS:
        x = _np.ascontiguousarray(inputs[name])
        arrays[f"in_{name}"] = x
        args[name] = nc.dram_tensor(f"in_{name}", x.shape, _mybir.dt.from_np(x.dtype), kind="ExternalInput").ap()
    outs = [nc.dram_tensor(f"out_{i}", s, _mybir.dt.float32, kind="ExternalOutput").ap() for i, s in enumerate(_OUTS)]
    program(nc, args, outs)
    r = _run(nc, [arrays], core_ids=[0])
    return tuple(r.results[0][f"out_{i}"] for i in range(len(_OUTS)))
```

```python
from contextlib import ExitStack

import concourse.bass as bass
from concourse import mybir

P = 128
F32 = mybir.dt.float32
I32 = mybir.dt.int32
ALU = mybir.AluOpType
ACT = mybir.ActivationFunctionType
AX_X = mybir.AxisListType.X

D = 1024
KT = D // P
SEQ, NB, NS = 256, 8, 4
SMP = NB * NS
T = SEQ + SMP
NTT = 3
TN = [P, P, SMP]
TO = [0, P, 2 * P]
H = 4
QK = 512
CH = 3 * QK
HEAD = 3
RAW = HEAD + SEQ + NB * (HEAD + NS)
CW = RAW - HEAD
LEVELS = 7
E_N, TOPK, FF = 32, 4, 1024
CAP = 64
PAIRS = E_N // 2
EPS = 1e-6
NEG = -3.0e38
C_Z, C_A, C_B = 1536, 2048, 2052
C_GQ, C_GV, C_GG, C_LR = 2056, 2568, 3080, 3592


def program(nc, a, o):
    ctx = ExitStack()
    with ctx:
        def sb(name, shape, dt=F32):
            return ctx.enter_context(nc.sbuf_tensor(name, shape, dt))

        def sem(name):
            return ctx.enter_context(nc.semaphore(name))

        bank = [ctx.enter_context(nc.psum_tensor(f"bank{i}", [P, 512], F32)) for i in range(8)]

        def cut(base, at, *shape):
            n = 1
            for s in shape:
                n *= s
            v = base[:, at:at + n]
            if len(shape) == 2:
                v = v.rearrange("p (a b) -> p a b", a=shape[0])
            if len(shape) == 3:
                v = v.rearrange("p (a b c) -> p a b c", a=shape[0], b=shape[1])
            return v

        UNIT = 4096
        ring = sb("ring", [P, 6 * UNIT])
        slot = [ring[:, i * UNIT:(i + 1) * UNIT] for i in range(6)]
        sgs = cut(ring, 0, NB, H, P)
        S3 = 3 * UNIT
        KQ = cut(ring, S3, 2, H, T)
        kbT = cut(ring, S3 + 2304, H, T)
        nM = cut(ring, S3 + 3456, 2 * H, P)
        nMs = cut(ring, S3 + 4480, H, SMP)
        AT = cut(ring, S3 + 4608, 2 * H, P)
        ATs = cut(ring, S3 + 5632, H, SMP)
        U = cut(ring, S3 + 5760, 2 * H, P)
        Us = cut(ring, S3 + 6784, H, SMP)
        Ti = cut(ring, S3 + 6912, 2 * H, P)
        Tis = cut(ring, S3 + 7936, H, SMP)
        Y = cut(ring, S3 + 8064, 2 * H, P)
        Ys = cut(ring, S3 + 9088, H, SMP)
        Dt = cut(ring, S3 + 9216, 2 * H, P)
        Dts = cut(ring, S3 + 10240, H, SMP)
        gE = cut(ring, S3 + 10368, 2, T)
        gQ = cut(ring, S3 + 10944, 2, T)
        gK = cut(ring, S3 + 11520, 2, T)
        kbs = [ring[:, at:at + QK] for at in (S3 + 3456, S3 + 4608, S3 + 5120)]
        crow = ring[:, S3 + 8064:S3 + 8064 + CH]
        gdiag = cut(ring, S3 + 6912, H, T)
        kdm = cut(ring, S3 + 9216, NB, P)

        qksq = ring[:, S3 + 8 * RAW:S3 + 8 * RAW + D]
        osqs = [ring[:, at:at + D] for at in (S3 + 8064, S3 + 6912)]
        skT = sb("skT", [P, 2, P])
        sqT = sb("sqT", [P, 2, 64])
        qs = sb("qs", [P, 2, SMP])
        xb = sb("xb", [P, 3 * D])
        xt = cut(xb, 0, 3, D)
        gqk = cut(xb, 0, 4, T)
        kdg = cut(xb, 0, 3, 256)
        vg = cut(xb, 1152, 3, 512)
        ob = sb("ob", [P, 3 * D])
        raws = [cut(ob, 0, 4, RAW), cut(ring, S3, 4, RAW)]
        ces = [cut(ob, 4 * RAW, 4, RAW), cut(ring, S3 + 4 * RAW, 4, RAW)]
        ce_z = cut(ob, 1260, 4, T)
        ot = cut(ob, 0, 3, D)
        hist = ob[0:27, 0:D]
        xeT = cut(xb, 0, KT, P)
        yr = xb[:, D:2 * D]
        gu = cut(xb, 2 * D, 2, 512)
        hT = sb("hT", [P, KT, T])
        hTf = hT[:].rearrange("p a b -> p (a b)")
        b_gu = hTf[:, 0:512]
        b_dn = hTf[:, 512:1024]
        sel_gu = cut(hTf, 1024, 4, CAP)
        sel_dn = cut(hTf, 1280, 2, CAP)
        zg = sb("zg", [P, KT, T])
        zf = zg[:].rearrange("p a b -> p (a b)")
        aT = cut(zf, 0, 4, P)
        sg = cut(zf, 512, 512)
        G = cut(zf, 1280, 3, P)
        GG = cut(zf, 1664, 3, P)
        convf = sb("convT", [P, 4 * T])
        convT = cut(convf, 0, 4, T)
        AG = cut(convf, 0, 2 * H, P)
        AGs = cut(convf, 2 * H * P, H, SMP)
        wbc = convf[:, 0:D]
        qf = sb("qkv", [P, 3 * CH])
        qkv = cut(qf, 0, 3, CH)
        x2 = cut(qf, 0, 3, D)
        kgm = cut(qf, 3 * D, NB, P)
        vn = qkv[:, :, 0:QK]
        ident = sb("ident", [P, P])
        ones = sb("ones", [P, P])
        upi = sb("upi", [P, P])
        upis = sb("upis", [SMP, SMP])
        mu = sb("mu", [P, LEVELS, P], I32)
        mlf = sb("ml", [P, LEVELS * P])
        ml = cut(mlf[:].bitcast(I32), 0, LEVELS, P)
        mone = sb("mone", [P, P], I32)
        seqm = sb("seqm", [SMP, NB])
        resets = sb("resets", [P, T])
        sgp = sb("sgp", [P, H, P])
        sls = sb("sls", [P, 2, NB, P])
        slp = sb("slp", [P, 2, P])
        bTf = sb("bT", [P, 2 * T])
        bT = cut(bTf, 0, 2, T)
        S = bTf[:, 0:T]
        lg = mlf[:, 0:96]
        m8 = sb("m8", [P, 3, 8])
        gts = mlf[:, 96:192]
        eqs = mlf[:, 192:288]
        pre = mlf[:, 288:384]
        selm = mlf[:, 384:480]
        gates = mlf[:, 480:576]
        posm = mlf[:, 576:672]
        r32 = mlf[:, 672:768]
        ndd = sb("ndd", [P, 3])
        den = sb("den", [P, 3])
        tri = sb("tri", [P, P])
        cnt = sb("cnt", [1, 2])
        cgt = sb("cgt", [1, 4])
        rnd = sb("rnd", [1, 1], I32)
        slots_io = sb("slots_io", [P, CAP])
        pp = sb("pp", [P, 3, 2])
        gp2 = sb("gp2", [P, 3, 2])
        wsmf = sb("wsm", [P, KT * 80])
        wsm = cut(wsmf, 0, KT, 80)
        wr = cut(wsmf, 0, KT, E_N)
        brt = wsmf[:, KT * E_N:KT * E_N + E_N]
        sm = sb("sm", [80, T])
        gb = sb("gb", [68, T])
        gtmp = sb("gtmp", [36, 2, T])
        hist_rest = sb("hist_rest", [P, QK])
        gt = sb("gt", [P, 3, 68])
        eg = sb("eg", [P, 3, H])
        ekd = sb("ekd", [P, 3, H])
        nbeg = sb("nbeg", [P, 3, H])
        egl = sb("egl", [P, H, 10])
        gate2 = sb("gate2", [4, 3])
        vrow = sb("vrow", [60, P])
        vecT = sb("vecT", [P, 60])
        gkw = sb("gkw", [80, 256])
        cT = sb("cT", [P, 12, 24])
        cs = sb("cs", [P, 12, 27])
        ss = sb("ss", [P, 3])
        rst = sb("rst", [P, 3])
        ss8 = sb("ss8", [P, 24])
        rs8 = sb("rs8", [P, 24])
        mhalf = sb("mhalf", [P, 24])
        ebl = sb("ebl", [P, 2, 10])

        names = """ld_x ld_vec ld_gate ld_cst ld_sm ld_bias ld_st ld_router w_in1 w_in2
            ident_ok masks_ok v_step ss_ok rst_in rst_ok h_ok p_vec vec_ok p_hT
            hT_ok p_cT cT_ok p_at p_proj proj_ok conv_lin conv_sig conv_ok
            cs_ok p_convt convt_ok p_gk gk_x gk_e gk_l bT_ok gate_x gate_e
            gate_l gb_ok p_gt gt_ok gt_exp p_gi di_ok dexp_ok d_ok ss8_ok
            rs8_ok qkn_ok p_qkT qkT_ok p_MA MA_ok p_y y_ok p_inv inv_ok
            p_tm p_ch ch_ok vd_ok p_smp g_abs g_exp g_lvl p_glvl p_low ag_ok
            ebl_ok zg_ok smk_ok smr_ok p_gkd kdg_ok p_gch gch_ok p_gs gsT_ok
            p_o0 p_gag og_ok slp_ok qs_e qs_ok sq_ok qksq_ok
            osq_ok o_ok p_oT oT_ok w_out w_out2 x_again p_x2 x2_ok xw_ok p_xnT
            xnT_ok p_lgT lgT_ok p_lg route_ok ss2_ok rs2_in xn_ok p_pos kdm_ok dec_ok p_up_s
            st_ok p_rows rows_ok hist_out out_done ld_ffn ld_fin lg_ok tri_ok rnd_ok G_ok
            p_gat p_up p_yd p_sc p_S w_used gu_ok act_ok
            yb_ok sc_ok xe_ok sel_ok S_ok sig_ok ld_w0 ld_w1 ld_w2 ld_w3
            ld_w4 ld_w5 st_out st_out2 pp_ok bz_ok pad_ok gexp_ok gu_cl ta_ok
            aT_ok ss3_ok rs3_in rs3_ok y_fin""".split()
        WSLOT = [3, 4, 2, 1, 5, 0]
        INV = [(l, t) for l in range(1, LEVELS) for t in ((0, 1, 2) if l == 1 else (0, 1))]
        FILL = [1 if k < 10 else 2 for k in range(len(INV))]
        HALVES = [sum(FILL[:k]) for k in range(len(INV) + 1)]
        gate_tiles = [range(HALVES[k] // 2, HALVES[k + 1] // 2) for k in range(len(INV))]
        INV_BANKS = ((2, 3), (4, 5), (6, 6))
        inv_at = {(0, t): t + 1 for t in range(3)} | {x: 4 + i for i, x in enumerate(INV)}
        NMt = [nM[:, 0:H], nM[:, H:2 * H], nMs[0:SMP]]
        Att = [AT[:, 0:H], AT[:, H:2 * H], ATs[0:SMP]]
        Ut = [U[:, 0:H], U[:, H:2 * H], Us[0:SMP]]
        Tt = [Ti[:, 0:H], Ti[:, H:2 * H], Tis[0:SMP]]
        Yt = [Y[:, 0:H], Y[:, H:2 * H], Ys[0:SMP]]
        Dtt = [Dt[:, 0:H], Dt[:, H:2 * H], Dts[0:SMP]]
        AGt = [AG[:, 0:H], AG[:, H:2 * H], AGs[0:SMP]]
        LAST_BANKS = (6, 7, 0, 1, 2, 3)
        sems = {n: sem(n) for n in names}
        block = ctx.enter_context(nc.Block())

        class Count:

            def __init__(self, eng):
                self.eng, self.n = eng, {}

            def tick(self, ins, name):
                ins.then_inc(sems[name], 1)
                self.n[name] = self.n.get(name, 0) + 1

            def done(self, ins, name):
                self.tick(ins, name)
                self.eng.wait_ge(sems[name], self.n[name])

        def wait(eng, name, value):
            if value > 0:
                eng.wait_ge(sems[name], value)

        def bc(ap, *shape):
            return ap.broadcast_to(list(shape))

        def samples(ap):
            return ap.rearrange("p (b j) -> p b j", b=NB)

        @block.sync
        def _(sp):
            sp.dma_start(xt[:, 0:2, :], a["x_prompt"].rearrange("a (t p) d -> p (a t) d", p=P)).then_inc(sems["ld_x"], 16)
            sp.dma_start(xt[0:SMP, 2, :], a["x_sample"].rearrange("b s d -> (b s) d")).then_inc(sems["ld_x"], 16)
            rows = [(a["rms_mix_w"].rearrange("l (k p) -> (l k) p", p=P), 0, 8),
                    (a["conv_w"].rearrange("l i (c p) -> (l i c) p", p=P), 8, 48),
                    (a["gla_gk_b"].rearrange("l (j p) -> (l j) p", p=P), 56, 2),
                    (a["gdn_norm_w"], 58, 1), (a["gla_norm_w"], 59, 1)]
            for src, at, n in rows:
                sp.dma_start(vrow[at:at + n, :], src).then_inc(sems["ld_vec"], 16)
            w_in = a["w_in"].rearrange("l (k p) n -> p (l k) n", p=P)
            sp.dma_start(wsm[:, :, 0:4], w_in[:, :, C_A:C_A + 4]).then_inc(sems["ld_sm"], 16)
            sp.dma_start(wsm[:, :, 32:36], w_in[:, :, C_B:C_B + 4]).then_inc(sems["ld_sm"], 16)
            sp.dma_start(wsm[:, :, 64:80], w_in[:, :, C_LR:C_LR + 16]).then_inc(sems["ld_sm"], 16)
            units = [0, 512, 1024, C_GQ, C_GV, C_Z, C_GG]
            for u in range(7):
                if u >= 2:
                    sp.wait_ge(sems["p_proj"], 1 + 4 * (u - 1))
                dst = slot[1 + u % 2].rearrange("p (k n) -> p k n", k=KT)
                sp.dma_start(dst, w_in[:, :, units[u]:units[u] + 512]).then_inc(sems[f"w_in{1 + u % 2}"], 16)
                if u == 1:
                    sp.dma_start(crow[0:24, :], a["state_gdn_conv"].rearrange("l b r c -> (l b r) c")).then_inc(sems["ld_cst"], 16)
                    sp.dma_start(gate2[:, 0:1], a["gdn_a_log"].rearrange("l h -> h l")).then_inc(sems["ld_gate"], 16)
                    sp.dma_start(gate2[:, 1:2], a["gdn_dt_bias"].rearrange("l h -> h l")).then_inc(sems["ld_gate"], 16)
                    sp.dma_start(gkw[64:80, :], a["gla_gk_w"][0]).then_inc(sems["ld_gate"], 16)
                    for h in range(H):
                        sp.dma_start(sgs[:, :, h, :], a["state_gdn"][0, :, h].rearrange("b k v -> k b v")).then_inc(sems["ld_st"], 16)
                    for h in range(H):
                        r = 64 * (h % 2)
                        sp.dma_start(sls[r:r + 64, h // 2, :, :], a["state_gla"][0, :, h].rearrange("b k v -> k b v")).then_inc(sems["ld_st"], 16)

            w_o = a["w_out"].rearrange("l (k p) n -> p (l k) n", p=P)
            for u in range(2):
                sp.wait_ge(sems["p_proj"], (25, 29)[u])
                dst = slot[2 - u].rearrange("p (k n) -> p k n", k=KT)
                sp.dma_start(dst, w_o[:, :, 512 * u:512 * (u + 1)]).then_inc(sems[("w_out", "w_out2")[u]], 16)

            sp.wait_ge(sems["p_gs"], 2)
            sp.dma_start(wbc, a["rms_ffn_w"].partition_broadcast(P).rearrange("q l d -> q (l d)")).then_inc(sems["ld_ffn"], 16)
            sp.dma_start(wr, a["w_router"].rearrange("l (k p) e -> p (l k) e", p=P)).then_inc(sems["ld_router"], 16)
            sp.dma_start(brt, a["b_router"].partition_broadcast(P).rearrange("q l d -> q (l d)")).then_inc(sems["ld_router"], 16)
            sp.wait_ge(sems["ch_ok"], 6)
            sp.dma_start(x2[:, 0:2, :], a["x_prompt"].rearrange("a (t p) d -> p (a t) d", p=P)).then_inc(sems["x_again"], 16)
            sp.dma_start(x2[0:SMP, 2, :], a["x_sample"].rearrange("b s d -> (b s) d")).then_inc(sems["x_again"], 16)

            up = a["w_up"][0].rearrange("e (p k) n -> e p (k n)", p=P)
            dn = a["w_down"][0].rearrange("e (k p) n -> e p k n", p=P)

            def load_unit(e, u):
                dst = slot[WSLOT[u]]
                if u < 4:
                    src = up[e, :, UNIT * u:UNIT * (u + 1)]
                else:
                    dst = dst.rearrange("p (k n) -> p k n", k=4)
                    src = dn[e, :, 4 * (u - 4):4 * (u - 4) + 4, :]
                sp.dma_start(dst, src).then_inc(sems[f"ld_w{u}"], 16)

            sp.wait_ge(sems["osq_ok"], 3)
            sp.wait_ge(sems["p_oT"], 1)
            load_unit(0, 0)
            load_unit(0, 1)
            sp.wait_ge(sems["p_proj"], 33)
            load_unit(0, 2)
            sp.wait_ge(sems["p_proj"], 37)
            load_unit(0, 3)
            sp.wait_ge(sems["p_up_s"], 4)
            load_unit(0, 4)
            sp.wait_ge(sems["out_done"], 16 * 2)
            load_unit(0, 5)
            sp.wait_ge(sems["p_lg"], 1)
            sp.dma_start(b_gu, a["b_up"].rearrange("l e (j n) -> (l e j) n", n=512)).then_inc(sems["ld_bias"], 16)
            sp.dma_start(b_dn[0:2 * E_N], a["b_down"].rearrange("l e (j n) -> (l e j) n", n=512)).then_inc(sems["ld_bias"], 16)
            sp.wait_ge(sems["xn_ok"], 3)
            sp.dma_start(wbc, a["rms_final_w"].partition_broadcast(P)).then_inc(sems["ld_fin"], 16)
            sp.wait_ge(sems["rnd_ok"], 1)
            rounds = sp.value_load(rnd[0:1, 0:1], min_val=1, max_val=5)
            with sp.Fori(1, rounds * E_N) as m:
                e = m % E_N
                for u, (name, value) in enumerate([("w_used", m * 4 - 3), ("w_used", m * 4 - 2), ("w_used", m * 4 - 1),
                                                   ("p_up", m), ("w_used", m * 4), ("p_yd", m)]):
                    sp.wait_ge(sems[name], value)
                    load_unit(e, u)
            for t in range(NTT):
                sp.wait_ge(sems["y_fin"], t + 1)
                dst = o[0][0, P * t:P * (t + 1), :] if t < 2 else o[1].rearrange("b s d -> (b s) d")
                sp.dma_start(dst, x2[0:TN[t], t, :]).then_inc(sems["st_out"], 16)
            sp.wait_ge(sems["st_out"], 48)

        @block.gpsimd
        def _(g):
            c = Count(g)
            g.memset(ident[:], 0.0)
            c.done(g.memset(ones[:], 1.0), "ident_ok")
            c.done(g.affine_select(out=ident[:], in_=ident[:], compare_op=ALU.not_equal, fill=1.0, base=0,
                                   pattern=[[-1, P]], channel_multiplier=1), "ident_ok")
            g.wait_ge(sems["rst_in"], 2)
            c.done(g.tensor_tensor(rst[:], rst[:], mhalf[:, 0:3], ALU.pow), "rst_ok")
            c.done(g.affine_select(out=upi[:], in_=ones[:], compare_op=ALU.is_ge, fill=0.0, base=0,
                                   pattern=[[1, P]], channel_multiplier=-1), "masks_ok")
            us = upis[:].rearrange("p (b s) -> p b s", b=NB)
            c.done(g.affine_select(out=us, in_=upi[0:SMP, 0:SMP].rearrange("p (b s) -> p b s", b=NB),
                                   compare_op=ALU.is_ge, fill=0.0, base=0, pattern=[[-NS, NB], [0, NS]],
                                   channel_multiplier=1), "masks_ok")
            c.done(g.affine_select(out=seqm[:], in_=ones[0:SMP, 0:NB], compare_op=ALU.is_ge, fill=0.0, base=0,
                                   pattern=[[-NS, NB]], channel_multiplier=1), "masks_ok")
            c.done(g.affine_select(out=seqm[:], in_=seqm[:], compare_op=ALU.is_ge, fill=0.0, base=NS - 1,
                                   pattern=[[NS, NB]], channel_multiplier=-1), "masks_ok")
            g.memset(mu[:], 0)
            c.done(g.memset(ml, 0), "masks_ok")
            for l in range(LEVELS):
                w, nb = 1 << l, P >> (l + 1)
                for m, lo, hi in ((mu, w, 2 * w), (ml, 0, w)):
                    v = m[:, l, :].rearrange("p (b r) -> p b r", b=nb)[:, :, lo:hi]
                    c.done(g.memset(v, 1), "masks_ok")
                    other = 0 if m is mu else w
                    c.done(g.affine_select(out=v, in_=v, compare_op=ALU.is_ge, fill=0.0, base=-other,
                                           pattern=[[-2 * w, nb], [0, w]], channel_multiplier=1), "masks_ok")
                    c.done(g.affine_select(out=v, in_=v, compare_op=ALU.is_ge, fill=0.0, base=other + w - 1,
                                           pattern=[[2 * w, nb], [0, w]], channel_multiplier=-1), "masks_ok")
            c.done(g.tensor_copy(mone[:], ident[:]), "masks_ok")
            for u in range(3):
                g.wait_ge(sems["proj_ok"], 1 + 4 * (u + 1))
                d, raw = cs[:, 4 * u:4 * u + 4, :], raws[u % 2]
                g.tensor_copy(d[:, :, 0:3], raw[:, :, SEQ:SEQ + 3])
                for n in range(4):
                    r = samples(raw[:, n, HEAD + SEQ:RAW])
                    i = g.tensor_copy(samples(d[:, n, 3:27]), r[:, :, NS:NS + HEAD])
                c.done(i, "cs_ok")
            g.wait_ge(sems["ss8_ok"], 1)
            c.done(g.tensor_tensor(rs8[:], ss8[:], mhalf[:], ALU.pow), "rs8_ok")

            g.wait_ge(sems["rows_ok"], 6)
            for dst, at in ((o[2][0, 0], slice(0, 3)), (o[5].rearrange("l b r c -> (l b r) c"), slice(3, 27))):
                g.dma_start(dst[:, 0:D], hist[at]).then_inc(sems["hist_out"], 16)
                g.dma_start(dst[:, D:CH], hist_rest[at]).then_inc(sems["hist_out"], 16)

            c.done(g.tensor_tensor(tri[:], upi[:], ident[:], ALU.subtract), "tri_ok")
            c.done(g.iota(slots_io[:], pattern=[[1, CAP]], base=0, channel_multiplier=0,
                          allow_small_or_imprecise_dtypes=True), "tri_ok")

            def seq_rows(h):
                if h < 4:
                    dst, src = kdm, qkv[0:SMP, 2, QK + h * P:QK + (h + 1) * P]
                else:
                    dst, src = kgm, kdg[0:SMP, 2, (h - 4) * P:(h - 3) * P]
                c.tick(g.tensor_tensor(dst[0:SMP], bc(src.unsqueeze(1), SMP, NB, P), bc(seqm[:].unsqueeze(2), SMP, NB, P), ALU.mult), "kdm_ok")

            g.wait_ge(sems["p_smp"], 1)
            for h in range(4):
                c.tick(g.tensor_tensor(sgs[:, :, h, :], sgs[:, :, h, :], bc(egl[:, h, 2:10].unsqueeze(2), P, NB, P), ALU.mult), "dec_ok")
            seq_rows(0)
            g.wait_ge(sems["p_gs"], 1)
            g.wait_ge(sems["ebl_ok"], 2)
            for h in range(4, 6):
                st = sls[:, h - 4]
                c.tick(g.tensor_tensor(st, st, bc(ebl[:, h - 4, 2:10].unsqueeze(2), P, NB, P), ALU.mult), "dec_ok")
            for t in range(NTT):
                g.wait_ge(sems["osq_ok"], t + 1)
                e8 = slice(8 * t, 8 * t + 8)
                c.done(g.tensor_tensor(rs8[:, e8], ss8[:, e8], mhalf[:, e8], ALU.pow), "rs8_ok")
            for h in range(1, 5):
                g.wait_ge(sems["p_up_s"], h)
                seq_rows(h)
            g.memset(S, 0.0).then_inc(sems["S_ok"], 1)
            g.memset(yr, 0.0).then_inc(sems["yb_ok"], 1)
            g.wait_ge(sems["ch_ok"], 5)
            g.wait_ge(sems["st_ok"], 4)
            g.dma_start(o[3][0, 0].rearrange("h k v -> k h v"), sgp[:]).then_inc(sems["out_done"], 16)
            g.dma_start(o[6][0].rearrange("b h k v -> k (b h) v"), ring[:, 0:UNIT].rearrange("p (a v) -> p a v", v=P)).then_inc(sems["out_done"], 16)
            g.wait_ge(sems["ss2_ok"], 3)
            g.wait_ge(sems["rs2_in"], 1)
            c.done(g.tensor_tensor(rst[:], rst[:], mhalf[:, 0:3], ALU.pow), "rst_ok")
            for at, n in ((SMP, 32), (64, 64)):
                g.memset(G[at:at + n, 2, :], 0.0)
                g.memset(ot[at:at + n, 2, :], 0.0).then_inc(sems["pad_ok"], 1)
            g.wait_ge(sems["p_lg"], 1)
            c.tick(g.memset(b_dn[2 * E_N:P], 0.0), "bz_ok")
            g.wait_ge(sems["p_up_s"], 5)
            seq_rows(5)
            g.wait_ge(sems["gch_ok"], 2)
            for r in range(2):
                g.dma_start(o[4][0, 0].rearrange("(j r) k v -> r k j v", r=2)[r], slp[64 * r:64 * r + 64]).then_inc(sems["st_out2"], 16)
            g.wait_ge(sems["st_ok"], 6)
            for h in range(H):
                r = 64 * (h % 2)
                g.dma_start(o[7][0, :, h].rearrange("b k v -> k b v"), sls[r:r + 64, h // 2, :, :]).then_inc(sems["st_out2"], 16)
            for t in range(NTT):
                g.wait_ge(sems["rs3_in"], t + 1)
                c.done(g.tensor_tensor(rst[:, t:t + 1], rst[:, t:t + 1], mhalf[:, t:t + 1], ALU.pow), "rs3_ok")
            g.wait_ge(sems["hist_out"], 16 * 4)
            g.wait_ge(sems["out_done"], 16 * 2)
            g.wait_ge(sems["st_out2"], 16 * 6)

        @block.tensor
        def _(pe):
            c = Count(pe)

            def turn(out, src, n):
                return pe.transpose(out, src, ident[0:n, 0:n])

            pe.wait_ge(sems["ident_ok"], 2)
            pe.wait_ge(sems["ld_vec"], 80)
            c.tick(turn(bank[7][:, 0:60], vrow[:], 60), "p_vec")
            pe.wait_ge(sems["h_ok"], 3)
            for k in range(KT):
                wait(pe, "hT_ok", k - 3)
                for t in range(NTT):
                    i = turn(bank[k % 4][:, TO[t]:TO[t] + TN[t]], xt[0:TN[t], t, k * P:(k + 1) * P], TN[t])
                c.tick(i, "p_hT")
            def g_sums(t):
                n = TN[t]
                b = bank[(7, 4, 5)[t]]
                i = pe.matmul(b[0:n, 0:H * n], ones[0:4, 0:n], gdiag[0:4, :, TO[t]:TO[t] + n], start=True, stop=True)
                if t == 2:
                    pe.matmul(b[:, P:P + 8], ones[0:4, :], gdiag[0:4, :, P - 1:SEQ:P], start=True, stop=True)
                    i = pe.matmul(b[:, P + 8:P + 40], ones[0:4, :], gdiag[0:4, :, SEQ + NS - 1:T:NS], start=True, stop=True)
                c.tick(i, "p_gi")

            def rows_t(t):
                n = TN[t]
                pe.wait_ge(sems["qkn_ok"], 3 * t + 2)
                for j in range(3):
                    at = 3 * t + j
                    wait(pe, "qkT_ok", at - 3)
                    src = qkv[0:n, t, (QK, 0)[j]:(QK, 0)[j] + QK] if j < 2 else kbs[t][0:n, :]
                    for h in range(H):
                        i = turn(bank[4 + at % 4][:, h * n:(h + 1) * n], src[:, h * P:(h + 1) * P], n)
                    c.tick(i, "p_qkT")

            def project(u):
                pe.wait_ge(sems[f"w_in{1 + u % 2}"], 16 * (u // 2 + 1))
                w = slot[1 + u % 2].rearrange("p (k n) -> p k n", k=KT)
                for n in range(4):
                    if u == 4 and n == 0:
                        g_sums(0)
                        g_sums(1)
                    if u == 4 and n == 1:
                        pe.wait_ge(sems["gk_x"], 1)
                        g_sums(2)
                    if u == 4 and n == 2:
                        pe.wait_ge(sems["di_ok"], 4)
                        rows_t(0)
                    if u == 4 and n == 3:
                        rows_t(1)
                        rows_t(2)
                    at = 1 + 4 * u + n
                    wait(pe, "proj_ok", at - 3)
                    for k in range(KT):
                        i = pe.matmul(bank[at % 4][:, 0:T], w[:, k, n * P:(n + 1) * P], hT[:, k, :],
                                      start=k == 0, stop=k == KT - 1)
                    c.tick(i, "p_proj")

            def conv_rows(u):
                pe.wait_ge(sems["conv_ok"], u + 1)
                for t in range(NTT):
                    at = 3 * u + t
                    wait(pe, "convt_ok", at - 2)
                    for n in range(4):
                        i = turn(bank[4 + at % 3][0:TN[t], n * P:(n + 1) * P],
                                 convT[:, n, TO[t]:TO[t] + TN[t]], P)
                    c.tick(i, "p_convt")

            pe.wait_ge(sems["hT_ok"], 8)
            pe.wait_ge(sems["ld_sm"], 48)
            pe.wait_ge(sems["v_step"], 1)
            for k in range(KT):
                i = pe.matmul(bank[0][0:80, 0:T], wsm[:, k, :], hT[:, k, :], start=k == 0, stop=k == KT - 1)
            c.tick(i, "p_proj")
            project(0)
            pe.wait_ge(sems["ld_cst"], 16)
            for n in range(12):
                i = turn(bank[4][:, 24 * n:24 * n + 24], crow[0:24, n * P:(n + 1) * P], 24)
            c.tick(i, "p_cT")
            project(1)
            pe.wait_ge(sems["cT_ok"], 1)
            conv_rows(0)
            project(2)
            pe.wait_ge(sems["gb_ok"], 1)
            for t in range(NTT):
                i = turn(bank[7][0:TN[t], 68 * t:68 * t + 68], gb[:, TO[t]:TO[t] + TN[t]], 68)
            c.tick(i, "p_gt")
            conv_rows(1)
            project(3)
            conv_rows(2)
            pe.wait_ge(sems["ld_gate"], 48)
            pe.wait_ge(sems["convt_ok"], 9)
            for j in range(2):
                i = pe.matmul(bank[5 + j][:, 0:T], gkw[64:80, j * P:(j + 1) * P], sm[64:80, :], start=True, stop=True)
            c.tick(i, "p_gk")
            project(4)
            pe.wait_ge(sems["qkT_ok"], 9)
            for t in range(NTT):
                n = TN[t]
                if t == 2:
                    pe.wait_ge(sems["proj_ok"], 21)
                tok = slice(TO[t], TO[t] + n)
                for j in range(2):
                    b = bank[(4, 5, 6, 7, 0, 1)[2 * t + j]]
                    for h in range(H):
                        i = pe.matmul(b[0:n, h * n:(h + 1) * n], KQ[:, 0, h, tok],
                                      (kbT[:, h, tok], KQ[:, 1, h, tok])[j], start=True, stop=True)
                    c.tick(i, "p_MA")
            def gdn_sample(b, h0):
                if b == 0 and h0 == 0:
                    pe.wait_ge(sems["ld_st"], 128)
                    pe.wait_ge(sems["ag_ok"], 3)
                for h in range(h0, h0 + 2):
                    ov = bank[1][:, 64 * h:64 * h + 64].rearrange("p (a i) -> p a i", a=2)[:, :, NS * b:NS * (b + 1)]
                    i = pe.matmul(ov, sgs[:, b, h, :], KQ[:, :, h, SEQ + NS * b:SEQ + NS * (b + 1)], start=True, stop=True)
                if b == NB - 1 and h0 == 2:
                    c.tick(i, "p_smp")

            def gla_sample(r, b):
                if b == 0 and r == 0:
                    pe.wait_ge(sems["qs_ok"], 1)
                    pe.wait_ge(sems["smk_ok"], 1)
                if b == 0 and r == 1:
                    pe.wait_ge(sems["p_low"], 4)
                for j in range(2):
                    at = 64 * r + 32 * j + NS * b
                    i = pe.matmul(bank[1][:, at:at + NS], sls[64 * r:64 * r + 64, j, b, :],
                                  qs[64 * r:64 * r + 64, j, NS * b:NS * (b + 1)], start=True, stop=True)
                if b == NB - 1:
                    c.tick(i, "p_low" if r == 0 else "p_gs")

            def gate_half(x):
                u, n, at = 5 + x // 8, x // 2 % 4, 21 + x // 2
                if x % 2 == 0:
                    pe.wait_ge(sems[f"w_in{1 + u % 2}"], 16 * (u // 2 + 1))
                    pe.wait_ge(sems["proj_ok"], at)
                w = slot[1 + u % 2].rearrange("p (k n) -> p k n", k=KT)
                for k in range(4 * (x % 2), 4 * (x % 2) + 4):
                    i = pe.matmul(bank[0][:, 0:T], w[:, k, n * P:(n + 1) * P], hT[:, k, :],
                                  start=k == 0, stop=k == KT - 1)
                    if k == KT - 1:
                        c.tick(i, "p_proj")
                    if 6 <= x < 10:
                        gdn_sample(2 * (x - 6) + k % 4 // 2, 2 * (k % 2))
                    if 10 <= x < 14:
                        gla_sample((x - 10) // 2, 4 * (x % 2) + k % 4)

            def gla_level(k):
                gq, gk = (gqk[:, 0:2, :], gqk[:, 2:4, :]) if k == 0 else (gQ, gK)
                wait(pe, "g_lvl", k)
                wait(pe, "ag_ok", k)
                for r in range(2):
                    rows_ = slice(64 * r, 64 * r + 64)
                    for t in range(2):
                        for j in range(2):
                            m = 2 * t + j
                            i = pe.matmul(bank[6 + r][:, m * P:(m + 1) * P], gk[rows_, j, TO[t]:TO[t] + P],
                                          gq[rows_, j, TO[t]:TO[t] + P], start=True, stop=True)
                if k < 3:
                    for r in range(2):
                        rows_ = slice(64 * r, 64 * r + 64)
                        for j in range(2):
                            i = pe.matmul(bank[1][0:SMP, (2 * j + r) * SMP:(2 * j + r + 1) * SMP], gk[rows_, j, SEQ:T],
                                          gq[rows_, j, SEQ:T], start=True, stop=True)
                        if r == 0:
                            c.done(i, "p_low")
                c.tick(i, "p_glvl")

            pe.wait_ge(sems["cs_ok"], 3)
            for at in range(6):
                wait(pe, "rows_ok", at - 1)
                for n in range(4):
                    if at < 3:
                        i = turn(bank[2 + at % 2][0:TN[at], n * P:(n + 1) * P], convT[:, n, TO[at]:TO[at] + TN[at]], P)
                    else:
                        i = turn(bank[2 + at % 2][0:27, n * P:(n + 1) * P], cs[:, 4 * (at - 3) + n, :], P)
                c.tick(i, "p_rows")
            pe.wait_ge(sems["rows_ok"], 5)
            for t in range(NTT):
                n = TN[t]
                pe.wait_ge(sems["MA_ok"], 2 * t + 1)
                for h in range(H):
                    i = turn(bank[INV_BANKS[t][0]][0:n, h * n:(h + 1) * n], NMt[t][:, h, :], n)
                c.tick(i, "p_tm")
            pe.wait_ge(sems["MA_ok"], 6)
            for k, (l, t) in enumerate(INV):
                n = TN[t]
                by, bu = INV_BANKS[t]
                bt, uo = by, H * n if bu == by else 0
                pe.wait_ge(sems["inv_ok"], inv_at[l - 1, t])
                for h in range(H):
                    i = pe.matmul(bank[by][0:n, h * n:(h + 1) * n], NMt[t][:, h, :], Tt[t][:, h, :], start=True, stop=True)
                c.tick(i, "p_y")
                for x in range(HALVES[k], HALVES[k + 1]):
                    gate_half(x)
                pe.wait_ge(sems["y_ok"], k + 1)
                if l < LEVELS - 1:
                    for h in range(H):
                        pe.matmul(bank[bt][0:n, h * n:(h + 1) * n], Ut[t][:, h, :], Yt[t][:, h, :], start=True, stop=True)
                for h in range(H):
                    i = pe.matmul(bank[bu][0:n, uo + h * n:uo + (h + 1) * n], Yt[t][:, h, :], Ut[t][:, h, :], start=True, stop=True)
                c.tick(i, "p_inv")
                if k == 3:
                    pe.wait_ge(sems["inv_ok"], inv_at[1, 2])
                if 3 <= k <= LEVELS + 3:
                    gla_level(k - 3)
            vr = lambda t, h: qkv[0:TN[t], t, 2 * QK + h * P:2 * QK + (h + 1) * P]
            kr = lambda t, h: qkv[0:TN[t], t, QK + h * P:QK + (h + 1) * P]
            nr = lambda t, h: vn[0:TN[t], t, h * P:(h + 1) * P]

            def heads(b, lhs, rhs, name, n=P):
                for h in range(H):
                    i = pe.matmul(b[0:n, h * P:(h + 1) * P], lhs(h), rhs(h), start=True, stop=True)
                if name:
                    c.tick(i, name)

            vgr = lambda t, h: vg[0:TN[t], t, h * P:(h + 1) * P]

            def gla_state(t):
                for h in range(H):
                    r = 64 * (h % 2)
                    i = pe.matmul(bank[4][r:r + 64, (h // 2) * P:(h // 2) * P + P], kdg[:, t, 64 * h:64 * h + 64],
                                  vgr(t, h), start=True, stop=True)
                c.tick(i, "p_gch")

            pe.wait_ge(sems["inv_ok"], 3 + len(INV))
            pe.wait_ge(sems["vd_ok"], 3)
            pe.wait_ge(sems["proj_ok"], 29)
            heads(bank[0], lambda h: Ut[0][:, h, :], lambda h: vr(0, h), "p_ch")
            pe.wait_ge(sems["g_lvl"], LEVELS + 1)
            pe.wait_ge(sems["ag_ok"], LEVELS + 1)
            for t in range(NTT):
                for j in range(2):
                    at = (0, 256, 0)[t] + j * P
                    i = turn(bank[(4, 4, 7)[t]][0:TN[t], at:at + P], gK[:, j, TO[t]:TO[t] + TN[t]], P)
            c.tick(i, "p_gkd")
            pe.wait_ge(sems["ch_ok"], 1)
            pe.wait_ge(sems["gsT_ok"], 1)
            heads(bank[1], lambda h: kr(0, h), lambda h: nr(0, h), "p_ch")
            heads(bank[5], lambda h: Att[0][:, h, :], lambda h: nr(0, h), "p_o0")
            pe.wait_ge(sems["rows_ok"], 6)
            heads(bank[6], lambda h: AGt[0][:, h, :], lambda h: vgr(0, h), "p_gag")
            pe.wait_ge(sems["ch_ok"], 2)
            heads(bank[2], lambda h: KQ[:, 0, h, P:SEQ], lambda h: sgp[:, h, :], None)
            heads(bank[3], lambda h: KQ[:, 1, h, P:SEQ], lambda h: sgp[:, h, :], "p_ch")
            pe.wait_ge(sems["kdg_ok"], 3)
            gla_state(0)
            heads(bank[7], lambda h: AGt[1][:, h, :], lambda h: vgr(1, h), "p_gag")
            pe.wait_ge(sems["ch_ok"], 3)
            heads(bank[0], lambda h: Ut[1][:, h, :], lambda h: vr(1, h), "p_ch")
            for j in range(2):
                pe.wait_ge(sems["og_ok"], 2 + j)
                for h in range(H):
                    i = turn(bank[6 + j][0:SMP, h * P:(h + 1) * P], skT[:].rearrange("p a b -> p (a b)")[:, 64 * h + 32 * j:64 * h + 32 * j + 32], P)
            c.tick(i, "p_smp")
            pe.wait_ge(sems["ch_ok"], 4)
            heads(bank[1], lambda h: kr(1, h), lambda h: nr(1, h), "p_ch")
            heads(bank[5], lambda h: Att[1][:, h, :], lambda h: nr(1, h), "p_ch")
            pe.wait_ge(sems["slp_ok"], 1)
            for h in range(H):
                r = 64 * (h % 2)
                i = pe.matmul(bank[2 + h % 2][:, (h // 2) * P:(h // 2) * P + P], gQ[r:r + 64, h // 2, P:SEQ],
                              slp[r:r + 64, h // 2, :], start=True, stop=True)
            c.tick(i, "p_gch")
            gla_state(1)
            pe.wait_ge(sems["smr_ok"], 1)
            heads(bank[6], lambda h: Ut[2][:, h, :], lambda h: vr(2, h), "p_smp", SMP)
            for h in range(H):
                i = turn(bank[7][0:SMP, h * P:(h + 1) * P], sqT[:, h % 2, 32 * (h // 2):32 * (h // 2) + 32], P)
            heads(bank[0], lambda h: AGt[2][:, h, :], lambda h: vgr(2, h), "p_gs", SMP)
            pe.wait_ge(sems["smr_ok"], 2)
            heads(bank[6], lambda h: Att[2][:, h, :], lambda h: nr(2, h), "p_smp", SMP)
            for t in range(NTT):
                n = TN[t]
                pe.wait_ge(sems["o_ok"], t + 1)
                for j in range(2):
                    at = 2 * t + j
                    wait(pe, "oT_ok", at - 1)
                    for h in range(H):
                        i = turn(bank[3 + 2 * (at % 2)][:, h * n:(h + 1) * n], ot[0:n, t, (4 * j + h) * P:(4 * j + h + 1) * P], n)
                    c.tick(i, "p_oT")
            def state_update(h):
                pe.wait_ge(sems["kdm_ok"], h + 1)
                b0 = (4, 6, 4, 6, 2, 0)[h]
                if h < 4:
                    wait(pe, "st_ok", h - 1)
                for b in range(NB):
                    out_b = bank[b0 + b // 4]
                    cols = slice((b % 4) * P, (b % 4) * P + P)
                    if h < 4:
                        i = pe.matmul(out_b[:, cols], kdm[0:SMP, b, :], vn[0:SMP, 2, h * P:(h + 1) * P], start=True, stop=True)
                    else:
                        for r in range(2):
                            hh = 2 * (h - 4) + r
                            i = pe.matmul(out_b[64 * r:64 * r + 64, cols], kgm[0:SMP, b, 64 * r:64 * r + 64],
                                          vg[0:SMP, 2, hh * P:(hh + 1) * P], start=True, stop=True)
                c.tick(i, "p_up_s")

            def mix_rows(j):
                pe.wait_ge(sems["proj_ok"], 33 + 4 * j)
                for t in range(NTT):
                    at = 3 * j + t
                    wait(pe, "x2_ok", at - 1)
                    for n in range(4):
                        i = turn(bank[4 + at % 2][0:TN[t], n * P:(n + 1) * P], hT[:, 4 * j + n, TO[t]:TO[t] + TN[t]], P)
                    c.tick(i, "p_x2")

            pe.wait_ge(sems["oT_ok"], 6)
            for u in range(2):
                pe.wait_ge(sems[("w_out", "w_out2")[u]], 16)
                w = slot[2 - u].rearrange("p (k n) -> p k n", k=KT)
                for n in range(4):
                    at = 29 + 4 * u + n
                    wait(pe, "proj_ok", at - 3)
                    for k in range(KT):
                        i = pe.matmul(bank[at % 4][:, 0:T], w[:, k, n * P:(n + 1) * P], zg[:, k, :],
                                      start=k == 0, stop=k == KT - 1)
                    c.tick(i, "p_proj")
                    if 4 * u + n < 4:
                        state_update(4 * u + n)
                    else:
                        pe.wait_ge(sems["st_ok"], 4)
                        if 4 * u + n == 6:
                            mix_rows(0)
            mix_rows(1)

            for k in range(KT):
                pe.wait_ge(sems["xw_ok"], 3 if k < 4 else 6)
                wait(pe, "xnT_ok", k - 3)
                for t in range(NTT):
                    i = turn(bank[k % 4][:, TO[t]:TO[t] + TN[t]], ot[0:TN[t], t, k * P:(k + 1) * P], TN[t])
                c.tick(i, "p_xnT")
                if k % 4 == 3:
                    pe.wait_ge(sems["ld_router"], 32)
                    for m in range(k - 3, k + 1):
                        pe.wait_ge(sems["xnT_ok"], m + 1)
                        i = pe.matmul(bank[6][0:E_N, 0:T], wr[:, m, :], hT[:, m, :], start=m == 0, stop=m == KT - 1)
            c.tick(i, "p_lgT")
            pe.wait_ge(sems["lgT_ok"], 1)
            for t in range(NTT):
                i = turn(bank[4][0:TN[t], E_N * t:E_N * (t + 1)], sm[0:E_N, TO[t]:TO[t] + TN[t]], E_N)
            c.tick(i, "p_lg")
            state_update(4)
            pe.wait_ge(sems["route_ok"], 1)
            pe.wait_ge(sems["tri_ok"], 2)
            sel = lambda t: selm[0:TN[t], E_N * t:E_N * (t + 1)]
            for t in range(NTT):
                for t2 in range(t + 1):
                    lhs = ones[0:TN[t2], 0:TN[t]] if t2 < t else tri[0:TN[t], 0:TN[t]]
                    pe.matmul(bank[5][0:TN[t], E_N * t:E_N * (t + 1)], lhs, sel(t2), start=t2 == 0, stop=t2 == t)
            for t in range(NTT):
                i = pe.matmul(bank[6][0:32, 0:E_N], ones[0:TN[t], 0:32], sel(t), start=t == 0, stop=t == NTT - 1)
            c.tick(i, "p_pos")
            state_update(5)

            def scatter(w, ats, banks=(6, 7, 6, 7, 6, 7)):
                for at in ats:
                    t, j = at // 2, at % 2
                    if banks[at] in banks[:at] or at < 2:
                        pe.wait_ge(sems["sc_ok"], w * 6 + max(at, 1))
                    pe.matmul(bank[banks[at]][0:TN[t], :], S[:, TO[t]:TO[t] + TN[t]], yr[:, 512 * j:512 * (j + 1)],
                              start=True, stop=True).then_inc(sems["p_sc"], 1)

            def start(b, row_of, bias):
                for h in range(2):
                    pe.matmul(bank[b][CAP * h:CAP * (h + 1), :], row_of[:, h, :], bias, start=True, stop=False, skip_group_check=True)

            def up(i, q):
                pe.wait_ge(sems["sel_ok"], i * 4 + (2 * q + 1))
                for g in range(2):
                    start(g, sel_gu[:, 2 * g:2 * g + 2, :], b_gu)
                for u in range(4):
                    pe.wait_ge(sems[f"ld_w{u}"], i * 32 + 16 * (q + 1))
                    w = slot[WSLOT[u]].rearrange("p (k g h n) -> p k g h n", k=2, g=2, h=2)
                    for kk in range(2):
                        k = 2 * u + kk
                        for g in range(2):
                            for h in range(2):
                                last = pe.matmul(bank[g][CAP * h:CAP * (h + 1), :], xeT[:, k, q * CAP:(q + 1) * CAP], w[:, kk, g, h, :],
                                                 start=False, stop=k == KT - 1, skip_group_check=True)
                    last.then_inc(sems["w_used" if u < 3 else "p_up"], 1)

            def act_t(w):
                pe.wait_ge(sems["act_ok"], w)
                for j in range(4):
                    last = turn(bank[2][:, j * P:(j + 1) * P], gu[:, 1, j * P:(j + 1) * P], P)
                last.then_inc(sems["p_at"], 1)

            def down(i, q):
                pe.wait_ge(sems["sel_ok"], i * 4 + (2 * q + 3))
                start(3, sel_dn, b_dn)
                for u in range(4, 6):
                    pe.wait_ge(sems[f"ld_w{u}"], i * 32 + 16 * (q + 1))
                    w = slot[WSLOT[u]].rearrange("p (k h n) -> p k h n", k=4, h=2)
                    for k in range(4):
                        for h in range(2):
                            last = pe.matmul(bank[3][CAP * h:CAP * (h + 1), :], aT[:, k, CAP * (u - 4):CAP * (u - 3)], w[:, k, h, :],
                                             start=False, stop=u == 5 and k == 3, skip_group_check=True)
                    last.then_inc(sems["w_used" if u < 5 else "p_yd"], 1)

            def gather(j):
                for n in range(4):
                    for t in range(NTT):
                        lhs = ot[:, t, :].rearrange("p (m k) -> p k m", k=KT)[:, 4 * j + n, :]
                        last = pe.matmul(bank[4 + j][:, n * P:(n + 1) * P], lhs, G[:, t, :], start=t == 0, stop=t == NTT - 1)
                last.then_inc(sems["p_gat"], 1)

            pe.wait_ge(sems["G_ok"], 1)
            pe.wait_ge(sems["xn_ok"], 3)
            pe.wait_ge(sems["pad_ok"], 2)
            gather(0)
            gather(1)
            pe.wait_ge(sems["ld_bias"], 32)
            pe.wait_ge(sems["bz_ok"], 1)
            pe.wait_ge(sems["st_ok"], 6)
            pe.wait_ge(sems["rnd_ok"], 1)
            rounds = pe.value_load(rnd[0:1, 0:1], min_val=1, max_val=5)
            with pe.Fori(0, rounds * PAIRS) as i:
                pe.wait_ge(sems["xe_ok"], i * 2 + 2)
                up(i, 0)
                pe.wait_ge(sems["G_ok"], i * 2 + 2)
                for t in range(NTT):
                    last = turn(bank[4][:, TO[t]:TO[t] + TN[t]], GG[0:TN[t], t, :], TN[t])
                last.then_inc(sems["p_S"], 1)
                pe.wait_ge(sems["yb_ok"], i * 4 + 1)
                scatter(i, range(2))
                act_t(i * 2 + 1)
                scatter(i, range(2, 6))
                pe.wait_ge(sems["aT_ok"], i * 2 + 1)
                down(i, 0)
                up(i, 1)
                pe.wait_ge(sems["S_ok"], i + 2)
                pe.wait_ge(sems["G_ok"], i * 2 + 3)
                gather(0)
                act_t(i * 2 + 2)
                gather(1)
                pe.wait_ge(sems["aT_ok"], i * 2 + 2)
                pe.wait_ge(sems["yb_ok"], i * 4 + 3)
                down(i, 1)
            total = rounds * PAIRS
            pe.wait_ge(sems["S_ok"], total + 1)
            pe.wait_ge(sems["yb_ok"], total * 4 + 1)
            scatter(total, range(6), LAST_BANKS)

        @block.vector
        def _(v):
            c = Count(v)
            v.memset(wsm[:, :, 4:32], 0.0)
            c.done(v.memset(wsm[:, :, 36:64], 0.0), "v_step")
            v.memset(ss[:], 1.0)
            v.memset(ss8[:], 1.0)
            v.memset(mhalf[:], -0.5)
            v.memset(gb[:], 0.0)
            v.memset(resets[:], 1.0)
            c.done(v.memset(gt[:], 0.0), "v_step")
            c.done(v.memset(resets[:, 0:SEQ:P], 0.0), "v_step")
            c.done(v.memset(resets[:, SEQ:T:NS], 0.0), "v_step")
            c.done(v.memset(rst[:], 1.0), "rst_in")
            v.wait_ge(sems["ss_ok"], 3)
            c.done(v.tensor_scalar(rst[:], ss[:], 1.0 / D, EPS, ALU.mult, ALU.add), "rst_in")
            v.wait_ge(sems["rst_ok"], 1)
            for t in range(NTT):
                n = TN[t]
                c.done(v.tensor_scalar(xt[0:n, t, :], xt[0:n, t, :], rst[0:n, t:t + 1], None, ALU.mult), "h_ok")
            v.wait_ge(sems["p_vec"], 1)
            c.done(v.tensor_copy(vecT[:], bank[7][:, 0:60]), "vec_ok")
            for k in range(KT):
                v.wait_ge(sems["p_hT"], k + 1)
                c.done(v.tensor_scalar(hT[:, k, :], bank[k % 4][:, 0:T], vecT[:, k:k + 1], None, ALU.mult), "hT_ok")
            v.wait_ge(sems["proj_ok"], 1)
            v.wait_ge(sems["ld_gate"], 48)
            c.done(v.tensor_scalar(gtmp[0:4, 0, :], sm[0:4, :], gate2[:, 1:2], None, ALU.add), "v_step")
            c.tick(v.scalar_tensor_tensor(out=gtmp[0:4, 1, :], in0=gtmp[0:4, 0, :], scalar=-1.0, in1=gtmp[0:4, 0, :],
                                          op0=ALU.mult, op1=ALU.max), "gate_x")

            def conv(u):
                v.wait_ge(sems["proj_ok"], 1 + 4 * (u + 1))
                old = cT[:, 4 * u:4 * u + 4, :]
                raw, ce = raws[u % 2], ces[u % 2]
                c.done(v.memset(raw[:, :, 0:HEAD], 0.0), "v_step")
                for n in range(4):
                    c.done(v.tensor_copy(samples(raw[:, n, HEAD + SEQ:RAW])[:, :, 0:HEAD], samples(old[:, n, :])), "v_step")
                for i in range(4):
                    for n in range(4):
                        w = vecT[:, 8 + 12 * i + 4 * u + n:9 + 12 * i + 4 * u + n]
                        if i == 0:
                            c.done(v.tensor_scalar(ce[:, n, 0:CW], raw[:, n, 0:CW], w, None, ALU.mult), "v_step")
                        else:
                            tap = v.scalar_tensor_tensor(out=ce[:, n, 0:CW], in0=raw[:, n, i:i + CW], scalar=w,
                                                         in1=ce[:, n, 0:CW], op0=ALU.mult, op1=ALU.add)
                            if i == 3 and n == 3:
                                c.done(tap, "conv_lin")
                            else:
                                c.done(tap, "v_step")
                v.wait_ge(sems["conv_sig"], u + 1)
                e = raw[:, :, 0:CW]
                c.done(v.tensor_tensor(convT[:, :, 0:SEQ], ce[:, :, 0:SEQ], e[:, :, 0:SEQ], ALU.mult), "v_step")
                at = HEAD + SEQ
                for n in range(4):
                    r = lambda b: b[:, n, at:RAW].rearrange("p (b j) -> p b j", b=NB)[:, :, 0:NS]
                    i = v.tensor_tensor(convT[:, n, SEQ:T].rearrange("p (b j) -> p b j", b=NB), r(ce), r(raw), ALU.mult)
                c.done(i, "conv_ok")

            def rows(u):
                for t in range(NTT):
                    at = 3 * u + t
                    v.wait_ge(sems["p_convt"], at + 1)
                    dst = qkv[0:TN[t], t, QK * u:QK * (u + 1)]
                    c.done(v.tensor_copy(dst, bank[4 + at % 3][0:TN[t], :]), "convt_ok")

            v.wait_ge(sems["p_cT"], 1)
            c.done(v.tensor_copy(cT[:].rearrange("p a b -> p (a b)"), bank[4][:, 0:288]), "cT_ok")
            conv(0)
            v.wait_ge(sems["gate_e"], 3)
            v.wait_ge(sems["gate_l"], 1)
            g0 = gtmp[0:4, 0, :]
            c.done(v.tensor_scalar(g0, g0, 0.0, None, ALU.max), "v_step")
            c.done(v.tensor_tensor(g0, g0, gtmp[0:4, 1, :], ALU.add), "v_step")
            c.done(v.tensor_scalar(g0, g0, gate2[:, 2:3], -1.0, ALU.mult, ALU.mult), "v_step")
            c.done(v.tensor_tensor_scan(gb[0:4, :], resets[0:4, :], g0, 0.0, ALU.mult, ALU.add), "v_step")
            be = gtmp[32:36, 0, :]
            c.done(v.tensor_scalar(be, be, 1.0, None, ALU.add), "v_step")
            c.done(v.reciprocal(gb[32:36, :], be), "v_step")
            gp = gb[0:4, 0:SEQ].rearrange("p (c i) -> p c i", c=2)
            gs = gb[0:4, SEQ:T].rearrange("p (b j) -> p b j", b=NB)
            dp = gb[64:68, 0:SEQ].rearrange("p (c i) -> p c i", c=2)
            ds = gb[64:68, SEQ:T].rearrange("p (b j) -> p b j", b=NB)
            v.tensor_tensor(dp, bc(gp[:, :, P - 1:P], 4, 2, P), gp, ALU.subtract)
            v.tensor_tensor(ds, bc(gs[:, :, NS - 1:NS], 4, NB, NS), gs, ALU.subtract)
            c.done(v.tensor_tensor(gdiag[0:4], bc(gb[0:4, :].unsqueeze(1), 4, H, T),
                                   bc(ident[0:4, 0:4].unsqueeze(2), 4, H, T), ALU.mult), "gb_ok")
            rows(0)
            conv(1)
            v.wait_ge(sems["p_gt"], 1)
            for t in range(NTT):
                c.done(v.tensor_copy(gt[0:TN[t], t, :], bank[7][0:TN[t], 68 * t:68 * t + 68]), "gt_ok")
            rows(1)
            conv(2)
            v.wait_ge(sems["qksq_ok"], 3)
            c.done(v.tensor_scalar(ss8[:], ss8[:], EPS, None, ALU.add), "ss8_ok")
            rows(2)
            v.wait_ge(sems["p_gk"], 1)
            for j in range(2):
                c.done(v.tensor_scalar(gE[:, j, :], bank[5 + j][:, 0:T], vecT[:, 56 + j:57 + j], None, ALU.add), "v_step")
            c.tick(v.scalar_tensor_tensor(out=gQ, in0=gE, scalar=-1.0, in1=gE, op0=ALU.mult, op1=ALU.max), "gk_x")
            v.wait_ge(sems["rs8_ok"], 1)
            r8 = rs8[:].rearrange("p (t a) -> p t a", t=3)
            c.done(v.tensor_scalar(r8[:, :, 0:4], r8[:, :, 0:4], float(P) ** -0.5, None, ALU.mult), "v_step")

            def hd(ap):
                return ap.rearrange("p (a d) -> p a d", d=P)

            def g_diffs(t):
                n = TN[t]
                b = bank[(7, 4, 5)[t]]
                v.wait_ge(sems["p_gi"], t + 1)
                for h in range(H):
                    i = v.tensor_scalar(Dtt[t][:, h, :], b[0:n, h * n:(h + 1) * n], gt[0:n, t, h:h + 1], 0.0, ALU.subtract, ALU.min)
                c.done(i, "di_ok")
                if t == 2:
                    v.tensor_copy(egl[:, :, 0:2], b[:, P:P + 8].rearrange("p (h x) -> p h x", h=H))
                    c.done(v.tensor_copy(egl[:, :, 2:10], b[:, P + 8:P + 40].rearrange("p (h x) -> p h x", h=H)), "di_ok")

            v.wait_ge(sems["gt_exp"], 2)
            g_diffs(0)
            g_diffs(1)
            for t in range(NTT):
                if t == 1:
                    g_diffs(2)
                n = TN[t]
                q, k, vv = (hd(qkv[0:n, t, QK * j:QK * (j + 1)]) for j in range(3))
                beta = bc(gt[0:n, t, 32:36].unsqueeze(2), n, H, P)
                c.done(v.tensor_tensor(hd(qkv[0:n, t, 0:2 * QK]), hd(qkv[0:n, t, 0:2 * QK]), bc(r8[0:n, t, :].unsqueeze(2), n, 8, P), ALU.mult), "qkn_ok")
                c.done(v.tensor_tensor(hd(kbs[t][0:n, :]), k, beta, ALU.mult), "qkn_ok")
                c.done(v.tensor_tensor(vv, vv, beta, ALU.mult), "qkn_ok")
            c.done(v.tensor_tensor(nbeg[:], gt[:, :, 32:36], eg[:], ALU.mult), "v_step")
            c.done(v.tensor_scalar(nbeg[:], nbeg[:], -1.0, None, ALU.mult), "v_step")
            v.wait_ge(sems["dexp_ok"], 4)
            v.wait_ge(sems["masks_ok"], 48)
            for t in range(NTT):
                n = TN[t]
                m = upi[:] if t < 2 else upis[:]
                c.done(v.tensor_tensor(Dtt[t], Dtt[t], bc(m.unsqueeze(1), n, H, n), ALU.mult), "d_ok")
            for t in range(NTT):
                n = TN[t]
                for j in range(2):
                    v.wait_ge(sems["p_MA"], 2 * t + j + 1)
                    b = bank[(4, 5, 6, 7, 0, 1)[2 * t + j]][0:n, 0:H * n].rearrange("p (h i) -> p h i", h=H)
                    if j == 0:
                        c.done(v.scalar_tensor_tensor(out=NMt[t], in0=b, scalar=-1.0, in1=Dtt[t], op0=ALU.mult, op1=ALU.mult), "MA_ok")
                    else:
                        c.done(v.tensor_tensor(Att[t], b, Dtt[t], ALU.mult), "MA_ok")
            for t in range(NTT):
                n = TN[t]
                eye = bc(ident[0:n, 0:n].unsqueeze(1), n, H, n)
                v.tensor_copy(Ut[t], eye)
                c.done(v.tensor_copy(Tt[t], eye), "v_step")
                v.wait_ge(sems["p_tm"], t + 1)
                v.copy_predicated(Ut[t], bc(mu[0:n, 0, 0:n].unsqueeze(1), n, H, n), NMt[t])
                c.done(v.copy_predicated(Tt[t], bc(ml[0:n, 0, 0:n].unsqueeze(1), n, H, n),
                                         bank[INV_BANKS[t][0]][0:n, 0:H * n].rearrange("p (h i) -> p h i", h=H)), "inv_ok")
            v.wait_ge(sems["gk_l"], 1)
            c.done(v.tensor_scalar(gE, gE, 0.0, None, ALU.min), "v_step")
            c.done(v.tensor_tensor(gE, gE, gQ, ALU.subtract), "v_step")
            c.done(v.tensor_scalar(gE, gE, 1.0 / 16, None, ALU.mult), "v_step")
            for j in range(2):
                c.done(v.tensor_tensor_scan(bT[:, j, :], resets[:], gE[:, j, :], 0.0, ALU.mult, ALU.add), "bT_ok")
            for t in range(NTT):
                n = TN[t]
                k = hd(qkv[0:n, t, QK:2 * QK])
                c.done(v.tensor_tensor(k, k, bc(ekd[0:n, t, :].unsqueeze(2), n, H, P), ALU.mult), "vd_ok")
            v.wait_ge(sems["p_rows"], 3)
            v.memset(AG[:], 0.0)
            c.done(v.memset(AGs[:], 0.0), "v_step")

            def level(l):
                w = 1 << l
                n = T if l < 2 else SEQ
                b4 = bT[:, :, 0:n].rearrange("p j (b r) -> p j b r", r=2 * w)
                e4 = gE[:, :, 0:n].rearrange("p j (b r) -> p j b r", r=2 * w)
                nb = n // (2 * w)
                e = gE[:, :, 0:n]
                c.done(v.tensor_tensor(e4, b4, bc(b4[:, :, :, w - 1:w], P, 2, nb, 2 * w), ALU.subtract), "v_step")
                c.done(v.scalar_tensor_tensor(out=e, in0=e, scalar=-1.0, in1=e, op0=ALU.mult, op1=ALU.min), "g_abs")

            def decayed(l):
                n = T if l < 2 else SEQ
                e = gE[:, :, 0:n]
                v.wait_ge(sems["g_exp"], l + 1)
                v.tensor_tensor(gQ[:, :, 0:n], gqk[:, 0:2, 0:n], e, ALU.mult)
                c.done(v.tensor_tensor(gK[:, :, 0:n], gqk[:, 2:4, 0:n], e, ALU.mult), "g_lvl")

            def gather(k):
                v.wait_ge(sems["p_glvl"], k + 1)
                m = mone[:] if k == 0 else mu[:, k - 1, :]
                for r in range(2):
                    dst = AG[:].rearrange("p (q r) i -> p q r i", r=2)[:, :, r, :]
                    i = v.copy_predicated(dst, bc(m.unsqueeze(1), P, 4, P), bank[6 + r][:].rearrange("p (q i) -> p q i", q=4))
                if k < 3:
                    i = v.copy_predicated(AGs[0:SMP], bc(m[0:SMP, 0:SMP].unsqueeze(1), SMP, H, SMP),
                                          bank[1][0:SMP, 0:H * SMP].rearrange("p (q i) -> p q i", q=H))
                c.done(i, "ag_ok")

            for k, (l, t) in enumerate(INV):
                n = TN[t]
                bt, bu = INV_BANKS[t]
                uo = H * n if bu == bt else 0
                v.wait_ge(sems["p_inv"], k + 1)
                if l < LEVELS - 1:
                    v.copy_predicated(Tt[t], bc(ml[0:n, l, 0:n].unsqueeze(1), n, H, n), bank[bt][0:n, 0:H * n].rearrange("p (h i) -> p h i", h=H))
                c.done(v.copy_predicated(Ut[t], bc(mu[0:n, l, 0:n].unsqueeze(1), n, H, n),
                                         bank[bu][0:n, uo:uo + H * n].rearrange("p (h i) -> p h i", h=H)), "inv_ok")
                for x in gate_tiles[k]:
                    v.wait_ge(sems["proj_ok"], 22 + x)
                    c.done(v.tensor_tensor(zg[:, x, :], zg[:, x, :], ce_z[:, x % 4, :], ALU.mult), "zg_ok")
                if 3 <= k <= LEVELS + 3:
                    gather(k - 3)
                if 3 <= k < LEVELS + 3:
                    decayed(k - 3)
                if 2 <= k < LEVELS + 2:
                    level(k - 2)
                if k == 5:
                    v.wait_ge(sems["qs_e"], 1)
                    c.tick(v.tensor_tensor(qs[:], qs[:], gqk[:, 0:2, SEQ:T], ALU.mult), "qs_ok")
                if k == 4 + LEVELS:
                    v.wait_ge(sems["ebl_ok"], 2)
                    c.done(v.tensor_tensor(gQ, gqk[:, 0:2, :], gE, ALU.mult), "g_abs")
                    for j in range(2):
                        bp = bT[:, j, 0:SEQ].rearrange("p (c i) -> p c i", c=2)
                        bs = bT[:, j, SEQ:T].rearrange("p (b i) -> p b i", b=NB)
                        v.tensor_tensor(gE[:, j, 0:SEQ].rearrange("p (c i) -> p c i", c=2), bc(bp[:, :, P - 1:P], P, 2, P), bp, ALU.subtract)
                        i = v.tensor_tensor(gE[:, j, SEQ:T].rearrange("p (b i) -> p b i", b=NB), bc(bs[:, :, NS - 1:NS], P, NB, NS), bs, ALU.subtract)
                    c.done(i, "g_abs")
            v.wait_ge(sems["ebl_ok"], 3)
            c.done(v.tensor_tensor(gK, gqk[:, 2:4, :], gE, ALU.mult), "g_lvl")

            def col(ap, n):
                return bc(ap.unsqueeze(2), n, H, P)

            v.wait_ge(sems["p_ch"], 1)
            c.done(v.tensor_copy(vn[:, 0, :], bank[0][:]), "ch_ok")
            v.wait_ge(sems["p_ch"], 2)
            c.done(v.tensor_copy(sgp[:].rearrange("p h d -> p (h d)"), bank[1][:]), "ch_ok")
            v.wait_ge(sems["p_ch"], 3)
            tmp = hd(vn[:, 1, :])
            c.done(v.tensor_tensor(tmp, hd(bank[2][:]), col(nbeg[:, 1, :], P), ALU.mult), "v_step")
            vv = qkv[:, 1, 2 * QK:3 * QK]
            c.done(v.tensor_tensor(vv, vv, vn[:, 1, :], ALU.add), "ch_ok")
            o1 = ot[:, 1, 0:QK]
            c.done(v.tensor_tensor(hd(o1), hd(bank[3][:]), col(eg[:, 1, :], P), ALU.mult), "v_step")
            v.wait_ge(sems["p_ch"], 4)
            c.done(v.tensor_copy(vn[:, 1, :], bank[0][:]), "ch_ok")

            def squares(t):
                n = TN[t]
                s8 = ss8[0:n, 8 * t:8 * t + 8]
                v.wait_ge(sems["sq_ok"], t + 1)
                c.done(v.tensor_scalar(s8, s8, 1.0 / P, EPS, ALU.mult, ALU.add), "osq_ok")

            def unit_rows(t):
                n = TN[t]
                c.done(v.tensor_tensor(hd(ot[0:n, t, :]), hd(ot[0:n, t, :]), bc(r8[0:n, t, :].unsqueeze(2), n, 8, P), ALU.mult), "o_ok")

            def gated(t):
                n = TN[t]
                for j in range(2):
                    v.wait_ge(sems["p_oT"], 2 * t + j + 1)
                    z = zg[:, 4 * j:4 * j + 4, TO[t]:TO[t] + n]
                    c.done(v.scalar_tensor_tensor(out=z, in0=bank[3 + 2 * j][:, 0:4 * n].rearrange("p (h i) -> p h i", h=H), scalar=vecT[:, 58 + j:59 + j],
                                                  in1=z, op0=ALU.mult, op1=ALU.mult), "oT_ok")

            v.wait_ge(sems["p_smp"], 2)
            os_ = ot[0:SMP, 2, 0:QK]
            vs = qkv[0:SMP, 2, 2 * QK:3 * QK]
            c.done(v.tensor_tensor(hd(vn[0:SMP, 2, :]), hd(bank[6][0:SMP, :]), col(nbeg[0:SMP, 2, :], SMP), ALU.mult), "v_step")
            v.tensor_tensor(hd(os_), hd(bank[7][0:SMP, :]), col(eg[0:SMP, 2, :], SMP), ALU.mult)
            c.done(v.tensor_tensor(vs, vs, vn[0:SMP, 2, :], ALU.add), "smr_ok")
            v.wait_ge(sems["p_ch"], 5)
            c.done(v.tensor_tensor(sgp[:], sgp[:], bc(egl[:, :, 1:2], P, H, P), ALU.mult), "v_step")
            c.done(v.tensor_tensor(sgp[:].rearrange("p h d -> p (h d)"), sgp[:].rearrange("p h d -> p (h d)"), bank[1][:], ALU.add), "ch_ok")
            v.wait_ge(sems["p_smp"], 3)
            c.done(v.tensor_copy(vn[0:SMP, 2, :], bank[6][0:SMP, :]), "smr_ok")
            squares(0)
            v.wait_ge(sems["p_ch"], 6)
            c.done(v.tensor_tensor(o1, o1, bank[5][:], ALU.add), "ch_ok")
            v.wait_ge(sems["p_gch"], 2)
            v.wait_ge(sems["og_ok"], 3)
            for r in range(2):
                d = ot[:, 1, QK:D].rearrange("p (j r d) -> p j r d", j=2, r=2)[:, :, r, :]
                i = v.tensor_tensor(d, d, bank[2 + r][:, 0:256].rearrange("p (j d) -> p j d", j=2), ALU.add)
            c.done(i, "gch_ok")
            v.wait_ge(sems["rs8_ok"], 2)
            unit_rows(0)
            v.wait_ge(sems["p_gs"], 2)
            og = ot[0:SMP, 2, QK:D]
            c.done(v.tensor_copy(og, bank[7][0:SMP, :]), "v_step")
            c.done(v.tensor_tensor(og, og, bank[0][0:SMP, :], ALU.add), "v_step")
            v.wait_ge(sems["p_smp"], 4)
            c.done(v.tensor_tensor(os_, os_, bank[6][0:SMP, :], ALU.add), "smr_ok")
            squares(1)
            gated(0)
            squares(2)
            v.wait_ge(sems["rs8_ok"], 3)
            unit_rows(1)
            v.wait_ge(sems["rs8_ok"], 4)
            unit_rows(2)
            v.wait_ge(sems["p_gch"], 3)
            for j in range(2):
                i = v.scalar_tensor_tensor(out=slp[:, j, :], in0=slp[:, j, :], scalar=ebl[:, j, 1:2], in1=bank[4][:, j * P:(j + 1) * P],
                                           op0=ALU.mult, op1=ALU.add)
            c.done(i, "gch_ok")
            gated(1)
            gated(2)

            def states(h):
                v.wait_ge(sems["p_up_s"], h + 1)
                v.wait_ge(sems["dec_ok"], h + 1)
                for k in range(2):
                    st = sgs[:, 4 * k:4 * k + 4, h, :] if h < 4 else sls[:, h - 4, 4 * k:4 * k + 4, :]
                    i = v.tensor_tensor(st, st, bank[(4, 6, 4, 6, 2, 0)[h] + k][:].rearrange("p (b d) -> p b d", b=4), ALU.add)
                c.done(i, "st_ok")

            for h in range(4):
                states(h)
            v.wait_ge(sems["x_again"], 32)
            for j in range(2):
                for t in range(NTT):
                    at = 3 * j + t
                    v.wait_ge(sems["p_x2"], at + 1)
                    d = x2[0:TN[t], t, 512 * j:512 * (j + 1)]
                    c.done(v.tensor_tensor(d, d, bank[4 + at % 2][0:TN[t], :], ALU.add), "x2_ok")
                    v.wait_ge(sems["ld_ffn"], 16)
                    cols = slice(512 * j, 512 * (j + 1))
                    c.tick(v.tensor_tensor(ot[0:TN[t], t, cols], d, wbc[0:TN[t], cols], ALU.mult), "xw_ok")
            v.wait_ge(sems["ss2_ok"], 3)
            c.done(v.tensor_scalar(rst[:], ss[:], 1.0 / D, EPS, ALU.mult, ALU.add), "rs2_in")
            v.wait_ge(sems["rst_ok"], 2)
            v.wait_ge(sems["xw_ok"], 6)
            v.wait_ge(sems["p_xnT"], 8)
            for t in range(NTT):
                n = TN[t]
                c.tick(v.tensor_scalar(ot[0:n, t, :], ot[0:n, t, :], rst[0:n, t:t + 1], None, ALU.mult), "xn_ok")
            v.memset(lg[:], 0.0)
            v.memset(r32[:], 1.0)
            c.done(v.memset(selm[:], 0.0), "v_step")
            c.done(v.memset(r32[:, 0:3 * E_N:E_N], 0.0), "v_step")
            v.wait_ge(sems["p_lg"], 1)
            for t in range(NTT):
                n = TN[t]
                c.done(v.scalar_tensor_tensor(out=lg[0:n, E_N * t:E_N * (t + 1)], in0=bank[4][0:n, E_N * t:E_N * (t + 1)],
                                              scalar=rst[0:n, t:t + 1], in1=brt[0:n], op0=ALU.mult, op1=ALU.add), "lg_ok")
            for t in range(NTT):
                c.done(v.max(m8[:, t, :], lg[:, E_N * t:E_N * (t + 1)]), "v_step")
            e3 = lambda ap: ap[:].rearrange("p (t e) -> p t e", t=3)
            c3 = lambda ap: bc(ap, P, 3, E_N)
            m1, m4 = m8[:, :, 0:1], m8[:, :, 3:4]
            c.done(v.tensor_tensor(e3(gates), e3(lg), c3(m1), ALU.subtract), "lg_ok")
            c.done(v.tensor_tensor(e3(gts), e3(lg), c3(m4), ALU.is_gt), "v_step")
            c.done(v.tensor_tensor(e3(eqs), e3(lg), c3(m4), ALU.is_equal), "v_step")
            c.done(v.tensor_reduce(ndd[:], e3(gts), AX_X, ALU.add), "v_step")
            c.done(v.tensor_scalar(ndd[:], ndd[:], -1.0, float(TOPK), ALU.mult, ALU.add), "v_step")
            c.done(v.tensor_tensor_scan(pre[:], r32[:], eqs[:], 0.0, ALU.mult, ALU.add), "v_step")
            c.done(v.tensor_tensor(e3(pre), e3(pre), c3(ndd[:].unsqueeze(2)), ALU.is_le), "v_step")
            c.done(v.tensor_tensor(eqs[:], eqs[:], pre[:], ALU.mult), "v_step")
            c.done(v.tensor_tensor(selm[:], gts[:], eqs[:], ALU.add), "route_ok")
            v.wait_ge(sems["gexp_ok"], 1)
            c.done(v.tensor_tensor(gates[:], gates[:], selm[:], ALU.mult), "v_step")
            c.done(v.tensor_reduce(den[:], e3(gates), AX_X, ALU.add), "v_step")
            c.done(v.reciprocal(den[:], den[:]), "v_step")
            c.done(v.tensor_tensor(e3(gates), e3(gates), c3(den[:].unsqueeze(2)), ALU.mult), "v_step")
            c.done(v.memset(posm[:], 0.0), "v_step")
            v.wait_ge(sems["p_pos"], 1)
            for t in range(NTT):
                n = TN[t]
                cols = slice(E_N * t, E_N * (t + 1))
                c.done(v.scalar_tensor_tensor(out=posm[0:n, cols], in0=bank[5][0:n, cols], scalar=1.0, in1=selm[0:n, cols], op0=ALU.add, op1=ALU.mult), "v_step")
            c.done(v.tensor_scalar(posm[:], posm[:], -1.0, None, ALU.add), "v_step")
            def pick_gu(e):
                v.tensor_copy(sel_gu, bc(ident[:, bass.ds(e * 4, 4)].unsqueeze(2), P, 4, CAP)).then_inc(sems["sel_ok"], 1)

            def pick_dn(e):
                v.tensor_copy(sel_dn, bc(ident[:, bass.ds(e * 2, 2)].unsqueeze(2), P, 2, CAP)).then_inc(sems["sel_ok"], 1)

            def swiglu(i, q):
                at = q + 1
                v.wait_ge(sems["p_up"], i * 2 + at)
                v.tensor_scalar(gu[:, 0], bank[0][:], 7.0, None, ALU.min).then_inc(sems["gu_ok"], 1)
                v.tensor_scalar(gu[:, 1], bank[1][:], 7.0, -7.0, ALU.min, ALU.max).then_inc(sems["gu_cl"], 1)
                v.wait_ge(sems["gu_ok"], i * 2 + at)
                v.wait_ge(sems["gu_cl"], i * 2 + at)
                v.scalar_tensor_tensor(out=gu[:, 1], in0=gu[:, 1], scalar=1.0, in1=gu[:, 0], op0=ALU.add, op1=ALU.mult).then_inc(sems["ta_ok"], 1)
                v.wait_ge(sems["ta_ok"], i * 2 + at)
                v.wait_ge(sems["sig_ok"], i * 2 + at)
                v.tensor_tensor(gu[:, 1], gu[:, 1], sg, ALU.mult).then_inc(sems["act_ok"], 1)
                e = i % PAIRS * 2 + q
                pick_dn(e)
                pick_gu(e + 1 if q == 0 else (i + 1) % PAIRS * 2)

            def gain(w, ats=range(6), banks=(6, 7, 6, 7, 6, 7)):
                for at in ats:
                    t, j = at // 2, at % 2
                    v.wait_ge(sems["p_sc"], w * 6 + (at + 1))
                    d = x2[0:TN[t], t, 512 * j:512 * (j + 1)]
                    v.tensor_tensor(d, d, bank[banks[at]][0:TN[t], :], ALU.add).then_inc(sems["sc_ok"], 1)

            pos3 = posm[:].rearrange("p (t e) -> p t e", t=3)
            gat3 = gates[:].rearrange("p (t e) -> p t e", t=3)
            two = lambda ap: ap.rearrange("p (q c) -> p q c", q=2)
            def gates_of(p):
                v.tensor_copy(pp[:], pos3[:, :, bass.ds(p * 2, 2)]).then_inc(sems["pp_ok"], 1)
                v.tensor_copy(gp2[:], gat3[:, :, bass.ds(p * 2, 2)]).then_inc(sems["pp_ok"], 1)
                return v.tensor_scalar(pos3[:, :, bass.ds(p * 2, 2)], pos3[:, :, bass.ds(p * 2, 2)], float(CAP), None, ALU.subtract)

            def token_rows(gcount, pcount):
                v.wait_ge(sems["pp_ok"], pcount)
                for t in range(NTT):
                    n = TN[t]
                    last = v.tensor_tensor(two(G[0:n, t, :]), bc(slots_io[0:n].unsqueeze(1), n, 2, CAP), bc(pp[0:n, t, :].unsqueeze(2), n, 2, CAP), ALU.is_equal)
                last.then_inc(sems["G_ok"], 1)
                v.wait_ge(sems["G_ok"], gcount)
                for t in range(NTT):
                    n = TN[t]
                    last = v.tensor_tensor(two(GG[0:n, t, :]), two(G[0:n, t, :]), bc(gp2[0:n, t, :].unsqueeze(2), n, 2, CAP), ALU.mult)
                last.then_inc(sems["G_ok"], 1)

            v.wait_ge(sems["tri_ok"], 2)
            pick_gu(0)
            gates_of(0).then_inc(sems["pp_ok"], 1)
            token_rows(1, 3)
            c.done(v.tensor_reduce(cnt[0:1, 0:1], bank[6][0:1, 0:E_N], AX_X, ALU.max), "v_step")
            for k in range(4):
                c.done(v.tensor_scalar(cgt[0:1, k:k + 1], cnt[0:1, 0:1], float(CAP * (k + 1)), None, ALU.is_gt), "v_step")
            c.done(v.tensor_reduce(cnt[0:1, 1:2], cgt[0:1, :], AX_X, ALU.add), "v_step")
            c.done(v.tensor_scalar(cnt[0:1, 1:2], cnt[0:1, 1:2], 1.0, None, ALU.add), "v_step")
            c.done(v.tensor_copy(rnd[:], cnt[0:1, 1:2]), "rnd_ok")
            v.memset(den[:], 1.0).then_inc(sems["sc_ok"], 1)
            c.done(v.memset(ndd[:], 1.0), "p_S")
            states(4)
            states(5)
            rounds = v.value_load(rnd[0:1, 0:1], min_val=1, max_val=5)
            with v.Fori(0, rounds * PAIRS) as i:
                swiglu(i, 0)
                gain(i)
                v.wait_ge(sems["p_S"], i + 2)
                gates_of((i + 1) % PAIRS).then_inc(sems["pp_ok"], 1)
                token_rows(i * 2 + 3, i * 3 + 6)
                swiglu(i, 1)
            total = rounds * PAIRS
            def mean_square(t):
                v.wait_ge(sems["ss3_ok"], t + 1)
                c.tick(v.tensor_scalar(rst[:, t:t + 1], ss[:, t:t + 1], 1.0 / D, EPS, ALU.mult, ALU.add), "rs3_in")

            gain(total, range(4), LAST_BANKS)
            mean_square(0)
            gain(total, range(4, 6), LAST_BANKS)
            mean_square(1)
            v.wait_ge(sems["sc_ok"], total * 6 + 7)
            v.wait_ge(sems["ld_fin"], 16)
            for t in range(NTT):
                n = TN[t]
                v.wait_ge(sems["rs3_ok"], t + 1)
                c.tick(v.scalar_tensor_tensor(out=x2[0:n, t, :], in0=x2[0:n, t, :], scalar=rst[0:n, t:t + 1], in1=wbc[0:n], op0=ALU.mult, op1=ALU.mult), "y_fin")
                if t == 0:
                    mean_square(2)

        @block.scalar
        def _(act):
            c = Count(act)
            act.wait_ge(sems["ld_x"], 32)
            act.wait_ge(sems["v_step"], 2)
            for t in range(NTT):
                n = TN[t]
                c.done(act.activation(ot[0:n, t, :], xt[0:n, t, :], ACT.Square, accum_out=ss[0:n, t:t + 1]), "ss_ok")

            def land(at):
                act.wait_ge(sems["p_proj"], at + 1)
                return bank[at % 4]

            b = land(0)
            c.done(act.copy(sm[:], b[0:80, 0:T]), "proj_ok")
            act.wait_ge(sems["gate_x"], 1)
            c.done(act.activation(gtmp[0:4, 1, :], gtmp[0:4, 1, :], ACT.Exp, scale=-1.0), "gate_e")
            c.done(act.activation(gtmp[32:36, 0, :], sm[32:36, :], ACT.Exp, scale=-1.0), "gate_e")
            c.done(act.activation(gate2[:, 2:3], gate2[:, 0:1], ACT.Exp), "gate_e")
            c.done(act.activation(gtmp[0:4, 1, :], gtmp[0:4, 1, :], ACT.Ln, bias=1.0), "gate_l")
            for u in range(3):
                raw, ce = raws[u % 2], ces[u % 2]
                wait(act, "conv_ok", u - 1)
                wait(act, "cs_ok", u - 1)
                for n in range(4):
                    at = 1 + 4 * u + n
                    b = land(at)
                    act.copy(raw[:, n, HEAD:HEAD + SEQ], b[:, 0:SEQ])
                    c.tick(act.copy(samples(raw[:, n, HEAD + SEQ:RAW])[:, :, HEAD:], samples(b[:, SEQ:T])), "proj_ok")
                if u == 2:
                    act.wait_ge(sems["convt_ok"], 6)
                    for t in range(NTT):
                        for e in range(8):
                            i = act.activation(qksq[0:TN[t], e * P:(e + 1) * P], qkv[0:TN[t], t, e * P:(e + 1) * P], ACT.Square,
                                               accum_out=ss8[0:TN[t], 8 * t + e:8 * t + e + 1])
                        c.done(i, "qksq_ok")
                act.wait_ge(sems["conv_lin"], u + 1)
                act.wait_ge(sems["cs_ok"], u + 1)
                c.tick(act.activation(raw[:, :, 0:CW], ce[:, :, 0:CW], ACT.Sigmoid), "conv_sig")
            for n in range(4):
                at = 13 + n
                b = land(at)
                c.tick(act.mul(gqk[:, n, :], b[:, 0:T], 0.125 if n < 2 else 1.0), "proj_ok")
            act.wait_ge(sems["gt_ok"], 3)
            c.done(act.activation(eg[:], gt[:, :, 0:4], ACT.Exp), "gt_exp")
            c.done(act.activation(ekd[:], gt[:, :, 64:68], ACT.Exp), "gt_exp")
            act.wait_ge(sems["gk_x"], 1)
            c.done(act.activation(gQ, gQ, ACT.Exp, scale=-1.0), "gk_e")
            c.done(act.activation(gQ, gQ, ACT.Ln, bias=1.0), "gk_l")
            def turned(t):
                n = TN[t]
                for j in range(3):
                    at = 3 * t + j
                    act.wait_ge(sems["p_qkT"], at + 1)
                    dst = (KQ[:, 0], KQ[:, 1], kbT)[j][:, :, TO[t]:TO[t] + n]
                    c.tick(act.copy(dst, bank[4 + at % 4][:, 0:H * n].rearrange("p (h i) -> p h i", h=H)), "qkT_ok")

            act.wait_ge(sems["p_convt"], 9)
            act.wait_ge(sems["conv_ok"], 3)
            act.wait_ge(sems["cs_ok"], 3)
            for n in range(4):
                if n == 2:
                    turned(0)
                if n == 3:
                    turned(1)
                    turned(2)
                at = 17 + n
                b = land(at)
                c.tick(act.copy(convT[:, n, :], b[:, 0:T]), "proj_ok")
                if n == 1:
                    for t in range(NTT):
                        act.wait_ge(sems["di_ok"], t + 1)
                        c.tick(act.activation(Dtt[t], Dtt[t], ACT.Exp), "dexp_ok")
                    act.wait_ge(sems["di_ok"], 4)
                    c.tick(act.activation(egl[:], egl[:], ACT.Exp), "dexp_ok")
            act.wait_ge(sems["conv_ok"], 3)
            for at in range(6):
                act.wait_ge(sems["p_rows"], at + 1)
                dst = vg[0:TN[at], at, :] if at < 3 else (hist[:, 0:512], hist[:, 512:D], hist_rest[0:27, :])[at - 3]
                n = TN[at] if at < 3 else 27
                c.tick(act.copy(dst, bank[2 + at % 2][0:n, :]), "rows_ok")
            for k, (l, t) in enumerate(INV):
                n = TN[t]
                act.wait_ge(sems["p_y"], k + 1)
                c.tick(act.copy(Yt[t], bank[INV_BANKS[t][0]][0:n, 0:H * n].rearrange("p (h i) -> p h i", h=H)), "y_ok")
                for x in gate_tiles[k]:
                    act.wait_ge(sems["p_proj"], 22 + x)
                    wait(act, "zg_ok", x - 3)
                    b = bank[0]
                    act.copy(zg[:, x, :], b[:, 0:T])
                    c.tick(act.activation(ce_z[:, x % 4, :], b[:, 0:T], ACT.Sigmoid), "proj_ok")
                if 3 <= k < 3 + LEVELS:
                    n = T if k - 3 < 2 else SEQ
                    act.wait_ge(sems["g_abs"], k - 2)
                    c.tick(act.activation(gE[:, :, 0:n], gE[:, :, 0:n], ACT.Exp), "g_exp")
                if k == 4:
                    c.tick(act.activation(qs[:], bT[:, :, SEQ:T], ACT.Exp), "qs_e")
                if k == 9:
                    act.wait_ge(sems["p_smp"], 1)
                    c.tick(act.copy(skT[:].rearrange("p a b -> p (a b)"), bank[1][:, 0:256]), "smk_ok")
                if k == 11:
                    act.wait_ge(sems["p_gs"], 1)
                    c.tick(act.copy(sqT[:].rearrange("p a b -> p (a b)"), bank[1][:, 0:128]), "gsT_ok")
                if k == 3 + LEVELS:
                    act.wait_ge(sems["g_lvl"], LEVELS)
                    c.tick(act.activation(gE, bT, ACT.Exp), "ebl_ok")
                    act.copy(ebl[:, :, 0:2], bT[:, :, P - 1:SEQ:P])
                    c.done(act.copy(ebl[:, :, 2:10], bT[:, :, SEQ + NS - 1:T:NS]), "gt_exp")
                    c.done(act.activation(ebl[:], ebl[:], ACT.Exp), "ebl_ok")
                if k == 5 + LEVELS:
                    act.wait_ge(sems["g_abs"], LEVELS + 2)
                    c.tick(act.activation(gE, gE, ACT.Exp), "ebl_ok")
            act.wait_ge(sems["p_gkd"], 1)
            for t in range(NTT):
                n = TN[t]
                at = (0, 256, 0)[t]
                c.tick(act.copy(kdg[0:n, t, :], bank[(4, 4, 7)[t]][0:n, at:at + 256]), "kdg_ok")
            act.wait_ge(sems["hist_out"], 64)
            act.wait_ge(sems["p_o0"], 1)
            c.tick(act.copy(ot[:, 0, 0:QK], bank[5][:]), "og_ok")
            act.wait_ge(sems["p_gag"], 1)
            c.tick(act.copy(ot[:, 0, QK:D], bank[6][:]), "og_ok")
            act.wait_ge(sems["p_gch"], 1)
            c.tick(act.copy(slp[:].rearrange("p j d -> p (j d)"), bank[4][:, 0:256]), "slp_ok")
            act.wait_ge(sems["p_gag"], 2)
            c.tick(act.copy(ot[:, 1, QK:D], bank[7][:]), "og_ok")
            act.wait_ge(sems["og_ok"], 3)
            for t in range(NTT):
                if t == 1:
                    act.wait_ge(sems["ch_ok"], 6)
                    act.wait_ge(sems["gch_ok"], 1)
                if t == 2:
                    act.wait_ge(sems["smr_ok"], 3)
                n = TN[t]
                for e in range(8):
                    i = act.activation(osqs[t % 2][0:n, e * P:(e + 1) * P], ot[0:n, t, e * P:(e + 1) * P], ACT.Square,
                                       accum_out=ss8[0:n, 8 * t + e:8 * t + e + 1])
                c.done(i, "sq_ok")
            for n in range(8):
                at = 29 + n
                b = land(at)
                c.tick(act.copy(hT[:, n, :], b[:, 0:T]), "proj_ok")

            for k in range(KT):
                if k == 4:
                    for t in range(NTT):
                        n = TN[t]
                        act.wait_ge(sems["x2_ok"], t + 4)
                        c.done(act.activation(zf[0:n, 0:D], x2[0:n, t, :], ACT.Square, accum_out=ss[0:n, t:t + 1]), "ss2_ok")
                act.wait_ge(sems["p_xnT"], k + 1)
                c.tick(act.copy(hT[:, k, :], bank[k % 4][:, 0:T]), "xnT_ok")
            act.wait_ge(sems["p_lgT"], 1)
            c.tick(act.copy(sm[0:E_N, :], bank[6][0:E_N, 0:T]), "lgT_ok")
            act.wait_ge(sems["lg_ok"], 4)
            c.tick(act.activation(gates[:], gates[:], ACT.Exp), "gexp_ok")

            def rows_in(j, value):
                act.wait_ge(sems["p_gat"], value)
                act.copy(xeT[:, 4 * j:4 * j + 4, :].rearrange("p a b -> p (a b)"), bank[4 + j][:]).then_inc(sems["xe_ok"], 1)

            def activation(w):
                act.wait_ge(sems["gu_ok"], w)
                act.activation(sg, gu[:, 0], ACT.Sigmoid, scale=1.702).then_inc(sems["sig_ok"], 1)
                act.wait_ge(sems["p_at"], w)
                act.copy(aT.rearrange("p a b -> p (a b)"), bank[2][:]).then_inc(sems["aT_ok"], 1)

            def rows_out(q, w):
                act.wait_ge(sems["p_yd"], w)
                for h in range(2):
                    act.copy(yr[CAP * q:CAP * (q + 1), 512 * h:512 * (h + 1)], bank[3][CAP * h:CAP * (h + 1), :]).then_inc(sems["yb_ok"], 1)

            rows_in(0, 1)
            rows_in(1, 2)
            act.wait_ge(sems["rnd_ok"], 1)
            rounds = act.value_load(rnd[0:1, 0:1], min_val=1, max_val=5)
            with act.Fori(0, rounds * PAIRS) as i:
                activation(i * 2 + 1)
                act.wait_ge(sems["p_sc"], i * 6 + 6)
                act.wait_ge(sems["p_S"], i + 2)
                act.copy(S, bank[4][:, 0:T]).then_inc(sems["S_ok"], 1)
                rows_out(0, i * 2 + 1)
                activation(i * 2 + 2)
                rows_in(0, i * 2 + 3)
                rows_in(1, i * 2 + 4)
                rows_out(1, i * 2 + 2)
            for t in range(NTT):
                n = TN[t]
                act.wait_ge(sems["sc_ok"], rounds * (PAIRS * 6) + (2 * t + 3))
                c.tick(act.activation(zf[0:n, 0:D], x2[0:n, t, :], ACT.Square, accum_out=ss[0:n, t:t + 1]), "ss3_ok")
                act.wait_ge(sems["ss3_ok"], t + 1)

_INS = ["x_prompt", "x_sample", "state_gdn_conv", "state_gdn", "state_gla", "rms_mix_w", "w_in", "conv_w",
        "gdn_a_log", "gdn_dt_bias", "gdn_norm_w", "gla_gk_w", "gla_gk_b", "gla_norm_w", "w_out", "rms_ffn_w",
        "w_router", "b_router", "w_up", "b_up", "w_down", "b_down", "rms_final_w"]
_OUTS = [(1, 256, 1024), (8, 4, 1024), (1, 1, 3, 1536), (1, 1, 4, 128, 128), (1, 1, 4, 64, 128),
         (1, 8, 3, 1536), (1, 8, 4, 128, 128), (1, 8, 4, 64, 128)]


def kernel(**inputs):
    import numpy as _np
    import concourse.bacc as _bacc
    from concourse import mybir as _mybir
    from concourse.bass_utils import run_bass_kernel_spmd as _run

    nc = _bacc.Bacc("TRN2", target_bir_lowering=False, num_devices=1)
    arrays, args = {}, {}
    for name in _INS:
        x = _np.ascontiguousarray(inputs[name])
        arrays[f"in_{name}"] = x
        args[name] = nc.dram_tensor(f"in_{name}", x.shape, _mybir.dt.from_np(x.dtype), kind="ExternalInput").ap()
    outs = [nc.dram_tensor(f"out_{i}", s, _mybir.dt.float32, kind="ExternalOutput").ap() for i, s in enumerate(_OUTS)]
    program(nc, args, outs)
    r = _run(nc, [arrays], core_ids=[0])
    return tuple(r.results[0][f"out_{i}"] for i in range(len(_OUTS)))
```
